# Optimizing a Trainium2 kernel written in Bass

```python
import math
import jax, jax.numpy as jnp
from jax import lax
import numpy as np

D_MODEL = 1024
BATCH = 1
SEQ = 512
DEPTH = 1

CHUNK = 64
D_MIX = D_MODEL
HEAD_DIM = 64
ATT_HEADS = (D_MIX // 2) // HEAD_DIM
ATT_KV_HEADS = 2
ATT_GROUP = ATT_HEADS // ATT_KV_HEADS
D_ATT = ATT_HEADS * HEAD_DIM
D_KV = ATT_KV_HEADS * HEAD_DIM
WINDOW = 128
WINDOW_CHUNKS = WINDOW // CHUNK
ROPE_THETA = 10000.0
D_LRU = D_MIX - D_ATT
LRU_BLOCKS = 8
LRU_BLOCK_DIM = D_LRU // LRU_BLOCKS
CONV_WIDTH = 4
LRU_C = 8.0
D_IN_PROJ = D_ATT + 2 * D_KV + 2 * D_LRU
MEM_TOKENS = 256
MEM_HEADS = 4
MEM_HEAD_DIM = D_MODEL // MEM_HEADS
N_GROUPS = 4
EXPERTS_PER_GROUP = 4
N_EXPERTS = N_GROUPS * EXPERTS_PER_GROUP
TOP_K = 2
D_EXPERT = D_MODEL // 2
DEEPNORM_ALPHA = (2.0 * DEPTH) ** 0.25
DEEPNORM_BETA = (8.0 * DEPTH) ** -0.25
LN_EPS = 1e-5
NEG_INF = -1e30

kernel_name = "hybrid_swa_sink_rglru_hmoe_deepnorm"

def _layer_norm(x, g, b):
    xf = x.astype(jnp.float32)
    mu = jnp.mean(xf, axis=-1, keepdims=True)
    var = jnp.mean(jnp.square(xf - mu), axis=-1, keepdims=True)
    y = (xf - mu) * lax.rsqrt(var + LN_EPS) * g.astype(jnp.float32) + b.astype(jnp.float32)
    return y.astype(x.dtype)

def _rms_norm(x, g):
    xf = x.astype(jnp.float32)
    y = xf * lax.rsqrt(jnp.mean(jnp.square(xf), axis=-1, keepdims=True) + LN_EPS) * g.astype(jnp.float32)
    return y.astype(x.dtype)

def _rotary(t, cos, sin):
    c = cos[None, :, None, :].astype(t.dtype)
    s = sin[None, :, None, :].astype(t.dtype)
    t1, t2 = jnp.split(t, 2, axis=-1)
    return jnp.concatenate([t1 * c - t2 * s, t2 * c + t1 * s], axis=-1)

def _band(t):
    n_chunks = t.shape[1]
    tp = jnp.pad(t, ((0, 0), (WINDOW_CHUNKS - 1, 0), (0, 0), (0, 0), (0, 0)))
    return jnp.concatenate([tp[:, w:w + n_chunks] for w in range(WINDOW_CHUNKS)], axis=2)

def _swa_sink_attention(q, k, v, sink):
    B, S = q.shape[0], q.shape[1]
    n_chunks = S // CHUNK
    qc = q.reshape(B, n_chunks, CHUNK, ATT_KV_HEADS, ATT_GROUP, HEAD_DIM)
    kb = _band(k.reshape(B, n_chunks, CHUNK, ATT_KV_HEADS, HEAD_DIM))
    vb = _band(v.reshape(B, n_chunks, CHUNK, ATT_KV_HEADS, HEAD_DIM))
    chunk_idx = jnp.arange(n_chunks)[:, None]
    key_block = jnp.arange(WINDOW_CHUNKS * CHUNK)[None, :] // CHUNK
    valid = (chunk_idx - (WINDOW_CHUNKS - 1) + key_block) >= 0
    scores = jnp.einsum('bcqkgd,bcjkd->bkgcqj', qc, kb).astype(jnp.float32) * (HEAD_DIM ** -0.5)
    scores = jnp.where(valid[None, None, None, :, None, :], scores, NEG_INF)
    sink_l = sink.astype(jnp.float32).reshape(ATT_KV_HEADS, ATT_GROUP)[None, :, :, None, None, None]
    m = jnp.maximum(jnp.max(scores, axis=-1, keepdims=True), sink_l)
    p = jnp.exp(scores - m)
    denom = jnp.sum(p, axis=-1, keepdims=True) + jnp.exp(sink_l - m)
    probs = (p / denom).astype(v.dtype)
    out = jnp.einsum('bkgcqj,bcjkd->bcqkgd', probs, vb)
    return out.reshape(B, S, D_ATT)

def _rg_lru_branch(x_l, gate, conv_w, conv_b, w_rgate, b_rgate, w_igate, b_igate, lru_lambda):
    B, S = x_l.shape[0], x_l.shape[1]
    xp = jnp.pad(x_l, ((0, 0), (CONV_WIDTH - 1, 0), (0, 0)))
    xc = conv_b
    for tap in range(CONV_WIDTH):
        xc = xc + conv_w[tap] * xp[:, tap:tap + S]
    xb = xc.reshape(B, S, LRU_BLOCKS, LRU_BLOCK_DIM)
    r = jax.nn.sigmoid(jnp.einsum('bshi,hij->bshj', xb, w_rgate).reshape(B, S, D_LRU) + b_rgate)
    i = jax.nn.sigmoid(jnp.einsum('bshi,hij->bshj', xb, w_igate).reshape(B, S, D_LRU) + b_igate)
    log_a = -LRU_C * r.astype(jnp.float32) * jax.nn.softplus(-lru_lambda.astype(jnp.float32))
    a = jnp.exp(log_a)
    mult = jnp.sqrt(jnp.maximum(-jnp.expm1(2.0 * log_a), 0.0))
    b = mult * (i * xc).astype(jnp.float32)

    def combine(lhs, rhs):
        a1, b1 = lhs
        a2, b2 = rhs
        return a1 * a2, a2 * b1 + b2

    _, h = lax.associative_scan(combine, (a, b), axis=1)
    return jax.nn.gelu(gate) * h.astype(x_l.dtype)

def _memory_attention(x, mem, wq, wk, wv, wo):
    B, S = x.shape[0], x.shape[1]
    M = mem.shape[1]
    q = (x @ wq).reshape(B, S, MEM_HEADS, MEM_HEAD_DIM)
    k = (mem @ wk).reshape(B, M, MEM_HEADS, MEM_HEAD_DIM)
    v = (mem @ wv).reshape(B, M, MEM_HEADS, MEM_HEAD_DIM)
    s = jnp.einsum('bshd,bmhd->bhsm', q, k).astype(jnp.float32) * (MEM_HEAD_DIM ** -0.5)
    p = jax.nn.softmax(s, axis=-1).astype(v.dtype)
    o = jnp.einsum('bhsm,bmhd->bshd', p, v).reshape(B, S, D_MODEL)
    return o @ wo

def _hierarchical_moe(x, w_rg, b_rg, w_re, b_re, w_gate, w_up, w_down):
    B, S, D = x.shape
    xt = x.reshape(B * S, D)
    p_group = jax.nn.softmax((xt @ w_rg + b_rg).astype(jnp.float32), axis=-1)
    p_g, g_idx = lax.top_k(p_group, 1)
    e_logits = (jnp.einsum('td,gde->tge', xt, w_re) + b_re).astype(jnp.float32)
    e_logits = jnp.take_along_axis(e_logits, g_idx[:, :, None], axis=1)[:, 0]
    e_probs = jax.nn.softmax(e_logits, axis=-1)
    top_v, top_i = lax.top_k(e_probs, TOP_K)
    top_v = top_v / jnp.sum(top_v, axis=-1, keepdims=True)
    within = jnp.sum(jax.nn.one_hot(top_i, EXPERTS_PER_GROUP, dtype=jnp.float32) * top_v[..., None], axis=1)
    gates = (jax.nn.one_hot(g_idx[:, 0], N_GROUPS, dtype=jnp.float32)[:, :, None]
             * within[:, None, :] * p_g[:, :, None]).reshape(B * S, N_EXPERTS).astype(x.dtype)
    y = jnp.zeros_like(xt)
    for e in range(N_EXPERTS):
        h = jax.nn.silu(xt @ w_gate[e]) * (xt @ w_up[e])
        y = y + gates[:, e:e + 1] * (h @ w_down[e])
    return y.reshape(B, S, D)

def setup_inputs(seed: int = 0) -> dict:
    key = jax.random.key(seed)
    ks = jax.random.split(key, 40)
    f32 = jnp.float32

    def nrm(k, shape, scale):
        return jax.random.normal(k, shape, f32) * scale

    L = DEPTH
    u = jax.random.uniform(ks[12], (L, D_LRU), f32, minval=0.9, maxval=0.999)
    a0 = u ** (1.0 / LRU_C)
    lru_lambda = jnp.log(a0) - jnp.log1p(-a0)
    return {
        "x": nrm(ks[0], (BATCH, SEQ, D_MODEL), 1.0),
        "mem": nrm(ks[1], (BATCH, MEM_TOKENS, D_MODEL), 1.0),
        "ln_in_g": 1.0 + nrm(ks[2], (D_MODEL,), 0.01),
        "ln_in_b": nrm(ks[3], (D_MODEL,), 0.01),
        "w_in": nrm(ks[4], (L, D_MODEL, D_IN_PROJ), D_MODEL ** -0.5),
        "attn_sink": nrm(ks[5], (L, ATT_HEADS), 0.5),
        "conv_w": nrm(ks[6], (L, CONV_WIDTH, D_LRU), CONV_WIDTH ** -0.5),
        "conv_b": nrm(ks[7], (L, D_LRU), 0.01),
        "w_rgate": nrm(ks[8], (L, LRU_BLOCKS, LRU_BLOCK_DIM, LRU_BLOCK_DIM), LRU_BLOCK_DIM ** -0.5),
        "b_rgate": nrm(ks[9], (L, D_LRU), 0.01),
        "w_igate": nrm(ks[10], (L, LRU_BLOCKS, LRU_BLOCK_DIM, LRU_BLOCK_DIM), LRU_BLOCK_DIM ** -0.5),
        "b_igate": nrm(ks[11], (L, D_LRU), 0.01),
        "lru_lambda": lru_lambda,
        "norm_attn_g": 1.0 + nrm(ks[13], (L, D_ATT), 0.01),
        "norm_lru_g": 1.0 + nrm(ks[14], (L, D_LRU), 0.01),
        "w_out": nrm(ks[15], (L, D_MIX, D_MODEL), D_MIX ** -0.5 * DEEPNORM_BETA),
        "ln1_g": 1.0 + nrm(ks[16], (L, D_MODEL), 0.01),
        "ln1_b": nrm(ks[17], (L, D_MODEL), 0.01),
        "wq_mem": nrm(ks[18], (L, D_MODEL, D_MODEL), D_MODEL ** -0.5),
        "wk_mem": nrm(ks[19], (L, D_MODEL, D_MODEL), D_MODEL ** -0.5),
        "wv_mem": nrm(ks[20], (L, D_MODEL, D_MODEL), D_MODEL ** -0.5),
        "wo_mem": nrm(ks[21], (L, D_MODEL, D_MODEL), D_MODEL ** -0.5 * DEEPNORM_BETA),
        "ln2_g": 1.0 + nrm(ks[22], (L, D_MODEL), 0.01),
        "ln2_b": nrm(ks[23], (L, D_MODEL), 0.01),
        "w_router_group": nrm(ks[24], (L, D_MODEL, N_GROUPS), D_MODEL ** -0.5),
        "b_router_group": nrm(ks[25], (L, N_GROUPS), 0.01),
        "w_router_expert": nrm(ks[26], (L, N_GROUPS, D_MODEL, EXPERTS_PER_GROUP), D_MODEL ** -0.5),
        "b_router_expert": nrm(ks[27], (L, N_GROUPS, EXPERTS_PER_GROUP), 0.01),
        "w_gate_e": nrm(ks[28], (L, N_EXPERTS, D_MODEL, D_EXPERT), D_MODEL ** -0.5),
        "w_up_e": nrm(ks[29], (L, N_EXPERTS, D_MODEL, D_EXPERT), D_MODEL ** -0.5),
        "w_down_e": nrm(ks[30], (L, N_EXPERTS, D_EXPERT, D_MODEL), D_EXPERT ** -0.5 * DEEPNORM_BETA),
        "ln3_g": 1.0 + nrm(ks[31], (L, D_MODEL), 0.01),
        "ln3_b": nrm(ks[32], (L, D_MODEL), 0.01),
    }

def reference(x, mem, ln_in_g, ln_in_b, w_in, attn_sink, conv_w, conv_b, w_rgate, b_rgate,
              w_igate, b_igate, lru_lambda, norm_attn_g, norm_lru_g, w_out, ln1_g, ln1_b,
              wq_mem, wk_mem, wv_mem, wo_mem, ln2_g, ln2_b, w_router_group, b_router_group,
              w_router_expert, b_router_expert, w_gate_e, w_up_e, w_down_e, ln3_g, ln3_b):
    B, S = x.shape[0], x.shape[1]
    pos = jnp.arange(S, dtype=jnp.float32)
    inv_freq = ROPE_THETA ** (-jnp.arange(0, HEAD_DIM, 2, dtype=jnp.float32) / HEAD_DIM)
    ang = pos[:, None] * inv_freq[None, :]
    cos, sin = jnp.cos(ang), jnp.sin(ang)

    x = _layer_norm(x, ln_in_g, ln_in_b)
    for l in range(DEPTH):
        proj = x @ w_in[l]
        q, k, v, x_l, g_l = jnp.split(
            proj, [D_ATT, D_ATT + D_KV, D_ATT + 2 * D_KV, D_ATT + 2 * D_KV + D_LRU], axis=-1)
        q = _rotary(q.reshape(B, S, ATT_HEADS, HEAD_DIM), cos, sin)
        k = _rotary(k.reshape(B, S, ATT_KV_HEADS, HEAD_DIM), cos, sin)
        v = v.reshape(B, S, ATT_KV_HEADS, HEAD_DIM)
        y_att = _swa_sink_attention(q, k, v, attn_sink[l])
        y_lru = _rg_lru_branch(x_l, g_l, conv_w[l], conv_b[l], w_rgate[l], b_rgate[l],
                               w_igate[l], b_igate[l], lru_lambda[l])
        y_mix = jnp.concatenate([_rms_norm(y_att, norm_attn_g[l]),
                                 _rms_norm(y_lru, norm_lru_g[l])], axis=-1) @ w_out[l]
        x = _layer_norm(DEEPNORM_ALPHA * x + y_mix, ln1_g[l], ln1_b[l])
        y_mem = _memory_attention(x, mem, wq_mem[l], wk_mem[l], wv_mem[l], wo_mem[l])
        x = _layer_norm(DEEPNORM_ALPHA * x + y_mem, ln2_g[l], ln2_b[l])
        y_moe = _hierarchical_moe(x, w_router_group[l], b_router_group[l], w_router_expert[l],
                                  b_router_expert[l], w_gate_e[l], w_up_e[l], w_down_e[l])
        x = _layer_norm(DEEPNORM_ALPHA * x + y_moe, ln3_g[l], ln3_b[l])
    return x


_drawn_inputs = setup_inputs


def setup_inputs(seed=0):
    import zlib

    import numpy as np

    out = dict(_drawn_inputs(seed))
    spreads = {}
    factors = {'ln_in_g': 4.188,
     'attn_sink': 64.0,
     'b_rgate': 8.0,
     'b_igate': 54.941,
     'norm_attn_g': 22.955,
     'norm_lru_g': 64.0,
     'ln1_g': 4.075,
     'ln1_b': 4.627,
     'ln2_g': 4.345,
     'ln2_b': 4.353,
     'b_router_group': 7.408,
     'b_router_expert': 8.0,
     'ln3_g': 193.439,
     'ln3_b': 183.307}
    for name, (base, spread) in spreads.items():
        noise = np.random.default_rng([zlib.crc32(name.encode()), seed]).standard_normal(out[name].shape)
        drawn = base * np.exp(spread * noise) if base else spread * noise
        out[name] = __import__('jax').numpy.asarray(drawn.astype(out[name].dtype))
    for name, factor in factors.items():
        out[name] = (out[name] * factor).astype(out[name].dtype)
    return out
```

```python
from contextlib import ExitStack

import numpy as np

import concourse.bass as bass
from concourse import mybir

F32 = mybir.dt.float32
F32R = mybir.dt.float32r
I32 = mybir.dt.int32
U32 = mybir.dt.uint32
ALU = mybir.AluOpType
ACT = mybir.ActivationFunctionType
AX = mybir.AxisListType.X

P = 128
D = 1024
T = 512
NT = T // P
KT = D // P
CHUNK = 64
HD = 64
HEADS = 8
KVH = 2
D_ATT = HEADS * HD
D_KV = KVH * HD
D_LRU = 512
FT = D_LRU // P
TAPS = 4
LRU_C = 8.0
D_IN = D_ATT + 2 * D_KV + 2 * D_LRU
MEM = 256
MT = MEM // P
MH = 4
MHD = D // MH
NG = 4
EPG = 4
NE = NG * EPG
TOPK = 2
F = 512
FFT = F // P
ALPHA = 2.0 ** 0.25
EPS = 1e-5
NEG = -1e30
EXTRA = (TOPK * T - 1) // P
CMAX = NE + EXTRA
IDXC = CMAX + 1

C_ID, C_TRI, C_ONES, C_PERM, C_MASK, C_ROW = (P * i for i in range(6))
C_CHK = 6 * P
C_EXP = C_CHK + IDXC
C_THR = C_EXP + NE
C_WG = C_THR + 3
C_TOK = C_WG + EPG
CONST_W = C_TOK + NT


def constants():
    c = np.zeros((P, CONST_W), np.float32)
    i = np.arange(P)
    c[:, C_ID:C_ID + P] = i[:, None] == i[None, :]
    c[:, C_TRI:C_TRI + P] = i[:, None] < i[None, :]
    c[:, C_ONES:C_ONES + P] = 1.0
    src = (i // HD) * HD + (i % HD + HD // 2) % HD
    c[:, C_PERM:C_PERM + P] = i[:, None] == src[None, :]
    c[:CHUNK, C_MASK:C_MASK + CHUNK] = NEG
    c[:, C_ROW:C_ROW + P] = i[None, :]
    c[:, C_CHK:C_CHK + IDXC] = np.arange(IDXC)[None, :]
    c[:, C_EXP:C_EXP + NE] = np.arange(NE)[None, :]
    c[:, C_THR:C_THR + 3] = P * np.arange(1, 4)[None, :]
    c[:, C_WG:C_WG + EPG] = EPG - np.arange(EPG)[None, :]
    c[:, C_TOK:C_TOK + NT] = i[:, None] + P * np.arange(NT)[None, :]
    inv = np.float32(10000.0) ** (-np.arange(0, HD, 2, dtype=np.float32) / np.float32(HD))
    ang = np.arange(T, dtype=np.float32)[None, :] * inv[i % (HD // 2)][:, None].astype(np.float32)
    sign = np.where(i % HD < HD // 2, -1.0, 1.0).astype(np.float32)[:, None]
    rot = np.stack([np.cos(ang), np.sin(ang) * sign], 1).astype(np.float32)
    return c, rot


def psum_groups():
    g = [("x0T", t, k) for t in range(NT) for k in range(2)]
    g += [("in", n) for n in range(D_IN // P)]
    g += [("gate", ft, w) for ft in range(FT) for w in range(2)]
    g += [("rope", n) for n in range(5)] + [("vwin", 0), ("vwin", 1)]
    g += [("S", t, par) for t in range(2) for par in range(2)]
    for t in range(NT):
        g += [("PT", t, 0), ("PT", t, 1), ("O", t)]
        if t + 2 < NT:
            g += [("S", t + 2, 0), ("S", t + 2, 1)]
    g += [("memT", m, k) for m in range(MT) for k in range(2)]
    g += [("mk", n) for n in range(KT)]
    g += [("mv", q, m) for q in range(4) for m in range(MT)]
    g += [("sq", 0), ("sq", 1)]
    g += [("out", 0, t, b) for t in range(NT) for b in range(2)]
    for t in range(NT):
        g += [("out", 1, t, 0), ("out", 1, t, 1)]
        if t >= 2:
            g += [("x1T", t - 2, 0), ("x1T", t - 2, 1)]
    g += [("x1T", t, k) for t in (2, 3) for k in range(2)]
    for h in range(MH + 2):
        if h < MH:
            g += [("mq", h, n) for n in range(2)]
        if 2 <= h:
            g += [("mPT", h - 2, m) for m in range(MT)]
        if 1 <= h <= MH:
            g += [("mS", h - 1, n) for n in range(2)]
        if h >= 4:
            g += [("mO", h - 4, n) for n in range(2)]
    g += [("mO", 2, 0), ("mO", 2, 1), ("mO", 3, 0), ("mO", 3, 1)]
    g += [("wo", 0, t) for t in range(NT)]
    for t in range(NT):
        g += [("wo", 1, t)]
        if t >= 2:
            g += [("x2T", t - 2, 0), ("x2T", t - 2, 1)]
    g += [("x2T", t, k) for t in (2, 3) for k in range(2)]
    g += [("logits",), ("rank",), ("table",)]
    return {name: n for n, name in enumerate(g)}


def weight_pieces(w_in, wk, wv, w_out, wq, wo):
    cols = [("in", w_in, 256 * c) for c in (3, 4, 5, 6, 2, 0, 1)]
    cols += [("mk", wk, 256 * c) for c in range(4)] + [("mv", wv, 256 * c) for c in range(4)]
    out = []
    for name, w, c0 in cols:
        out.append((name, [w[h * 512:(h + 1) * 512, c0:c0 + 256] for h in range(2)], 256))
    for name, w in (("out", w_out), ("mq", wq), ("wo", wo)):
        for q in range(4):
            if name == "mq":
                out.append((name, [w[h * 512:(h + 1) * 512, q * 256:(q + 1) * 256] for h in range(2)], 256))
            else:
                n, k = q // 2, q % 2
                out.append((name, [w[k * 512 + h * 256:k * 512 + (h + 1) * 256, n * 512:(n + 1) * 512]
                                   for h in range(2)], 512))
    return out


def encoder_layer(nc, A, consts, rots, y_out):
    G = psum_groups()
    pieces = weight_pieces(A["w_in"][0], A["wk_mem"][0], A["wv_mem"][0], A["w_out"][0],
                           A["wq_mem"][0], A["wo_mem"][0])
    first_piece = {}
    for n, (name, _, _) in enumerate(pieces):
        first_piece.setdefault(name, n)
    RING = 3

    def last_use(w):
        name = pieces[w][0]
        q = w - first_piece[name]
        return {"in": ("in", 2 * q + 1), "mk": ("mk", 2 * q + 1), "mv": ("mv", q, MT - 1), "mq": ("mq", q, 1),
                "out": ("out", q // 2, NT - 1, q % 2), "wo": ("wo", q // 2, NT - 1)}[name]

    ctx = ExitStack()
    with ctx:
        def sb(name, shape, dt=F32):
            return ctx.enter_context(nc.sbuf_tensor(name, shape, dt))

        def sem(name):
            return ctx.enter_context(nc.semaphore(name))

        xres = sb("xres", [P, NT, D])
        actT = sb("actT", [P, 2, KT, T], F32R)
        memT = sb("memT", [P, 2, KT, MEM], F32R)
        qs = sb("qs", [P, 4, T])
        wring = sb("wring", [P, RING, 2, 2048], F32R)
        stage = sb("stage", [P, 2, 1024])
        kvm = sb("kvm", [P, 4, 1024])
        scr = sb("scr", [P, 6, 2048])
        lngb = sb("lngb", [P, 2, D])
        cst = sb("cst", [P, CONST_W])
        w_rt = sb("w_rt", [P, KT, NG + NE])
        b_rt = sb("b_rt", [P, NG + NE])
        sink = sb("sink", [P, HEADS])
        feat = sb("feat", [P, 11, FT])
        sp = sb("sp", [P, 8, FT])
        stats = sb("stats", [P, NT, 2, 6])
        mv = sb("mv", [P, NT, 2])
        rstd = sb("rstd", [P, NT])
        rms = sb("rms", [P, 2, NT])
        mx = sb("mx", [P, 2, HEADS])
        nmx = sb("nmx", [P, 2, HEADS])
        psm = sb("psm", [P, 2, HEADS])
        esk = sb("esk", [P, 2, HEADS])
        rden = sb("rden", [P, 2, HEADS])
        gates = sb("gates", [P, NT, TOPK])
        slot_i = sb("slot_i", [P, NT, TOPK], U32)
        tokidx = sb("tokidx", [P, IDXC], U32)
        idx_now = sb("idx_now", [P, 1], U32)
        ctab = sb("ctab", [1, 2 + CMAX], I32)

        ident = cst[:, C_ID:C_ID + P]
        tri = cst[:, C_TRI:C_TRI + P]
        ones = cst[:, C_ONES:C_ONES + P]
        perm = cst[:, C_PERM:C_PERM + P]
        mask0 = cst[:, C_MASK:C_MASK + P]

        prob = kvm[:, 0:2, :].rearrange("p b (h k) -> p b h k", h=HEADS)
        probT = kvm[:, 2, :].rearrange("p (h q) -> p h q", h=HEADS)
        vwin = kvm[:, 3, :].rearrange("p (c v) -> p c v", c=T // CHUNK)
        rot = kvm[:, 1, :].rearrange("p (a t) -> p a t", a=2)
        gate_bd = kvm[:, 2, :].rearrange("p (g f j) -> p g f j", g=2, f=FT)
        mkT = kvm[:, 0:2, :].rearrange("p a (k m) -> p (a k) m", m=MEM)
        mvv = kvm[:, 2:4, :]
        mprob = scr[:, 3, :].rearrange("p (b t m) -> p b t m", b=2, t=NT)
        mq = scr[:, 4:6, :].rearrange("p a (k t) -> p (a k) t", t=T)
        mpT = qs[:, :, :].rearrange("p (b m) t -> p b m t", b=2)
        x2T = kvm[:, :, :].rearrange("p a (k t) -> p (a k) t", t=T)
        xl, xc, gel, ra, th = (scr[:, i, :].rearrange("p (f t) -> p f t", f=FT) for i in range(5))
        KP = CHUNK + T
        kpad = [scr[:, 5, i * KP:(i + 1) * KP] for i in range(2)]
        vpad = scr[:, 5, 2 * KP:3 * KP]
        memr = lngb
        g_w = scr[:, 0:2, :].rearrange("p a (k f) -> p a k f", k=4)
        u_w = scr[:, 2:4, :].rearrange("p a (k f) -> p a k f", k=4)
        d_w = scr[:, 4:6, :].rearrange("p a (k n) -> p a k n", k=2)
        xg = kvm[:, 0, :]
        xgT = kvm[:, 1, :].rearrange("p (k s) -> p k s", k=KT)
        moe_o = kvm[:, 2, :]
        silu_g = kvm[:, 3, 0:512]
        h_act = kvm[:, 3, 512:1024]
        hT = qs[:, 3, :].rearrange("p (f s) -> p f s", f=FFT)
        back = scr[:, 0:4, :].rearrange("p a (b n) -> p (a b) n", n=D)

        rt = qs[:, 0:3, :].rearrange("p a b -> p (a b)")
        rt_at = [0]

        def rtmp(*shape):
            n = int(np.prod(shape))
            a = rt[:, rt_at[0]:rt_at[0] + n]
            rt_at[0] += n
            assert rt_at[0] <= 3 * T
            if len(shape) == 1:
                return a
            names = "abc"[:len(shape)]
            return a.rearrange(f"p ({' '.join(names)}) -> p {' '.join(names)}",
                               **{k: s for k, s in zip(names, shape)})

        below, below_exp = rtmp(NT, 1 + NG), rtmp(NT, 1 + NG)
        moh = rtmp(3, NT, NE)
        sel_c = rtmp(8, IDXC)
        selT = stage[:, :, :].rearrange("p a (b r) -> p (a b) r", r=P)

        psum = ctx.enter_context(nc.psum_tensor("psum", [P, 8, 512], F32))

        x2_rows = nc.dram_tensor("x2_rows", (T, D), F32, kind="Internal").ap()
        moe_rows = nc.dram_tensor("moe_rows", (CMAX * P, D), F32, kind="Internal").ap()

        psum_full = [sem(f"psum_full{b}") for b in range(8)]
        psum_read = [sem(f"psum_read{b}") for b in range(8)]
        x_in = [sem(f"x_in{t}") for t in range(NT)]
        const_in = sem("const_in")
        small_in = sem("small_in")
        sink_in = sem("sink_in")
        rot_in = sem("rot_in")
        bd_in = sem("bd_in")
        bd_zero = sem("bd_zero")
        pad_zero = sem("pad_zero")
        rows_src = sem("rows_src")
        rows_zero = sem("rows_zero")
        lngb_in = sem("lngb_in")
        mem_in = sem("mem_in")
        stage_in = [sem(f"stage_in{h}") for h in range(2)]
        w_hi = sem("w_hi")
        w_lo = sem("w_lo")
        dve_step = sem("dve_step")
        ln_done = sem("ln_done")
        actT_hi = sem("actT_hi")
        scaled = sem("scaled")
        xc_done = sem("xc_done")
        kswap = sem("kswap")
        sig_i = sem("sig_i")
        sp_abs = sem("sp_abs")
        sp_exp = sem("sp_exp")
        sp_done = sem("sp_done")
        decay = sem("decay")
        gelu_done = sem("gelu_done")
        lru_y = sem("lru_y")
        lru_sq = sem("lru_sq")
        lru_hi = sem("lru_hi")
        lru_lo = sem("lru_lo")
        row_max = sem("row_max")
        exp_done = sem("exp_done")
        prob_done = sem("prob_done")
        att_y = sem("att_y")
        att_hi = sem("att_hi")
        att_lo = sem("att_lo")
        memT_hi = sem("memT_hi")
        m_max = sem("m_max")
        m_prob = sem("m_prob")
        mo_hi = sem("mo_hi")
        var_ready = sem("var_ready")
        rstd_ready = sem("rstd_ready")
        ms_ready = sem("ms_ready")
        rms_ready = sem("rms_ready")
        gain_sq = sem("gain_sq")
        gain = sem("gain")
        x2_stored = sem("x2_stored")
        onehots = sem("onehots")
        selected = sem("selected")
        table_done = sem("table_done")
        slot_done = sem("slot_done")
        gu_in = [sem(f"gu_in{i}") for i in range(4)]
        d_in = [sem(f"d_in{i}") for i in range(2)]
        gu_half = sem("gu_half")
        gateup_done = sem("gateup_done")
        silu_done = sem("silu_done")
        h_ready = sem("h_ready")
        htrans_done = sem("htrans_done")
        hT_ready = sem("hT_ready")
        down_done = sem("down_done")
        o_lo = sem("o_lo")
        o_hi = sem("o_hi")
        o_stored = sem("o_stored")
        xtrans_done = sem("xtrans_done")
        xgT_a = sem("xgT_a")
        xgT_b = sem("xgT_b")
        all_stored = sem("all_stored")
        gathered = sem("gathered")
        back_in = [sem(f"back_in{i}") for i in range(NT * TOPK)]
        y_ready = sem("y_ready")
        y_stored = sem("y_stored")

        def bank(g):
            return psum[:, G[g] % 8, :]

        def wait_full(eng, g):
            eng.wait_ge(psum_full[G[g] % 8], G[g] // 8 + 1)

        def wait_free(eng, g):
            if G[g] >= 8:
                eng.wait_ge(psum_read[G[g] % 8], G[g] // 8)

        def full(ins, g):
            ins.then_inc(psum_full[G[g] % 8], 1)

        def free(ins, g):
            ins.then_inc(psum_read[G[g] % 8], 1)

        def wait_read(eng, *groups):
            for g in groups:
                eng.wait_ge(psum_read[G[g] % 8], G[g] // 8 + 1)

        FEAT = {n: i for i, n in enumerate(("conv0", "conv1", "conv2", "conv3", "conv_b", "b_r", "b_i",
                                            "lam", "g_att", "g_lru"))}

        def fv(name, ft):
            return feat[:, FEAT[name], ft:ft + 1]

        N_CONST, N_SMALL, N_LN = 1, 10 + 4 + 1, 2
        LN_SEQ = ["ln_in", "ln1", "ln2", "ln3"]

        def in_slices(n):
            return n // 2, (n % 2) * P

        IN_KIND = ["xl"] * 4 + ["g"] * 4 + ["k", "v"] + ["q"] * 4
        block = ctx.enter_context(nc.Block())

        @block.sync
        def _(eng):
            for t in range(NT):
                eng.dma_start(xres[:, t, :], A["x"][0, t * P:(t + 1) * P, :]).then_inc(x_in[t], 16)
            eng.dma_start(cst[:, :], consts).then_inc(const_in, 16)

            def load_ln(name):
                for i, part in enumerate("gb"):
                    v = A[f"{name}_{part}"]
                    v = v if name == "ln_in" else v[0]
                    eng.dma_start(lngb[:, i, :], v.partition_broadcast(P)).then_inc(lngb_in, 16)

            load_ln("ln_in")

            def load_piece(w):
                _, halves, width = pieces[w]
                for h in range(2):
                    if w >= 1:
                        eng.wait_ge(w_lo, 2 * (w - 1) + h + 1)
                    eng.dma_start(stage[:, h, :].rearrange("p (k n) -> p k n", n=width),
                                  halves[h].rearrange("(k p) n -> p k n", p=P)).then_inc(stage_in[h], 16)

            load_piece(0)
            for i in range(TAPS):
                eng.dma_start(feat[:, i, :], A["conv_w"][0, i].rearrange("(f p) -> p f", p=P),
                              allow_slow_non_contiguous=True).then_inc(small_in, 16)
            for name, key in (("conv_b", "conv_b"), ("b_r", "b_rgate"), ("b_i", "b_igate"),
                              ("lam", "lru_lambda"), ("g_att", "norm_attn_g"), ("g_lru", "norm_lru_g")):
                eng.dma_start(feat[:, FEAT[name], :], A[key][0].rearrange("(f p) -> p f", p=P),
                              allow_slow_non_contiguous=True).then_inc(small_in, 16)
            load_piece(1)
            eng.dma_start(rot, rots).then_inc(rot_in, 16)
            eng.wait_ge(bd_zero, 1)
            for g, key in enumerate(("w_rgate", "w_igate")):
                w = A[key][0].rearrange("(f two) i j -> two i f j", two=2)
                for par in range(2):
                    s = slice(par * 64, par * 64 + 64)
                    eng.dma_start(gate_bd[s, g, :, s], w[par]).then_inc(bd_in, 16)
            for w in range(2, 8):
                load_piece(w)
            eng.wait_ge(ln_done, NT)
            eng.dma_start(memr[:, :, :], A["mem"][0].rearrange("(m p) d -> p m d", p=P)).then_inc(mem_in, 16)
            eng.dma_start(b_rt[:, 0:NG], A["b_router_group"][0].partition_broadcast(P)).then_inc(small_in, 16)
            eng.dma_start(b_rt[:, NG:], A["b_router_expert"][0].rearrange("g e -> (g e)")
                          .partition_broadcast(P)).then_inc(small_in, 16)
            eng.dma_start(w_rt[:, :, 0:NG], A["w_router_group"][0].rearrange("(k p) g -> p k g", p=P),
                          allow_slow_non_contiguous=True).then_inc(small_in, 16)
            for g in range(NG):
                eng.dma_start(w_rt[:, :, NG + g * EPG:NG + (g + 1) * EPG],
                              A["w_router_expert"][0, g].rearrange("(k p) e -> p k e", p=P),
                              allow_slow_non_contiguous=True).then_inc(small_in, 16)
            for w in range(8, first_piece["out"] + 2):
                load_piece(w)
            for m in range(MT):
                for k in range(2):
                    wait_full(eng, ("memT", m, k))
            load_ln("ln1")
            for w in range(first_piece["out"] + 2, first_piece["wo"]):
                load_piece(w)
            eng.wait_ge(ln_done, 2 * NT)
            load_ln("ln2")
            for w in range(first_piece["wo"], len(pieces)):
                load_piece(w)
            def load_gu(i, e):
                src = (A["w_gate_e"], A["w_up_e"])[i % 2]
                rows = slice((i // 2) * 512, (i // 2 + 1) * 512)
                w = src[0, e] if isinstance(e, int) else src[0, bass.ds(e, 1)].rearrange("a k f -> (a k) f")
                dst = (g_w, u_w)[i % 2][:, i // 2]
                eng.dma_start(dst, w[rows, :].rearrange("(k p) f -> p k f", p=P)).then_inc(gu_in[i], 16)

            wait_full(eng, ("mPT", MH - 1, MT - 1))
            for i in range(4):
                load_gu(i, 0)
            for t in range(NT):
                eng.wait_ge(ln_done, 2 * NT + t + 1)
                eng.dma_start(x2_rows[t * P:(t + 1) * P, :], xres[:, t, :]).then_inc(x2_stored, 16)
            eng.wait_ge(ln_done, 3 * NT)
            load_ln("ln3")
            eng.wait_ge(table_done, 1)
            n = eng.value_load(ctab[0:1, 0:1], min_val=NE, max_val=CMAX)
            with eng.Fori(1, CMAX) as c:
                with eng.If(c < n):
                    e = eng.value_load(ctab[0:1, bass.ds(c + 1, 1)], min_val=0, max_val=NE - 1)
                    eng.wait_ge(gu_half, c)
                    load_gu(0, e)
                    load_gu(1, e)
                    eng.wait_ge(gateup_done, c)
                    load_gu(2, e)
                    load_gu(3, e)
            for t in range(NT):
                eng.wait_ge(y_ready, t + 1)
                eng.dma_start(y_out[0, t * P:(t + 1) * P, :], xres[:, t, :]).then_inc(y_stored, 16)
            eng.wait_ge(y_stored, NT * 16)

        @block.gpsimd
        def _(eng):
            eng.memset(kvm[:, 2, :], 0.0).then_inc(bd_zero, 1)
            eng.memset(kvm[:, 3, :], 0.0).then_inc(rows_src, 1)
            for k in (kpad[0], kpad[1], vpad):
                eng.memset(k[:, 0:CHUNK], 0.0).then_inc(pad_zero, 1)
            eng.dma_start(sink[:, :], A["attn_sink"][0].partition_broadcast(P)).then_inc(sink_in, 16)

            eng.wait_ge(rows_src, 1)
            for c in range(NE, CMAX):
                eng.dma_start(moe_rows[c * P:(c + 1) * P, :], kvm[:, 3, :]).then_inc(rows_zero, 16)

            def scale_residual(group):
                for t in range(NT):
                    for k in range(2):
                        wait_full(eng, (group, t, k))
                    if group == "x2T":
                        eng.wait_ge(x2_stored, 16 * NT)
                    eng.tensor_scalar(xres[:, t, :], xres[:, t, :], ALPHA, None, ALU.mult).then_inc(scaled, 1)

            scale_residual("x0T")
            scale_residual("x1T")
            scale_residual("x2T")

            def gather(c):
                col = tokidx[:, c:c + 1] if isinstance(c, int) else tokidx[:, bass.ds(c, 1)]
                wait_read(eng, ("table",))
                eng.tensor_copy(idx_now[:, :], col)
                eng.drain()
                eng.wait_ge(x2_stored, 16 * NT)
                eng.indirect_dma_start(xg, None, x2_rows, bass.IndirectOffsetOnAxis(idx_now[:, 0:1], 0)
                                       ).then_inc(gathered, 16)

            eng.wait_ge(table_done, 1)
            gather(0)
            eng.wait_ge(xtrans_done, 1)
            eng.wait_ge(gathered, 16)
            gather(1)
            n = eng.value_load(ctab[0:1, 0:1], min_val=NE, max_val=CMAX)
            with eng.Fori(1, CMAX) as c:
                with eng.If(c < n):
                    eng.wait_ge(gathered, c * 16 + 16)
                    eng.wait_ge(xtrans_done, c + 1)
                    gather(c + 1)
            eng.wait_ge(slot_done, 1)
            eng.wait_ge(all_stored, 1)
            for t in range(NT):
                for k in range(TOPK):
                    eng.indirect_dma_start(back[:, t * TOPK + k, :], None, moe_rows,
                                           bass.IndirectOffsetOnAxis(slot_i[:, t, k:k + 1], 0)
                                           ).then_inc(back_in[t * TOPK + k], 16)

        @block.scalar
        def _(eng):
            def split_hi(w):
                for h in range(2):
                    eng.wait_ge(stage_in[h], 16 * (w + 1))
                    if w >= RING:
                        wait_full(eng, last_use(w - RING))
                    eng.activation(wring[:, w % RING, 0, h * 1024:(h + 1) * 1024], stage[:, h, :],
                                   ACT.Copy).then_inc(w_hi, 1)

            def actT_tiles(group, t):
                for k in range(2):
                    wait_full(eng, (group, t, k))
                    eng.activation(actT[:, 0, 4 * k:4 * k + 4, t * P:(t + 1) * P],
                                   bank((group, t, k)).rearrange("p (k t) -> p k t", t=P),
                                   ACT.Copy).then_inc(actT_hi, 1)

            def inverse_deviation(n, t):
                eng.wait_ge(var_ready, n * NT + t + 1)
                eng.activation(rstd[:, t:t + 1], rstd[:, t:t + 1], ACT.Sqrt).then_inc(rstd_ready, 1)

            eng.wait_ge(sp_abs, 1)
            eng.activation(sp[:, 1, :], sp[:, 0, :], ACT.Exp, scale=-1.0).then_inc(sp_exp, 1)
            inverse_deviation(0, 0)
            split_hi(0)
            for t in range(NT):
                if t + 1 < NT:
                    inverse_deviation(0, t + 1)
                actT_tiles("x0T", t)
            split_hi(1)
            split_hi(2)
            eng.wait_ge(pad_zero, 3)
            for n, kind in enumerate(IN_KIND):
                wait_full(eng, ("in", n))
                src = bank(("in", n))
                if kind == "xl":
                    i = eng.activation(xl[:, n, :], src, ACT.Copy)
                    free(i, ("in", n))
                elif kind == "g":
                    free(eng.activation(gel[:, n - 4, :], src, ACT.Gelu_apprx_tanh), ("in", n))
                else:
                    dst = kpad[0][:, CHUNK:] if kind == "k" else vpad[:, CHUNK:] if kind == "v" else qs[:, n - 10, :]
                    i = eng.activation(dst, src, ACT.Copy)
                    free(i, ("in", n))
                if n % 2 and n // 2 + 3 < 11:
                    split_hi(n // 2 + 3)

            for ft in range(FT):
                wait_full(eng, ("gate", ft, 0))
                i = eng.activation(ra[:, ft, :], bank(("gate", ft, 0)), ACT.Sigmoid, bias=fv("b_r", ft))
                free(i, ("gate", ft, 0))
                wait_full(eng, ("gate", ft, 1))
                eng.activation(bank(("gate", ft, 1)), bank(("gate", ft, 1)), ACT.Sigmoid,
                               bias=fv("b_i", ft)).then_inc(sig_i, 1)
            eng.wait_ge(rows_zero, 16 * EXTRA)
            for b in range(2):
                wait_full(eng, ("vwin", b))
                i = eng.activation(vwin[:, 4 * b:4 * b + 4, :],
                                   bank(("vwin", b)).rearrange("p (c v) -> p c v", v=P), ACT.Copy)
                free(i, ("vwin", b))

            eng.wait_ge(sp_done, 1)
            wait_read(eng, *[("gate", ft, 0) for ft in range(FT)])

            def decays(ft):
                eng.activation(th[:, ft, :], ra[:, ft, :], ACT.Tanh, scale=sp[:, 6, ft:ft + 1]).then_inc(decay, 1)
                eng.wait_ge(decay, 2 * ft + 1)
                eng.activation(ra[:, ft, :], ra[:, ft, :], ACT.Exp, scale=sp[:, 7, ft:ft + 1]).then_inc(decay, 1)

            def soft_exp(t):
                b = t % 2
                eng.wait_ge(row_max, t + 1)
                if t >= 2:
                    for k in range(2):
                        wait_full(eng, ("PT", t - 2, k))
                for h in range(HEADS):
                    par, hp = h % 2, h // 2
                    i = eng.activation(prob[:, b, h, :], bank(("S", t, par))[:, hp * P:(hp + 1) * P], ACT.Exp,
                                       bias=nmx[:, b, h:h + 1], scale=HD ** -0.5, accum_out=psm[:, b, h:h + 1])
                    if hp == 3:
                        free(i, ("S", t, par))
                eng.activation(esk[:, b, :], esk[:, b, :], ACT.Exp).then_inc(exp_done, 1)

            def prob_T(t):
                for k in range(2):
                    wait_full(eng, ("PT", t, k))
                    if t >= 1:
                        wait_full(eng, ("O", t - 1))
                    i = eng.activation(probT[:, 4 * k:4 * k + 4, :],
                                       bank(("PT", t, k)).rearrange("p (h q) -> p h q", q=P), ACT.Copy)
                    free(i, ("PT", t, k))

            def att_split(t):
                s = slice(t * P, (t + 1) * P)
                eng.wait_ge(att_y, t + 1)
                eng.activation(actT[:, 0, 0:4, s], qs[:, :, s], ACT.Copy).then_inc(att_hi, 1)

            def att_square(t):
                g = ("O", t)
                eng.wait_ge(att_lo, t + 1)
                i = eng.activation(qs[:, :, t * P:(t + 1) * P], bank(g).rearrange("p (f t) -> p f t", t=P), ACT.Square)
                free(i, g)

            soft_exp(0)
            for ft in range(FT):
                decays(ft)
            soft_exp(1)
            for ft in range(FT):
                eng.wait_ge(gain_sq, ft + 1)
                eng.activation(th[:, ft, :], th[:, ft, :], ACT.Sqrt).then_inc(gain, 1)
            for t in range(NT):
                prob_T(t)
                if t + 2 < NT:
                    soft_exp(t + 2)
                att_split(t)
                if t >= 1:
                    att_square(t - 1)
            att_square(NT - 1)

            for m in range(MT):
                for k in range(2):
                    wait_full(eng, ("memT", m, k))
                    eng.activation(memT[:, 0, 4 * k:4 * k + 4, m * P:(m + 1) * P],
                                   bank(("memT", m, k)).rearrange("p (k t) -> p k t", t=P),
                                   ACT.Copy).then_inc(memT_hi, 1)

            def lru_out(ft):
                s = eng
                s.wait_ge(lru_y, ft + 1)
                s.activation(actT[:, 0, FT + ft, :], xl[:, ft, :], ACT.Copy, scale=fv("g_lru", ft)
                             ).then_inc(lru_hi, 1)
                s.activation(ra[:, ft, :], xl[:, ft, :], ACT.Square).then_inc(lru_sq, 1)

            mk0, mv0 = first_piece["mk"], first_piece["mv"]
            for q in range(4):
                for n in (2 * q, 2 * q + 1):
                    wait_full(eng, ("mk", n))
                    i = eng.activation(mkT[:, n, :], bank(("mk", n))[:, 0:MEM], ACT.Copy)
                    free(i, ("mk", n))
                split_hi(mk0 + q + 3)
                lru_out(q)
            for q in range(4):
                for m in range(MT):
                    wait_full(eng, ("mv", q, m))
                    i = eng.activation(mvv[:, m, q * 256:(q + 1) * 256], bank(("mv", q, m))[:, 0:256], ACT.Copy)
                    free(i, ("mv", q, m))
                split_hi(mv0 + q + 3)
            o0 = first_piece["out"]
            eng.wait_ge(ms_ready, 1)
            eng.activation(rms[:, :, :], rms[:, :, :], ACT.Sqrt).then_inc(rms_ready, 1)
            split_hi(o0 + 3)
            split_hi(o0 + 4)
            for t in range(NT):
                inverse_deviation(1, t)
                if t >= 2:
                    actT_tiles("x1T", t - 2)
            split_hi(o0 + 5)
            actT_tiles("x1T", 2)
            split_hi(o0 + 6)
            actT_tiles("x1T", 3)

            def m_exps(h):
                b = h % 2
                eng.wait_ge(m_max, h + 1)
                if h >= 2:
                    wait_full(eng, ("mPT", h - 2, 1))
                for t in range(NT):
                    i = eng.activation(mprob[:, b, t, :], bank(("mS", h, t // 2))[:, (t % 2) * MEM:(t % 2 + 1) * MEM],
                                       ACT.Exp, bias=nmx[:, b, t:t + 1], scale=MHD ** -0.5,
                                       accum_out=psm[:, b, t:t + 1])
                    if t % 2:
                        free(i, ("mS", h, t // 2))

            def m_queries(h):
                for n in range(2):
                    wait_full(eng, ("mq", h, n))
                    i = eng.activation(mq[:, 2 * h + n, :], bank(("mq", h, n)), ACT.Copy)
                    free(i, ("mq", h, n))

            def m_out_hi(h):
                for n in range(2):
                    wait_full(eng, ("mO", h, n))
                    eng.activation(actT[:, 0, 2 * h + n, :], bank(("mO", h, n)), ACT.Copy).then_inc(mo_hi, 1)

            def m_prob_T(h):
                for m in range(MT):
                    wait_full(eng, ("mPT", h, m))
                    if h >= 2:
                        wait_full(eng, ("mO", h - 2, 1))
                    i = eng.activation(mpT[:, h % 2, m, :], bank(("mPT", h, m)), ACT.Copy)
                    free(i, ("mPT", h, m))

            q0 = first_piece["mq"]
            for h in range(MH + 2):
                if h < MH:
                    m_queries(h)
                    if q0 + h + 3 < len(pieces):
                        split_hi(q0 + h + 3)
                if 2 <= h:
                    m_prob_T(h - 2)
                if 1 <= h <= MH:
                    m_exps(h - 1)
                if h >= 4:
                    m_out_hi(h - 4)
            m_out_hi(2)
            m_out_hi(3)
            split_hi(len(pieces) - 1)

            for t in range(NT + 2):
                if t < NT:
                    inverse_deviation(2, t)
                for k in range(2 if t >= 2 else 0):
                    g = ("x2T", t - 2, k)
                    wait_full(eng, g)
                    wait_full(eng, ("mO", 3, 1))
                    i = eng.activation(x2T[:, 4 * k:4 * k + 4, (t - 2) * P:(t - 1) * P],
                                       bank(g).rearrange("p (k t) -> p k t", t=P), ACT.Copy)
                    free(i, g)

            def load_d(i, e):
                w = A["w_down_e"][0, e] if isinstance(e, int) else \
                    A["w_down_e"][0, bass.ds(e, 1)].rearrange("a k n -> (a k) n")
                eng.dma_start(d_w[:, i], w[i * 256:(i + 1) * 256, :].rearrange("(k p) n -> p k n", p=P)
                              ).then_inc(d_in[i], 16)

            load_d(0, 0)
            load_d(1, 0)
            eng.wait_ge(onehots, 1)
            eng.activation(below_exp, below, ACT.Exp).then_inc(onehots, 1)

            def silu(c):
                eng.wait_ge(gateup_done, c + 1)
                eng.activation(silu_g, psum[:, 2, :], ACT.Silu).then_inc(silu_done, 1)

            def evac_x(c):
                eng.wait_ge(xtrans_done, c + 1)
                eng.activation(xgT[:, 4:8, :], psum[:, 1, :].rearrange("p (k s) -> p k s", s=P), ACT.Copy
                               ).then_inc(xgT_b, 1)

            def evac_o(c, stored):
                eng.wait_ge(down_done, c + 1)
                if stored is not None:
                    eng.wait_ge(o_stored, stored)
                eng.activation(moe_o[:, 512:], psum[:, 6, :], ACT.Copy).then_inc(o_hi, 1)

            def store_o(c):
                eng.wait_ge(o_lo, c + 1)
                eng.wait_ge(o_hi, c + 1)
                rows = moe_rows[c * P:(c + 1) * P, :] if isinstance(c, int) else moe_rows[bass.ds(c * P, P), :]
                eng.dma_start(rows, moe_o).then_inc(o_stored, 16)

            evac_x(0)
            silu(0)
            evac_x(1)
            eng.wait_ge(table_done, 1)
            n = eng.value_load(ctab[0:1, 0:1], min_val=NE, max_val=CMAX)

            def act_chunk(c, stored):
                silu(c)
                evac_o(c - 1, stored)
                e = eng.value_load(ctab[0:1, c + 1:c + 2] if isinstance(c, int) else ctab[0:1, bass.ds(c + 1, 1)],
                                   min_val=0, max_val=NE - 1)
                load_d(0, e)
                load_d(1, e)
                store_o(c - 1)
                evac_x(c + 1)

            act_chunk(1, None)
            with eng.Fori(2, CMAX) as c:
                with eng.If(c < n):
                    act_chunk(c, 16 * (c - 1))
            last = eng.value_load(ctab[0:1, 1 + CMAX:2 + CMAX], min_val=NE - 1, max_val=CMAX - 1)
            evac_o(last, 16 * last)
            store_o(last)
            eng.wait_ge(o_stored, 16 * n)
            eng.activation(esk[:, 0, 0:1], esk[:, 0, 1:2], ACT.Copy).then_inc(all_stored, 1)
            for t in range(NT):
                inverse_deviation(3, t)


        @block.vector
        def _(eng):
            steps = [0]

            def link(ins):
                steps[0] += 1
                ins.then_inc(dve_step, 1)
                eng.wait_ge(dve_step, steps[0])

            def split_lo(w):
                for h in range(2):
                    eng.wait_ge(w_hi, 2 * w + h + 1)
                    s = slice(h * 1024, (h + 1) * 1024)
                    eng.tensor_tensor(wring[:, w % RING, 1, s], stage[:, h, :],
                                      wring[:, w % RING, 0, s].bitcast(F32), ALU.subtract).then_inc(w_lo, 1)

            def layer_norm(n, t):
                x = xres[:, t, :]
                for h in range(2):
                    last = eng.bn_stats(stats[:, t, h, :], x[:, h * 512:(h + 1) * 512])
                link(last)
                link(eng.bn_aggr(mv[:, t, :], stats[:, t, :, :]))
                link(eng.tensor_scalar(rstd[:, t:t + 1], mv[:, t, 1:2], EPS, None, ALU.add))
                eng.reciprocal(rstd[:, t:t + 1], rstd[:, t:t + 1]).then_inc(var_ready, 1)
                eng.wait_ge(lngb_in, 32 * (n + 1))
                link(eng.scalar_tensor_tensor(x, x, mv[:, t, 0:1], lngb[:, 0, :], ALU.subtract, ALU.mult))
                eng.wait_ge(rstd_ready, n * NT + t + 1)
                i = eng.scalar_tensor_tensor(x, x, rstd[:, t:t + 1], lngb[:, 1, :], ALU.mult, ALU.add)
                i.then_inc(y_ready if n == 3 else ln_done, 1)

            actT_count = [0]

            def actT_lo_tile(group, t):
                for k in range(2):
                    actT_count[0] += 1
                    eng.wait_ge(actT_hi, actT_count[0])
                    d = slice(4 * k, 4 * k + 4)
                    s = slice(t * P, (t + 1) * P)
                    i = eng.tensor_tensor(actT[:, 1, d, s], bank((group, t, k)).rearrange("p (k t) -> p k t", t=P),
                                          actT[:, 0, d, s].bitcast(F32), ALU.subtract)
                    free(i, (group, t, k))

            lam = feat[:, FEAT["lam"], :]
            eng.wait_ge(small_in, 16 * 10)
            link(eng.tensor_scalar(sp[:, 5, :], lam, -1.0, None, ALU.mult))
            eng.tensor_tensor(sp[:, 0, :], sp[:, 5, :], lam, ALU.max).then_inc(sp_abs, 1)
            for t in range(NT):
                eng.wait_ge(x_in[t], 16)
                layer_norm(0, t)
                if t == 0:
                    split_lo(0)
                if t >= 1:
                    actT_lo_tile("x0T", t - 1)
            actT_lo_tile("x0T", NT - 1)
            split_lo(1)
            split_lo(2)

            eng.wait_ge(sp_exp, 1)
            e1, z, z2, p = sp[:, 1, :], sp[:, 2, :], sp[:, 3, :], sp[:, 4, :]
            link(eng.tensor_scalar(z, e1, 2.0, None, ALU.add))
            link(eng.reciprocal(z, z))
            link(eng.tensor_tensor(z, z, e1, ALU.mult))
            link(eng.tensor_tensor(z2, z, z, ALU.mult))
            link(eng.tensor_scalar(p, z2, 1.0 / 15, None, ALU.mult))
            for k in (13, 11, 9, 7, 5, 3):
                link(eng.scalar_tensor_tensor(p, p, 1.0 / k, z2, ALU.add, ALU.mult))
            link(eng.scalar_tensor_tensor(p, p, 1.0, z, ALU.add, ALU.mult))
            link(eng.tensor_scalar(sp[:, 5, :], lam, -1.0, 0.0, ALU.mult, ALU.max))
            link(eng.scalar_tensor_tensor(p, p, 2.0, sp[:, 5, :], ALU.mult, ALU.add))
            link(eng.tensor_scalar(sp[:, 6, :], p, LRU_C, None, ALU.mult))
            eng.tensor_scalar(sp[:, 7, :], p, -LRU_C, None, ALU.mult).then_inc(sp_done, 1)

            def conv(ft):
                wait_read(eng, ("in", ft))
                x, y = xl[:, ft, :], xc[:, ft, :]
                link(eng.tensor_scalar(y, x, fv("conv3", ft), fv("conv_b", ft), ALU.mult, ALU.add))
                for s in (1, 2, 3):
                    i = eng.scalar_tensor_tensor(y[:, s:], x[:, :T - s], fv(f"conv{3 - s}", ft), y[:, s:],
                                                 ALU.mult, ALU.add)
                    if s < 3:
                        link(i)
                i.then_inc(xc_done, 1)

            for n in range(7):
                if n < 2:
                    conv(2 * n)
                    conv(2 * n + 1)
                if n + 3 < 11:
                    split_lo(n + 3)

            for ft in range(FT):
                eng.wait_ge(sig_i, ft + 1)
                i = eng.tensor_tensor(xc[:, ft, :], xc[:, ft, :], bank(("gate", ft, 1)), ALU.mult)
                free(i, ("gate", ft, 1))
            eng.wait_ge(rot_in, 16)
            for n in range(5):
                dst = kpad[0][:, CHUNK:] if n == 0 else qs[:, n - 1, :]
                b = bank(("rope", n))
                wait_full(eng, ("rope", n))
                eng.tensor_tensor(b, b, rot[:, 1, :], ALU.mult)
                link(eng.tensor_tensor(dst, dst, rot[:, 0, :], ALU.mult))
                i = eng.tensor_tensor(dst, dst, b, ALU.add)
                free(i, ("rope", n))
                if n == 0:
                    wait_read(eng, ("rope", 0))
                    eng.wait_ge(pad_zero, 3)
                    eng.tensor_copy(kpad[1][0:64, CHUNK:], kpad[0][64:128, CHUNK:])
                    eng.tensor_copy(kpad[1][64:128, CHUNK:], kpad[0][0:64, CHUNK:]).then_inc(kswap, 1)

            eng.wait_ge(sink_in, 16)

            def soft_max(t):
                b = t % 2
                for par in range(2):
                    g = ("S", t, par)
                    wait_full(eng, g)
                    s = bank(g).rearrange("p (h k) -> p h k", k=P)
                    if t == 0:
                        link(eng.tensor_tensor(s, s, mask0.unsqueeze(1).to_broadcast([P, 4, P]), ALU.add))
                    i = eng.tensor_reduce(mx[:, b, par::2], s, AX, ALU.max)
                link(i)
                link(eng.scalar_tensor_tensor(mx[:, b, :], mx[:, b, :], HD ** -0.5, sink[:, :], ALU.mult, ALU.max))
                eng.tensor_scalar(nmx[:, b, :], mx[:, b, :], -1.0, None, ALU.mult)
                eng.tensor_tensor(esk[:, b, :], sink[:, :], mx[:, b, :], ALU.subtract).then_inc(row_max, 1)

            def soft_norm(t):
                b = t % 2
                eng.wait_ge(exp_done, t + 1)
                link(eng.tensor_tensor(rden[:, b, :], psm[:, b, :], esk[:, b, :], ALU.add))
                link(eng.reciprocal(rden[:, b, :], rden[:, b, :]))
                eng.tensor_tensor(prob[:, b], prob[:, b], rden[:, b, :].unsqueeze(2).to_broadcast([P, HEADS, P]),
                                  ALU.mult).then_inc(prob_done, 1)

            def att_out(t):
                g = ("O", t)
                wait_full(eng, g)
                eng.tensor_tensor(qs[:, :, t * P:(t + 1) * P], bank(g).rearrange("p (f t) -> p f t", t=P),
                                  feat[:, FEAT["g_att"], :].unsqueeze(2).to_broadcast([P, FT, P]), ALU.mult
                                  ).then_inc(att_y, 1)

            def att_lo_t(t):
                s = slice(t * P, (t + 1) * P)
                eng.wait_ge(att_hi, t + 1)
                eng.tensor_tensor(actT[:, 1, 0:4, s], qs[:, :, s], actT[:, 0, 0:4, s].bitcast(F32),
                                  ALU.subtract).then_inc(att_lo, 1)

            def lru(ft):
                eng.wait_ge(decay, 2 * ft + 2)
                a, h, y = ra[:, ft, :], th[:, ft, :], xl[:, ft, :]
                link(eng.tensor_tensor(y, a, a, ALU.mult))
                link(eng.scalar_tensor_tensor(h, y, 1.0, h, ALU.add, ALU.mult))
                eng.tensor_scalar(h, h, 0.0, None, ALU.max).then_inc(gain_sq, 1)

            def lru_scan(ft):
                a, h, y = ra[:, ft, :], th[:, ft, :], xl[:, ft, :]
                eng.wait_ge(gain, ft + 1)
                link(eng.tensor_tensor(h, h, xc[:, ft, :], ALU.mult))
                link(eng.tensor_tensor_scan(y, a, h, 0.0, ALU.mult, ALU.add))
                eng.tensor_tensor(y, y, gel[:, ft, :], ALU.mult).then_inc(lru_y, 1)

            def lru_lo_t(ft):
                eng.wait_ge(lru_hi, ft + 1)
                eng.scalar_tensor_tensor(actT[:, 1, FT + ft, :], xl[:, ft, :], fv("g_lru", ft),
                                         actT[:, 0, FT + ft, :].bitcast(F32), ALU.mult, ALU.subtract
                                         ).then_inc(lru_lo, 1)

            soft_max(0)
            soft_norm(0)
            soft_max(1)
            for ft in range(FT):
                lru(ft)
            soft_norm(1)
            for t in range(NT):
                if t + 2 < NT:
                    soft_max(t + 2)
                att_out(t)
                lru_scan(t)
                if t + 2 < NT:
                    soft_norm(t + 2)
                att_lo_t(t)

            for m in range(MT):
                for k in range(2):
                    eng.wait_ge(memT_hi, 2 * m + k + 1)
                    d = slice(4 * k, 4 * k + 4)
                    s = slice(m * P, (m + 1) * P)
                    i = eng.tensor_tensor(memT[:, 1, d, s], bank(("memT", m, k)).rearrange("p (k t) -> p k t", t=P),
                                          memT[:, 0, d, s].bitcast(F32), ALU.subtract)
                    free(i, ("memT", m, k))
            mk0, mv0, o0 = first_piece["mk"], first_piece["mv"], first_piece["out"]
            for q in range(4):
                split_lo(mk0 + q + 3)
                lru_lo_t(q)
            for q in range(4):
                split_lo(mv0 + q + 3)
            for b in range(2):
                g = ("sq", b)
                wait_full(eng, g)
                free(eng.tensor_scalar(rms[:, b, :], bank(g)[:, 0:NT], 1.0 / D_ATT, EPS, ALU.mult, ALU.add), g)
            wait_read(eng, ("sq", 0), ("sq", 1))
            eng.reciprocal(rms[:, :, :], rms[:, :, :]).then_inc(ms_ready, 1)
            eng.wait_ge(rms_ready, 1)
            eng.wait_ge(scaled, NT)
            for h in range(2):
                for t in range(NT):
                    x = xres[:, t, h * 512:(h + 1) * 512]
                    for b in range(2):
                        g = ("out", h, t, b)
                        wait_full(eng, g)
                        i = eng.scalar_tensor_tensor(x, bank(g), rms[:, b, t:t + 1], x, ALU.mult, ALU.add)
                        free(i, g)
                        wait_read(eng, g)
                    if h == 1:
                        layer_norm(1, t)
                        if t >= 2:
                            actT_lo_tile("x1T", t - 2)
                if h == 0:
                    split_lo(o0 + 3)
                    split_lo(o0 + 4)
            split_lo(o0 + 5)
            actT_lo_tile("x1T", 2)
            split_lo(o0 + 6)
            actT_lo_tile("x1T", 3)

            def m_maxes(h):
                b = h % 2
                for n in range(2):
                    g = ("mS", h, n)
                    wait_full(eng, g)
                    i = eng.tensor_reduce(mx[:, b, 2 * n:2 * n + 2], bank(g).rearrange("p (t m) -> p t m", m=MEM),
                                          AX, ALU.max)
                link(i)
                eng.tensor_scalar(nmx[:, b, 0:NT], mx[:, b, 0:NT], -(MHD ** -0.5), None, ALU.mult
                                  ).then_inc(m_max, 1)

            def m_norm(h):
                b = h % 2
                wait_read(eng, ("mS", h, 0), ("mS", h, 1))
                link(eng.reciprocal(rden[:, b, 0:NT], psm[:, b, 0:NT]))
                eng.tensor_tensor(mprob[:, b], mprob[:, b], rden[:, b, 0:NT].unsqueeze(2).to_broadcast([P, NT, MEM]),
                                  ALU.mult).then_inc(m_prob, 1)

            def m_out_lo(h):
                for n in range(2):
                    eng.wait_ge(mo_hi, 2 * h + n + 1)
                    i = eng.tensor_tensor(actT[:, 1, 2 * h + n, :], bank(("mO", h, n)),
                                          actT[:, 0, 2 * h + n, :].bitcast(F32), ALU.subtract)
                    free(i, ("mO", h, n))

            q0 = first_piece["mq"]
            for h in range(MH + 2):
                if h < MH and q0 + h + 3 < len(pieces):
                    split_lo(q0 + h + 3)
                if 1 <= h <= MH:
                    m_maxes(h - 1)
                    m_norm(h - 1)
                if h >= 4:
                    m_out_lo(h - 4)
            m_out_lo(2)
            m_out_lo(3)
            split_lo(len(pieces) - 1)

            eng.wait_ge(scaled, 2 * NT)
            for h in range(2):
                for t in range(NT):
                    x = xres[:, t, h * 512:(h + 1) * 512]
                    g = ("wo", h, t)
                    wait_full(eng, g)
                    i = eng.tensor_tensor(x, bank(g), x, ALU.add)
                    free(i, g)
                    wait_read(eng, g)
                    if h == 1:
                        layer_norm(2, t)

            lg = rtmp(NT, NG + NE)
            eng.wait_ge(small_in, 16 * (10 + 2 + 1 + NG))
            g = ("logits",)
            wait_full(eng, g)
            i = eng.tensor_tensor(lg, bank(g)[:, 0:NT * (NG + NE)].rearrange("p (t e) -> p t e", t=NT),
                                  b_rt[:, :].unsqueeze(1).to_broadcast([P, NT, NG + NE]), ALU.add)
            free(i, g)
            wait_read(eng, g)
            wgt = cst[:, C_WG:C_WG + EPG].unsqueeze(1).to_broadcast([P, NT, EPG])
            tmp4 = rtmp(NT, 4)
            m1 = rtmp(NT)

            def first_hot(dst, v, m):
                link(eng.tensor_tensor(tmp4, v, m.unsqueeze(2).to_broadcast([P, NT, 4]), ALU.is_equal))
                link(eng.tensor_tensor(tmp4, tmp4, wgt, ALU.mult))
                link(eng.tensor_reduce(m1, tmp4, AX, ALU.max))
                link(eng.tensor_tensor(dst, tmp4, m1.unsqueeze(2).to_broadcast([P, NT, 4]), ALU.is_equal))

            gl = lg[:, :, 0:NG]
            gm, gh = rtmp(NT), rtmp(NT, NG)
            gx = rtmp(NT, NG)
            link(eng.tensor_reduce(gm, gl, AX, ALU.max))
            first_hot(gh, gl, gm)
            link(eng.tensor_tensor(gx, gl, gm.unsqueeze(2).to_broadcast([P, NT, NG]), ALU.subtract))
            pick = rtmp(NT, NG, EPG)
            link(eng.tensor_tensor(pick, lg[:, :, NG:].rearrange("p t (g e) -> p t g e", g=NG),
                                   gh.unsqueeze(3).to_broadcast([P, NT, NG, EPG]), ALU.mult))
            el = rtmp(NT, EPG)
            link(eng.tensor_reduce(el, pick.rearrange("p t g e -> p t e g"), AX, ALU.add))
            em1, em2, eh1, eh2, el2 = rtmp(NT), rtmp(NT), rtmp(NT, EPG), rtmp(NT, EPG), rtmp(NT, EPG)
            link(eng.tensor_reduce(em1, el, AX, ALU.max))
            first_hot(eh1, el, em1)
            link(eng.scalar_tensor_tensor(el2, eh1, 2 * NEG, el, ALU.mult, ALU.add))
            link(eng.tensor_reduce(em2, el2, AX, ALU.max))
            first_hot(eh2, el2, em2)
            eng.tensor_tensor(below[:, :, 0], em2, em1, ALU.subtract)
            link(eng.tensor_copy(below[:, :, 1:], gx))
            for k, eh in enumerate((eh1, eh2)):
                m = moh[:, k].rearrange("p t (g e) -> p t g e", g=NG)
                for gi in range(NG):
                    i = eng.tensor_tensor(m[:, :, gi, :], eh, gh[:, :, gi:gi + 1].to_broadcast([P, NT, EPG]), ALU.mult)
            link(i)
            eng.tensor_tensor(moh[:, 2], moh[:, 0], moh[:, 1], ALU.add).then_inc(onehots, 1)

            g = ("rank",)
            wait_full(eng, g)
            rk_all = rtmp(NT + 1, NE)
            i = eng.tensor_copy(rk_all, bank(g)[:, 0:(NT + 1) * NE].rearrange("p (t e) -> p t e", e=NE))
            free(i, g)
            wait_read(eng, g)
            cnt = rk_all[:, NT, :]
            xe, xs = rtmp(NE), rtmp(NE)
            big = rtmp(3, NE)
            thr = cst[:, C_THR:C_THR + 3]
            link(eng.tensor_tensor(big, cnt.unsqueeze(1).to_broadcast([P, 3, NE]),
                                   thr.unsqueeze(2).to_broadcast([P, 3, NE]), ALU.is_gt))
            link(eng.tensor_reduce(xe, big.rearrange("p j e -> p e j"), AX, ALU.add))
            one_row = cst[:, C_ONES:C_ONES + NE]
            link(eng.tensor_tensor_scan(xs, one_row, xe, 0.0, ALU.mult, ALU.add))
            endb = rtmp(EXTRA, NE)
            ctf = rtmp(1 + CMAX)
            link(eng.tensor_tensor(endb, xs.unsqueeze(1).to_broadcast([P, EXTRA, NE]),
                                   cst[:, C_CHK:C_CHK + EXTRA].unsqueeze(2).to_broadcast([P, EXTRA, NE]),
                                   ALU.is_le))
            eng.tensor_reduce(ctf[:, 1 + NE:], endb, AX, ALU.add)
            eng.tensor_copy(ctf[:, 1:1 + NE], cst[:, C_EXP:C_EXP + NE])
            link(eng.tensor_scalar(ctf[:, 0:1], xs[:, NE - 1:NE], float(NE), None, ALU.add))
            eng.tensor_scalar(ctab[0:1, 1:1 + CMAX], ctf[0:1, 1:], float(NE - 1), None, ALU.min)
            eng.tensor_scalar(ctab[0:1, 1 + CMAX:], ctf[0:1, 0:1], -1.0, None, ALU.add)
            eng.tensor_copy(ctab[0:1, 0:1], ctf[0:1, 0:1]).then_inc(table_done, 1)
            start = rtmp(NE)
            link(eng.tensor_tensor(start, xs, xe, ALU.subtract))
            link(eng.tensor_scalar(start, start, float(NE - 1), None, ALU.add))
            prod = rtmp(NT, NE)
            ev, rv, sv = rtmp(TOPK, NT), rtmp(TOPK, NT), rtmp(TOPK, NT)
            for k in range(TOPK):
                for dst, src in ((ev, cst[:, C_EXP:C_EXP + NE].unsqueeze(1).to_broadcast([P, NT, NE])),
                                 (rv, rk_all[:, 0:NT, :]),
                                 (sv, start.unsqueeze(1).to_broadcast([P, NT, NE]))):
                    link(eng.tensor_tensor(prod, moh[:, k], src, ALU.mult))
                    link(eng.tensor_reduce(dst[:, k, :], prod, AX, ALU.add))
            jv, hv, cv, row = rtmp(TOPK, NT), rtmp(TOPK, NT), rtmp(TOPK, NT), rtmp(TOPK, NT)
            link(eng.tensor_scalar(jv, rv, float(P), None, ALU.is_ge))
            eng.tensor_copy(hv, jv)
            for j in (2, 3):
                link(eng.scalar_tensor_tensor(jv, rv, float(j * P), jv, ALU.is_ge, ALU.add))
            link(eng.scalar_tensor_tensor(row, jv, -float(P), rv, ALU.mult, ALU.add))
            link(eng.tensor_tensor(sv, sv, jv, ALU.add))
            link(eng.tensor_tensor(sv, sv, ev, ALU.subtract))
            link(eng.tensor_tensor(sv, sv, hv, ALU.mult))
            link(eng.tensor_tensor(cv, sv, ev, ALU.add))
            iota_r = cst[:, C_ROW:C_ROW + P]
            iota_c = cst[:, C_CHK:C_CHK + IDXC]
            for k in range(TOPK):
                for t in range(NT):
                    eng.tensor_scalar(selT[:, k * NT + t, :], iota_r, row[:, k, t:t + 1], None, ALU.is_equal)
                    i = eng.tensor_scalar(sel_c[:, k * NT + t, :], iota_c, cv[:, k, t:t + 1],
                                          cst[:, C_TOK + t:C_TOK + t + 1], ALU.is_equal, ALU.mult)
            i.then_inc(selected, 1)
            slot_f = rtmp(TOPK, NT)
            link(eng.scalar_tensor_tensor(slot_f, cv, float(P), row, ALU.mult, ALU.add))
            eng.tensor_copy(slot_i[:, :, :], slot_f.rearrange("p k t -> p t k")).then_inc(slot_done, 1)
            g = ("table",)
            wait_full(eng, g)
            i = eng.tensor_copy(tokidx[:, :], bank(g)[:, 0:IDXC])
            free(i, g)
            eng.wait_ge(onehots, 2)
            den, dg = rtmp(NT), rtmp(NT)
            link(eng.tensor_reduce(dg, below_exp[:, :, 1:], AX, ALU.add))
            link(eng.scalar_tensor_tensor(den, below_exp[:, :, 0], 1.0, dg, ALU.add, ALU.mult))
            link(eng.reciprocal(gates[:, :, 0], den))
            link(eng.tensor_tensor(gates[:, :, 1], gates[:, :, 0], below_exp[:, :, 0], ALU.mult))

            def evac_x(c):
                eng.wait_ge(xtrans_done, c + 1)
                eng.tensor_copy(xgT[:, 0:4, :], psum[:, 0, :].rearrange("p (k s) -> p k s", s=P)
                                ).then_inc(xgT_a, 1)

            def h_mul(c):
                eng.wait_ge(silu_done, c + 1)
                eng.tensor_tensor(h_act, silu_g, psum[:, 3, :], ALU.mult).then_inc(h_ready, 1)

            def evac_h(c):
                eng.wait_ge(htrans_done, c + 1)
                eng.tensor_copy(hT, psum[:, 4, :].rearrange("p (f s) -> p f s", s=P)).then_inc(hT_ready, 1)

            def evac_o(c, stored):
                eng.wait_ge(down_done, c + 1)
                if stored is not None:
                    eng.wait_ge(o_stored, stored)
                eng.tensor_copy(moe_o[:, 0:512], psum[:, 5, :]).then_inc(o_lo, 1)

            evac_x(0)
            h_mul(0)
            evac_x(1)
            evac_h(0)
            n = eng.value_load(ctab[0:1, 0:1], min_val=NE, max_val=CMAX)

            def dve_chunk(c, stored):
                h_mul(c)
                evac_o(c - 1, stored)
                evac_x(c + 1)
                evac_h(c)

            dve_chunk(1, None)
            with eng.Fori(2, CMAX) as c:
                with eng.If(c < n):
                    dve_chunk(c, 16 * (c - 1))
            last = eng.value_load(ctab[0:1, 1 + CMAX:2 + CMAX], min_val=NE - 1, max_val=CMAX - 1)
            evac_o(last, 16 * last)

            eng.wait_ge(scaled, 3 * NT)
            for t in range(NT):
                for k in range(TOPK):
                    eng.wait_ge(back_in[t * TOPK + k], 16)
                    link(eng.scalar_tensor_tensor(xres[:, t, :], back[:, t * TOPK + k, :], gates[:, t, k:k + 1],
                                                  xres[:, t, :], ALU.mult, ALU.add))
                layer_norm(3, t)

        @block.tensor
        def _(eng):
            def mm3(out, s, m, first, last):
                eng.matmul(out, s[0], m[0], start=first, stop=False)
                eng.matmul(out, s[0], m[1], start=False, stop=False)
                return eng.matmul(out, s[1], m[0], start=False, stop=last)

            def wpiece(w, width):
                return [wring[:, w % RING, i, :].rearrange("p (k n) -> p k n", n=width) for i in range(2)]

            def transposes(g, srcs, width=P):
                wait_free(eng, g)
                for j, s in enumerate(srcs):
                    i = eng.transpose(bank(g)[:, j * width:(j + 1) * width], s, ident)
                full(i, g)

            def rows_T(group, t):
                for k in range(2):
                    transposes((group, t, k), [xres[:, t, (4 * k + j) * P:(4 * k + j + 1) * P] for j in range(4)])

            eng.wait_ge(const_in, 16)
            for t in range(NT):
                eng.wait_ge(ln_done, t + 1)
                rows_T("x0T", t)
            wait_read(eng, *[("x0T", t, k) for t in range(NT) for k in range(2)])
            for n in range(D_IN // P):
                w, c0 = in_slices(n)
                eng.wait_ge(w_lo, 2 * w + 2)
                wait_free(eng, ("in", n))
                wp = wpiece(w, 256)
                for k in range(KT):
                    i = mm3(bank(("in", n)), [q[:, k, c0:c0 + P] for q in wp],
                            [actT[:, j, k, :] for j in range(2)], k == 0, k == KT - 1)
                full(i, ("in", n))
            eng.wait_ge(bd_in, 64)
            for ft in range(FT):
                eng.wait_ge(xc_done, ft + 1)
                for w in range(2):
                    g = ("gate", ft, w)
                    wait_free(eng, g)
                    full(eng.matmul(bank(g), gate_bd[:, w, ft, :], xc[:, ft, :], start=True, stop=True), g)
            for n in range(5):
                wait_read(eng, ("in", 8 if n == 0 else 9 + n))
                wait_free(eng, ("rope", n))
                src = kpad[0][:, CHUNK:] if n == 0 else qs[:, n - 1, :]
                full(eng.matmul(bank(("rope", n)), perm, src, start=True, stop=True), ("rope", n))
            eng.wait_ge(pad_zero, 3)
            wait_read(eng, ("in", 9))
            for b in range(2):
                transposes(("vwin", b), [vpad[:, c * CHUNK:c * CHUNK + P] for c in range(4 * b, 4 * b + 4)])

            def scores(t):
                for par in range(2):
                    g = ("S", t, par)
                    wait_free(eng, g)
                    ps = slice(par * 64, par * 64 + 64)
                    for hp in range(4):
                        kk = kpad[0 if hp // 2 == par else 1]
                        for c in range(2):
                            ch = 2 * t + c
                            i = eng.matmul(psum[c * 64:c * 64 + 64, G[g] % 8, hp * P:(hp + 1) * P],
                                           qs[ps, hp, ch * CHUNK:(ch + 1) * CHUNK],
                                           kk[ps, ch * CHUNK:ch * CHUNK + P], start=True, stop=True)
                    full(i, g)

            def prob_T(t):
                eng.wait_ge(prob_done, t + 1)
                for k in range(2):
                    transposes(("PT", t, k), [prob[:, t % 2, 4 * k + j, :] for j in range(4)])

            def att_out(t):
                g = ("O", t)
                wait_read(eng, ("PT", t, 0), ("PT", t, 1), ("vwin", 0), ("vwin", 1))
                wait_free(eng, g)
                for c in range(2):
                    for kv in range(2):
                        for par in range(2):
                            dst = psum[par * 64:par * 64 + 64, G[g] % 8, :].rearrange("p (f t) -> p f t", t=P)
                            i = eng.matmul(dst[:, 2 * kv:2 * kv + 2, c * 64:c * 64 + 64],
                                           vwin[:, 2 * t + c, kv * 64:kv * 64 + 64],
                                           probT[:, 4 * kv + par:4 * kv + par + 3:2, c * 64:c * 64 + 64],
                                           start=True, stop=True)
                full(i, g)

            wait_read(eng, *[("rope", n) for n in range(5)])
            eng.wait_ge(kswap, 1)
            scores(0)
            scores(1)
            for t in range(NT):
                prob_T(t)
                att_out(t)
                if t + 2 < NT:
                    scores(t + 2)

            eng.wait_ge(mem_in, 16)
            for m in range(MT):
                for k in range(2):
                    transposes(("memT", m, k), [memr[:, m, (4 * k + j) * P:(4 * k + j + 1) * P] for j in range(4)])
            wait_read(eng, *[("memT", m, k) for m in range(MT) for k in range(2)])
            for n in range(KT):
                w = first_piece["mk"] + n // 2
                c0 = (n % 2) * P
                eng.wait_ge(w_lo, 2 * w + 2)
                wait_free(eng, ("mk", n))
                wp = wpiece(w, 256)
                for k in range(KT):
                    i = mm3(bank(("mk", n))[:, 0:MEM], [q[:, k, c0:c0 + P] for q in wp],
                            [memT[:, j, k, :] for j in range(2)], k == 0, k == KT - 1)
                full(i, ("mk", n))
            for q in range(4):
                w = first_piece["mv"] + q
                eng.wait_ge(w_lo, 2 * w + 2)
                wp = wpiece(w, 256)
                for m in range(MT):
                    wait_free(eng, ("mv", q, m))
                    for k in range(KT):
                        i = mm3(bank(("mv", q, m))[:, 0:256], [memT[:, j, k, m * P:(m + 1) * P] for j in range(2)],
                                [x[:, k, :] for x in wp], k == 0, k == KT - 1)
                    full(i, ("mv", q, m))

            wait_read(eng, *[("O", t) for t in range(NT)])
            eng.wait_ge(lru_sq, FT)
            for b in range(2):
                g = ("sq", b)
                wait_free(eng, g)
                for t in range(NT):
                    for f in range(FT):
                        src = qs[:, f, t * P:(t + 1) * P] if b == 0 else ra[:, f, t * P:(t + 1) * P]
                        i = eng.matmul(bank(g)[:, t:t + 1], src, ones[:, 0:1], start=f == 0, stop=f == FT - 1)
                full(i, g)

            def norm_T(n, t):
                eng.wait_ge(ln_done, n * NT + t + 1)
                rows_T(f"x{n}T", t)

            eng.wait_ge(att_lo, NT)
            eng.wait_ge(lru_lo, FT)
            w0 = first_piece["out"]
            for h in range(2):
                for t in range(NT):
                    for b in range(2):
                        w = w0 + 2 * h + b
                        eng.wait_ge(w_lo, 2 * w + 2)
                        g = ("out", h, t, b)
                        wait_free(eng, g)
                        wp = wpiece(w, 512)
                        for k in range(4):
                            i = mm3(bank(g), [actT[:, j, 4 * b + k, t * P:(t + 1) * P] for j in range(2)],
                                    [x[:, k, :] for x in wp], k == 0, k == 3)
                        full(i, g)
                    if h == 1 and t >= 2:
                        norm_T(1, t - 2)
            norm_T(1, 2)
            norm_T(1, 3)

            def m_query(h):
                w = first_piece["mq"] + h
                eng.wait_ge(w_lo, 2 * w + 2)
                wp = wpiece(w, 256)
                for n in range(2):
                    wait_free(eng, ("mq", h, n))
                    for k in range(KT):
                        i = mm3(bank(("mq", h, n)), [x[:, k, n * P:(n + 1) * P] for x in wp],
                                [actT[:, j, k, :] for j in range(2)], k == 0, k == KT - 1)
                    full(i, ("mq", h, n))

            def m_scores(h):
                wait_read(eng, ("mq", h, 0), ("mq", h, 1))
                for n in range(2):
                    g = ("mS", h, n)
                    wait_free(eng, g)
                    for u in range(2):
                        t = 2 * n + u
                        for k in range(2):
                            i = eng.matmul(bank(g)[:, u * MEM:(u + 1) * MEM],
                                           mq[:, 2 * h + k, t * P:(t + 1) * P], mkT[:, 2 * h + k, :],
                                           start=k == 0, stop=k == 1)
                    full(i, g)

            def m_prob_T(h):
                eng.wait_ge(m_prob, h + 1)
                for m in range(MT):
                    transposes(("mPT", h, m), [mprob[:, h % 2, t, m * P:(m + 1) * P] for t in range(NT)])

            def m_out(h):
                wait_read(eng, ("mPT", h, 0), ("mPT", h, 1))
                for n in range(2):
                    g = ("mO", h, n)
                    wait_free(eng, g)
                    for m in range(MT):
                        i = eng.matmul(bank(g), mvv[:, m, (2 * h + n) * P:(2 * h + n + 1) * P],
                                       mpT[:, h % 2, m, :], start=m == 0, stop=m == 1)
                    full(i, g)

            wait_read(eng, *[("x1T", t, k) for t in range(NT) for k in range(2)])
            wait_read(eng, *[("mk", n) for n in range(KT)])
            wait_read(eng, *[("mv", q, m) for q in range(4) for m in range(MT)])
            for h in range(MH + 2):
                if h < MH:
                    m_query(h)
                if 2 <= h:
                    m_prob_T(h - 2)
                if 1 <= h <= MH:
                    m_scores(h - 1)
                if h >= 4:
                    m_out(h - 4)
            m_out(2)
            m_out(3)

            wait_read(eng, *[("mO", h, n) for h in range(MH) for n in range(2)])
            w0 = first_piece["wo"]
            for h in range(2):
                for t in range(NT):
                    g = ("wo", h, t)
                    wait_free(eng, g)
                    for b in range(2):
                        w = w0 + 2 * h + b
                        eng.wait_ge(w_lo, 2 * w + 2)
                        wp = wpiece(w, 512)
                        for k in range(4):
                            i = mm3(bank(g), [actT[:, j, 4 * b + k, t * P:(t + 1) * P] for j in range(2)],
                                    [x[:, k, :] for x in wp], b + k == 0, b == 1 and k == 3)
                    full(i, g)
                    if h == 1 and t >= 2:
                        norm_T(2, t - 2)
            norm_T(2, 2)
            norm_T(2, 3)
            g = ("logits",)
            wait_read(eng, *[("x2T", t, k) for t in range(NT) for k in range(2)])
            eng.wait_ge(small_in, 16 * (10 + 2 + 1 + NG))
            wait_free(eng, g)
            W = NG + NE
            for t in range(NT):
                for k in range(KT):
                    i = eng.matmul(bank(g)[:, t * W:(t + 1) * W], x2T[:, k, t * P:(t + 1) * P], w_rt[:, k, :],
                                   start=k == 0, stop=k == KT - 1)
            full(i, g)
            g = ("rank",)
            eng.wait_ge(onehots, 1)
            wait_free(eng, g)
            for t in range(NT + 1):
                dst = bank(g)[:, t * NE:(t + 1) * NE]
                for s in range(min(t + 1, NT)):
                    i = eng.matmul(dst, tri if s == t else ones, moh[:, 2, s, :], start=s == 0,
                                   stop=s == min(t, NT - 1))
            full(i, g)
            g = ("table",)
            eng.wait_ge(selected, 1)
            wait_free(eng, g)
            for j in range(TOPK * NT):
                i = eng.matmul(bank(g)[:, 0:IDXC], selT[:, j, :], sel_c[:, j, :], start=j == 0,
                               stop=j == TOPK * NT - 1)
            full(i, g)

            def x_T(c):
                eng.wait_ge(gathered, 16 * c + 16)
                for k in range(KT):
                    i = eng.transpose(psum[:, k // 4, (k % 4) * P:(k % 4 + 1) * P], xg[:, k * P:(k + 1) * P], ident)
                i.then_inc(xtrans_done, 1)

            def gate_up(c, prev):
                eng.wait_ge(xgT_a, c + 1)
                eng.wait_ge(xgT_b, c + 1)
                if prev:
                    eng.wait_ge(h_ready, c)
                for k in range(KT):
                    if k % 4 == 0:
                        eng.wait_ge(gu_in[(k // 4) * 2], 16 * c + 16)
                        eng.wait_ge(gu_in[(k // 4) * 2 + 1], 16 * c + 16)
                    eng.matmul(psum[:, 2, :], xgT[:, k, :], g_w[:, k // 4, k % 4, :], start=k == 0, stop=k == KT - 1)
                    i = eng.matmul(psum[:, 3, :], xgT[:, k, :], u_w[:, k // 4, k % 4, :], start=k == 0,
                                   stop=k == KT - 1)
                    if k == 3:
                        i.then_inc(gu_half, 1)
                i.then_inc(gateup_done, 1)

            def h_T(c):
                eng.wait_ge(h_ready, c + 1)
                for f in range(FFT):
                    i = eng.transpose(psum[:, 4, f * P:(f + 1) * P], h_act[:, f * P:(f + 1) * P], ident)
                i.then_inc(htrans_done, 1)

            def down(c, prev):
                eng.wait_ge(hT_ready, c + 1)
                if prev:
                    eng.wait_ge(o_lo, c)
                    eng.wait_ge(o_hi, c)
                for f in range(FFT):
                    if f % 2 == 0:
                        eng.wait_ge(d_in[f // 2], 16 * c + 16)
                    for hf in range(2):
                        i = eng.matmul(psum[:, 5 + hf, :], hT[:, f, :], d_w[:, f // 2, f % 2, hf * 512:(hf + 1) * 512],
                                       start=f == 0, stop=f == FFT - 1)
                i.then_inc(down_done, 1)

            for b in range(8):
                last = max(v for v in G.values() if v % 8 == b)
                eng.wait_ge(psum_read[b], last // 8 + 1)
            x_T(0)
            gate_up(0, False)
            x_T(1)
            h_T(0)
            n = eng.value_load(ctab[0:1, 0:1], min_val=NE, max_val=CMAX)

            def pe_chunk(c, prev):
                gate_up(c, True)
                down(c - 1, prev)
                x_T(c + 1)
                h_T(c)

            pe_chunk(1, False)
            with eng.Fori(2, CMAX) as c:
                with eng.If(c < n):
                    pe_chunk(c, True)
            last = eng.value_load(ctab[0:1, 1 + CMAX:2 + CMAX], min_val=NE - 1, max_val=CMAX - 1)
            down(last, True)


_INS = ['x', 'mem', 'ln_in_g', 'ln_in_b', 'w_in', 'attn_sink', 'conv_w', 'conv_b', 'w_rgate', 'b_rgate',
        'w_igate', 'b_igate', 'lru_lambda', 'norm_attn_g', 'norm_lru_g', 'w_out', 'ln1_g', 'ln1_b', 'wq_mem',
        'wk_mem', 'wv_mem', 'wo_mem', 'ln2_g', 'ln2_b', 'w_router_group', 'b_router_group', 'w_router_expert',
        'b_router_expert', 'w_gate_e', 'w_up_e', 'w_down_e', 'ln3_g', 'ln3_b']


def kernel(**inputs):
    import concourse.bacc as bacc
    from concourse.bass_utils import run_bass_kernel_spmd

    nc = bacc.Bacc("TRN2", target_bir_lowering=False, num_devices=1)
    arrays, args = {}, {}
    for name in _INS:
        a = np.ascontiguousarray(inputs[name])
        arrays[f"in_{name}"] = a
        args[name] = nc.dram_tensor(f"in_{name}", a.shape, mybir.dt.from_np(a.dtype), kind="ExternalInput").ap()
    cst, rot = constants()
    aps = []
    for name, a in (("consts", cst), ("rots", rot)):
        arrays[name] = a
        aps.append(nc.dram_tensor(name, a.shape, F32, kind="ExternalInput").ap())
    y = nc.dram_tensor("y_out", (1, T, D), F32, kind="ExternalOutput").ap()
    encoder_layer(nc, args, aps[0], aps[1], y)
    r = run_bass_kernel_spmd(nc, [arrays], core_ids=[0])
    return r.results[0]["y_out"]
```

```python
from contextlib import ExitStack

import numpy as np

import concourse.bass as bass
from concourse import mybir

F32 = mybir.dt.float32
F32R = mybir.dt.float32r
F16 = mybir.dt.float16
I32 = mybir.dt.int32
U32 = mybir.dt.uint32
ALU = mybir.AluOpType
ACT = mybir.ActivationFunctionType
AX = mybir.AxisListType.X

P = 128
D = 1024
T = 512
NT = T // P
KT = D // P
CHUNK = 64
HD = 64
HEADS = 8
KVH = 2
D_ATT = HEADS * HD
D_KV = KVH * HD
D_LRU = 512
FT = D_LRU // P
TAPS = 4
LRU_C = 8.0
D_IN = D_ATT + 2 * D_KV + 2 * D_LRU
MEM = 256
MT = MEM // P
MH = 4
MHD = D // MH
NG = 4
EPG = 4
NE = NG * EPG
TOPK = 2
F = 512
FFT = F // P
ALPHA = 2.0 ** 0.25
EPS = 1e-5
NEG = -1e30
EXTRA = (TOPK * T - 1) // P
CMAX = NE + EXTRA
T_N, T_LAST, T_PREV, T_EXP = 0, 1, 2, 3
T_NEW = T_EXP + CMAX
TAB_W = T_NEW + CMAX

C_ID, C_TRI, C_ONES, C_PERM, C_MASK, C_ROW = (P * i for i in range(6))
C_CHK = 6 * P
C_EXP = C_CHK + CMAX
C_THR = C_EXP + NE
C_WG = C_THR + 3
C_TOK = C_WG + EPG
CONST_W = C_TOK + NT


def constants():
    c = np.zeros((P, CONST_W), np.float32)
    i = np.arange(P)
    c[:, C_ID:C_ID + P] = i[:, None] == i[None, :]
    c[:, C_TRI:C_TRI + P] = i[:, None] < i[None, :]
    c[:, C_ONES:C_ONES + P] = 1.0
    src = (i // HD) * HD + (i % HD + HD // 2) % HD
    c[:, C_PERM:C_PERM + P] = i[:, None] == src[None, :]
    c[:CHUNK, C_MASK:C_MASK + CHUNK] = NEG
    c[:, C_ROW:C_ROW + P] = i[None, :]
    c[:, C_CHK:C_CHK + CMAX] = np.arange(CMAX)[None, :]
    c[:, C_EXP:C_EXP + NE] = np.arange(NE)[None, :]
    c[:, C_THR:C_THR + 3] = P * np.arange(1, 4)[None, :]
    c[:, C_WG:C_WG + EPG] = EPG - np.arange(EPG)[None, :]
    c[:, C_TOK:C_TOK + NT] = i[:, None] + P * np.arange(NT)[None, :]
    inv = np.float32(10000.0) ** (-np.arange(0, HD, 2, dtype=np.float32) / np.float32(HD))
    ang = np.arange(T, dtype=np.float32)[None, :] * inv[i % (HD // 2)][:, None].astype(np.float32)
    sign = np.where(i % HD < HD // 2, -1.0, 1.0).astype(np.float32)[:, None]
    rot = np.stack([np.cos(ang), np.sin(ang) * sign], 1).astype(np.float32)
    return c, rot


def psum_groups():
    g = [("memT", m, k) for m in range(MT) for k in range(2)]
    g += [("mk", n) for n in range(KT)]
    g += [("x0T", t, k) for t in range(NT) for k in range(2)]
    g += [("mv", q, m) for q in range(4) for m in range(MT)]
    g += [("in", n) for n in range(D_IN // P)]
    g += [("gate", ft, w) for ft in range(FT) for w in range(2)]
    g += [("rope", n) for n in range(5)] + [("vwin", 0), ("vwin", 1)]
    g += [("S", t, par) for t in range(2) for par in range(2)]
    for t in range(NT):
        g += [("PT", t, 0), ("PT", t, 1), ("O", t)]
        if t + 2 < NT:
            g += [("S", t + 2, 0), ("S", t + 2, 1)]
    g += [("sq", 0), ("sq", 1)]
    g += [("out", 0, t, b) for t in range(NT) for b in range(2)]
    for t in range(NT):
        g += [("out", 1, t, 0), ("out", 1, t, 1)]
        if t >= 2:
            g += [("x1T", t - 2, 0), ("x1T", t - 2, 1)]
    g += [("x1T", t, k) for t in (2, 3) for k in range(2)]
    for h in range(MH + 2):
        if h < MH:
            g += [("mq", h, n) for n in range(2)]
        if 2 <= h:
            g += [("mPT", h - 2, m) for m in range(MT)]
        if 1 <= h <= MH:
            g += [("mS", h - 1, n) for n in range(2)]
        if h >= 4:
            g += [("mO", h - 4, n) for n in range(2)]
    g += [("mO", 2, 0), ("mO", 2, 1), ("mO", 3, 0), ("mO", 3, 1)]
    g += [("wo", 0, t) for t in range(NT)]
    for t in range(NT):
        g += [("wo", 1, t)]
        if t >= 2:
            g += [("x2T", t - 2, 0), ("x2T", t - 2, 1)]
    g += [("x2T", t, k) for t in (2, 3) for k in range(2)]
    g += [("logits",), ("rank",), ("table",)]
    return {name: n for n, name in enumerate(g)}


def weight_pieces(w_in, wk, wv, w_out, wq, wo):
    cols = [("mk", wk, 256 * c) for c in range(4)] + [("mv", wv, 256 * c) for c in range(4)]
    cols += [("in", w_in, 256 * c) for c in (3, 4, 5, 6, 2, 0, 1)]
    out = []
    for name, w, c0 in cols:
        if name in ("mk", "mv"):
            out.append((name, [w[:, c0:c0 + 256]], 256))
        else:
            out.append((name, [w[h * 512:(h + 1) * 512, c0:c0 + 256] for h in range(2)], 256))
    for name, w in (("out", w_out), ("mq", wq), ("wo", wo)):
        for q in range(4):
            if name == "mq":
                out.append((name, [w[h * 512:(h + 1) * 512, q * 256:(q + 1) * 256] for h in range(2)], 256))
            else:
                n, k = q // 2, q % 2
                out.append((name, [w[k * 512 + h * 256:k * 512 + (h + 1) * 256, n * 512:(n + 1) * 512]
                                   for h in range(2)], 512))
    return out


def encoder_layer(nc, A, consts, rots, y_out):
    G = psum_groups()
    pieces = weight_pieces(A["w_in"][0], A["wk_mem"][0], A["wv_mem"][0], A["w_out"][0],
                           A["wq_mem"][0], A["wo_mem"][0])
    first_piece = {}
    for n, (name, _, _) in enumerate(pieces):
        first_piece.setdefault(name, n)
    mk0, mv0, in0, o0, q0, wo0 = (first_piece[n] for n in ("mk", "mv", "in", "out", "mq", "wo"))
    RING = 3
    EARLY = in0
    EARLY_AT = [0, 1, 2, 3, 5]

    def last_use(w):
        name = pieces[w][0]
        q = w - first_piece[name]
        return {"in": ("in", 2 * q + 1), "mk": ("mk", 2 * q + 1), "mv": ("mv", q, MT - 1), "mq": ("mq", q, 1),
                "out": ("out", q // 2, NT - 1, q % 2), "wo": ("wo", q // 2, NT - 1)}[name]

    ctx = ExitStack()
    with ctx:
        def sb(name, shape, dt=F32):
            return ctx.enter_context(nc.sbuf_tensor(name, shape, dt))

        offset = {}

        def sb_at(name, shape, dt=F32):
            offset[name] = nc.sbuf_base
            return sb(name, shape, dt)

        def alias(name, of, shape, dt):
            return nc.alloc_sbuf_tensor_at(name, shape, dt, offset=offset[of])

        def sem(name):
            return ctx.enter_context(nc.semaphore(name))

        xres = sb("xres", [P, NT, D])
        actT = sb_at("actT", [P, 2, KT, T], F32R)
        memT = sb_at("memT", [P, 2, KT, MEM], F32R)
        qs = sb_at("qs", [P, 4, T])
        wring = sb("wring", [P, RING, 2, 2048], F32R)
        stage = sb_at("stage", [P, 2, 1024])
        kvm = sb_at("kvm", [P, 4, 1024])
        scr = sb_at("scr", [P, 6, 2048])
        lngb = sb("lngb", [P, 2, D])
        cst = sb("cst", [P, CONST_W])
        w_rt = sb("w_rt", [P, KT, NG + NE])
        b_rt = sb("b_rt", [P, NG + NE])
        sink = sb("sink", [P, HEADS])
        feat = sb("feat", [P, 11, FT])
        sp = sb("sp", [P, 8, FT])
        stats = sb("stats", [P, NT, 2, 6])
        mv = sb("mv", [P, NT, 2])
        rstd = sb("rstd", [P, NT])
        rms = sb("rms", [P, 2, NT])
        mx = sb("mx", [P, 2, HEADS])
        nmx = sb("nmx", [P, 2, HEADS])
        psm = sb("psm", [P, 2, HEADS])
        esk = sb("esk", [P, 2, HEADS])
        rden = sb("rden", [P, 2, HEADS])
        gates = sb("gates", [P, NT, TOPK])
        slot_i = sb("slot_i", [P, NT, TOPK], U32)
        tokidx = sb("tokidx", [P, CMAX], U32)
        idx_now = sb("idx_now", [P, 1], U32)
        ctab = sb("ctab", [1, TAB_W], I32)

        ident = cst[:, C_ID:C_ID + P]
        tri = cst[:, C_TRI:C_TRI + P]
        ones = cst[:, C_ONES:C_ONES + P]
        perm = cst[:, C_PERM:C_PERM + P]
        mask0 = cst[:, C_MASK:C_MASK + P]

        att = alias("att", "memT", [P, 4, 1024], F32)
        prob = att[:, 0:2, :].rearrange("p b (h k) -> p b h k", h=HEADS)
        probT = att[:, 2, :].rearrange("p (h q) -> p h q", h=HEADS)
        vwin = att[:, 3, :].rearrange("p (c v) -> p c v", c=T // CHUNK)
        rot = lngb[:, 0, :].rearrange("p (a t) -> p a t", a=2)
        gate_bd = lngb[:, 1, :].rearrange("p (g f j) -> p g f j", g=2, f=FT)
        mkT = kvm[:, 0:2, :].rearrange("p a (k m) -> p (a k) m", m=MEM)
        mvv = kvm[:, 2:4, :]
        mprob = scr[:, 3, :].rearrange("p (b t m) -> p b t m", b=2, t=NT)
        mq = scr[:, 4:6, :].rearrange("p a (k t) -> p (a k) t", t=T)
        mpT = qs[:, :, :].rearrange("p (b m) t -> p b m t", b=2)
        x2T = kvm[:, :, :].rearrange("p a (k t) -> p (a k) t", t=T)
        xl, xc, gel, ra, th = (scr[:, i, :].rearrange("p (f t) -> p f t", f=FT) for i in range(5))
        KP = CHUNK + T
        kpad = [scr[:, 5, i * KP:(i + 1) * KP] for i in range(2)]
        vpad = scr[:, 5, 2 * KP:3 * KP]
        memr = scr[:, 4, :].rearrange("p (m d) -> p m d", m=MT)
        moe_land = alias("moe_land", "actT", [P, 4, 2048], F32)
        moe_split = alias("moe_split", "scr", [P, 3, 2, 2048], F32R)
        xg = kvm[:, 0, :]
        xgT_hi = alias("kvm_r", "kvm", [P, 4, 1024], F32R)[:, 1, :]
        moe_o = kvm[:, 2, :]
        silu_g = kvm[:, 3, 0:512]
        h_act = kvm[:, 3, 512:1024]
        hT_hi = alias("qs_r", "qs", [P, 4, T], F32R)[:, 3, :]
        stage_r = alias("stage_r", "stage", [P, 2, 1024], F32R)
        xgT_lo, hT_lo = stage_r[:, 1, :], stage_r[:, 0, 0:512]
        att_land = att[:, :, :].rearrange("p (i a) b -> p i (a b)", i=2)

        def moe_landed(i):
            return att_land[:, i, :] if i < 2 else moe_land[:, i - 2, :]

        def moe_w(i, part):
            return wring[:, i, part, :] if i < 3 else moe_split[:, i - 3, part, :]

        back = scr[:, 0:4, :].rearrange("p a (b n) -> p (a b) n", n=D)

        rt = qs[:, 0:3, :].rearrange("p a b -> p (a b)")
        rt_at = [0]

        def rtmp(*shape):
            n = int(np.prod(shape))
            a = rt[:, rt_at[0]:rt_at[0] + n]
            rt_at[0] += n
            assert rt_at[0] <= 3 * T
            if len(shape) == 1:
                return a
            names = "abc"[:len(shape)]
            return a.rearrange(f"p ({' '.join(names)}) -> p {' '.join(names)}",
                               **{k: s for k, s in zip(names, shape)})

        below, below_exp = rtmp(NT, 1 + NG), rtmp(NT, 1 + NG)
        moh = rtmp(2, NT, NE)
        half = alias("half", "stage", [P, 4096], F16)
        selT = half[:, 0:1024].rearrange("p (j r) -> p j r", r=P)
        sel_c = half[:, 1024:1024 + 8 * CMAX].rearrange("p (j c) -> p j c", c=CMAX)
        moh_h = half[:, 1280:1280 + NT * NE].rearrange("p (t e) -> p t e", t=NT)
        tri_h, ones_h = half[:, 1408:1408 + P], half[:, 1536:1536 + P]

        psum = ctx.enter_context(nc.psum_tensor("psum", [P, 8, 512], F32))

        x2_rows = nc.dram_tensor("x2_rows", (T, D), F32, kind="Internal").ap()
        moe_rows = nc.dram_tensor("moe_rows", (CMAX * P, D), F32, kind="Internal").ap()

        psum_full = [sem(f"psum_full{b}") for b in range(8)]
        psum_read = [sem(f"psum_read{b}") for b in range(8)]
        x_in = [sem(f"x_in{t}") for t in range(NT)]
        const_in = sem("const_in")
        small_in = sem("small_in")
        router_in = sem("router_in")
        sink_in = sem("sink_in")
        rot_in = sem("rot_in")
        bd_in = sem("bd_in")
        bd_zero = sem("bd_zero")
        pad_zero = sem("pad_zero")
        rows_src = sem("rows_src")
        rows_zero = sem("rows_zero")
        lngb_in = sem("lngb_in")
        mem_in = sem("mem_in")
        early_in = [sem(f"early_in{i}") for i in range(len(EARLY_AT))]
        stage_in = [sem(f"stage_in{h}") for h in range(2)]
        w_hi = sem("w_hi")
        w_lo = sem("w_lo")
        dve_step = sem("dve_step")
        ln_done = sem("ln_done")
        actT_hi = sem("actT_hi")
        scaled = sem("scaled")
        xc_done = sem("xc_done")
        kswap = sem("kswap")
        sig_i = sem("sig_i")
        sp_abs = sem("sp_abs")
        sp_exp = sem("sp_exp")
        sp_done = sem("sp_done")
        decay = sem("decay")
        gelu_done = sem("gelu_done")
        lru_y = sem("lru_y")
        lru_sq = sem("lru_sq")
        lru_hi = sem("lru_hi")
        lru_lo = sem("lru_lo")
        row_max = sem("row_max")
        exp_done = sem("exp_done")
        prob_done = sem("prob_done")
        att_y = sem("att_y")
        att_hi = sem("att_hi")
        att_lo = sem("att_lo")
        memT_hi = sem("memT_hi")
        m_max = sem("m_max")
        m_prob = sem("m_prob")
        mo_hi = sem("mo_hi")
        var_ready = sem("var_ready")
        rstd_ready = sem("rstd_ready")
        ms_ready = sem("ms_ready")
        rms_ready = sem("rms_ready")
        gain_sq = sem("gain_sq")
        gain = sem("gain")
        x2_stored = sem("x2_stored")
        onehots = sem("onehots")
        selected = sem("selected")
        table_done = sem("table_done")
        slot_done = sem("slot_done")
        moe_in = [sem(f"moe_in{i}") for i in range(6)]
        moe_hi = [sem(f"moe_hi{i}") for i in range(6)]
        moe_lo = [sem(f"moe_lo{i}") for i in range(6)]
        gu_half = sem("gu_half")
        gateup_done = sem("gateup_done")
        silu_done = sem("silu_done")
        h_ready = sem("h_ready")
        htrans_done = sem("htrans_done")
        hT_hi_done = sem("hT_hi_done")
        hT_ready = sem("hT_ready")
        down_done = sem("down_done")
        o_read = sem("o_read")
        o_stored = sem("o_stored")
        xtrans_done = sem("xtrans_done")
        xgT_hi_done = sem("xgT_hi_done")
        xgT_ready = sem("xgT_ready")
        all_stored = sem("all_stored")
        gathered = sem("gathered")
        back_in = [sem(f"back_in{i}") for i in range(NT * TOPK)]
        y_ready = sem("y_ready")
        y_stored = sem("y_stored")

        def bank(g):
            return psum[:, G[g] % 8, :]

        def wait_full(eng, g):
            eng.wait_ge(psum_full[G[g] % 8], G[g] // 8 + 1)

        def wait_free(eng, g):
            if G[g] >= 8:
                eng.wait_ge(psum_read[G[g] % 8], G[g] // 8)

        def full(ins, g):
            ins.then_inc(psum_full[G[g] % 8], 1)

        def free(ins, g):
            ins.then_inc(psum_read[G[g] % 8], 1)

        def wait_read(eng, *groups):
            for g in groups:
                eng.wait_ge(psum_read[G[g] % 8], G[g] // 8 + 1)

        def table(eng, at, lo=0, hi=CMAX):
            return eng.value_load(ctab[0:1, at:at + 1] if isinstance(at, int) else ctab[0:1, bass.ds(at, 1)],
                                  min_val=lo, max_val=hi)

        def expert_of(eng, c):
            return table(eng, c + T_EXP, 0, NE - 1)

        def is_new(eng, c):
            return table(eng, c + T_NEW, 0, 1)

        FEAT = {n: i for i, n in enumerate(("conv0", "conv1", "conv2", "conv3", "conv_b", "b_r", "b_i",
                                            "lam", "g_att", "g_lru"))}

        def fv(name, ft):
            return feat[:, FEAT[name], ft:ft + 1]

        N_CONST, N_SMALL, N_LN = 1, 10 + 4 + 1, 2
        LN_SEQ = ["ln_in", "ln1", "ln2", "ln3"]

        def in_slices(n):
            return in0 + n // 2, (n % 2) * P

        def landed(w, h):
            if w < EARLY:
                return scr[:, EARLY_AT[w % len(EARLY_AT)], h * 1024:(h + 1) * 1024]
            return stage[:, h, :]

        def wait_landed(eng, w, h):
            if w < EARLY:
                eng.wait_ge(early_in[w % len(EARLY_AT)], 16 * (w // len(EARLY_AT) + 1))
            else:
                eng.wait_ge(stage_in[h], 16 * (w - EARLY + 1))

        IN_KIND = ["xl"] * 4 + ["g"] * 4 + ["k", "v"] + ["q"] * 4
        block = ctx.enter_context(nc.Block())

        @block.sync
        def _(eng):
            def load_ln(name):
                for i, part in enumerate("gb"):
                    v = A[f"{name}_{part}"]
                    v = v if name == "ln_in" else v[0]
                    eng.dma_start(lngb[:, i, :], v.partition_broadcast(P)).then_inc(lngb_in, 16)

            def load_piece(w):
                _, parts, width = pieces[w]
                if w < EARLY:
                    i = w % len(EARLY_AT)
                    if w >= len(EARLY_AT):
                        eng.wait_ge(w_lo, 2 * (w - len(EARLY_AT)) + 2)
                    eng.dma_start(scr[:, EARLY_AT[i], :].rearrange("p (k n) -> p k n", n=width),
                                  parts[0].rearrange("(k p) n -> p k n", p=P)).then_inc(early_in[i], 16)
                    return
                for h in range(2):
                    if w > EARLY:
                        eng.wait_ge(w_lo, 2 * (w - 1) + h + 1)
                    eng.dma_start(stage[:, h, :].rearrange("p (k n) -> p k n", n=width),
                                  parts[h].rearrange("(k p) n -> p k n", p=P)).then_inc(stage_in[h], 16)

            eng.dma_start(memr, A["mem"][0].rearrange("(m p) d -> p m d", p=P)).then_inc(mem_in, 16)
            eng.dma_start(cst[:, :], consts).then_inc(const_in, 16)
            load_piece(0)
            eng.dma_start(xres[:, 0, :], A["x"][0, 0:P, :]).then_inc(x_in[0], 16)
            load_ln("ln_in")
            load_piece(1)
            for t in range(1, NT):
                eng.dma_start(xres[:, t, :], A["x"][0, t * P:(t + 1) * P, :]).then_inc(x_in[t], 16)
            for w in range(2, EARLY + 1):
                load_piece(w)
            for i in range(TAPS):
                eng.dma_start(feat[:, i, :], A["conv_w"][0, i].rearrange("(f p) -> p f", p=P),
                              allow_slow_non_contiguous=True).then_inc(small_in, 16)
            for name, key in (("conv_b", "conv_b"), ("b_r", "b_rgate"), ("b_i", "b_igate"),
                              ("lam", "lru_lambda"), ("g_att", "norm_attn_g"), ("g_lru", "norm_lru_g")):
                eng.dma_start(feat[:, FEAT[name], :], A[key][0].rearrange("(f p) -> p f", p=P),
                              allow_slow_non_contiguous=True).then_inc(small_in, 16)
            eng.wait_ge(ln_done, NT)
            eng.dma_start(rot, rots).then_inc(rot_in, 16)
            eng.wait_ge(bd_zero, 1)
            for g, key in enumerate(("w_rgate", "w_igate")):
                w = A[key][0].rearrange("(f two) i j -> two i f j", two=2)
                for par in range(2):
                    s = slice(par * 64, par * 64 + 64)
                    eng.dma_start(gate_bd[s, g, :, s], w[par]).then_inc(bd_in, 16)
            for w in range(EARLY + 1, o0):
                load_piece(w)
            eng.dma_start(b_rt[:, 0:NG], A["b_router_group"][0].partition_broadcast(P)).then_inc(router_in, 16)
            eng.dma_start(b_rt[:, NG:], A["b_router_expert"][0].rearrange("g e -> (g e)")
                          .partition_broadcast(P)).then_inc(router_in, 16)
            eng.dma_start(w_rt[:, :, 0:NG], A["w_router_group"][0].rearrange("(k p) g -> p k g", p=P),
                          allow_slow_non_contiguous=True).then_inc(router_in, 16)
            for g in range(NG):
                eng.dma_start(w_rt[:, :, NG + g * EPG:NG + (g + 1) * EPG],
                              A["w_router_expert"][0, g].rearrange("(k p) e -> p k e", p=P),
                              allow_slow_non_contiguous=True).then_inc(router_in, 16)
            for w in range(o0, o0 + 4):
                load_piece(w)
            wait_read(eng, *[("rope", n) for n in range(5)])
            wait_full(eng, ("gate", FT - 1, 1))
            load_ln("ln1")
            for w in range(o0 + 4, wo0):
                load_piece(w)
            eng.wait_ge(ln_done, 2 * NT)
            load_ln("ln2")
            for w in range(wo0, len(pieces)):
                load_piece(w)
            def load_moe(i, e):
                key, rows = (("w_gate_e", 0), ("w_up_e", 0), ("w_gate_e", 512), ("w_up_e", 512),
                             ("w_down_e", 0), ("w_down_e", 256))[i]
                w = A[key][0, e] if isinstance(e, int) else A[key][0, bass.ds(e, 1)].rearrange("a k f -> (a k) f")
                n = D if key == "w_down_e" else F
                w = w[rows:rows + P * 2048 // n, :]
                eng.dma_start(moe_landed(i).rearrange("p (k n) -> p k n", n=n),
                              w.rearrange("(k p) n -> p k n", p=P)).then_inc(moe_in[i], 16)

            for i in range(2):
                load_moe(i, 0)
            wait_full(eng, ("wo", 1, NT - 1))
            load_moe(2, 0)
            for t in range(NT):
                eng.wait_ge(ln_done, 2 * NT + t + 1)
                eng.dma_start(x2_rows[t * P:(t + 1) * P, :], xres[:, t, :]).then_inc(x2_stored, 16)
            for i in range(3, 6):
                load_moe(i, 0)
            eng.wait_ge(ln_done, 3 * NT)
            load_ln("ln3")
            def next_expert(e, first=False):
                for i in range(4):
                    eng.wait_ge(moe_lo[i], e)
                    load_moe(i, e)
                if not first:
                    for i in (4, 5):
                        eng.wait_ge(moe_lo[i], e - 1)
                        load_moe(i, e - 1)

            next_expert(1, True)
            with eng.Fori(2, NE) as e:
                next_expert(e)
            for i in (4, 5):
                eng.wait_ge(moe_lo[i], NE - 1)
                load_moe(i, NE - 1)
            for t in range(NT):
                eng.wait_ge(y_ready, t + 1)
                eng.dma_start(y_out[0, t * P:(t + 1) * P, :], xres[:, t, :]).then_inc(y_stored, 16)
            eng.wait_ge(y_stored, NT * 16)

        @block.gpsimd
        def _(eng):
            eng.memset(qs[:, 0:2, :], 0.0).then_inc(rows_src, 1)
            eng.dma_start(sink[:, :], A["attn_sink"][0].partition_broadcast(P)).then_inc(sink_in, 16)
            eng.wait_ge(ln_done, NT)
            eng.memset(lngb[:, 1, :], 0.0).then_inc(bd_zero, 1)
            eng.wait_ge(w_lo, 2 * len(EARLY_AT))
            for k in (kpad[0], kpad[1], vpad):
                eng.memset(k[:, 0:CHUNK], 0.0).then_inc(pad_zero, 1)

            eng.wait_ge(rows_src, 1)
            wait_full(eng, ("mv", 3, MT - 1))
            for c in range(NE, CMAX):
                eng.dma_start(moe_rows[c * P:(c + 1) * P, :], qs[:, 0:2, :]).then_inc(rows_zero, 16)

            def scale_residual(group):
                for t in range(NT):
                    for k in range(2):
                        wait_full(eng, (group, t, k))
                    if group == "x2T":
                        eng.wait_ge(x2_stored, 16 * NT)
                    eng.tensor_scalar(xres[:, t, :], xres[:, t, :], ALPHA, None, ALU.mult).then_inc(scaled, 1)

            scale_residual("x0T")
            scale_residual("x1T")

            def gather(c):
                col = tokidx[:, c:c + 1] if isinstance(c, int) else tokidx[:, bass.ds(c, 1)]
                wait_read(eng, ("table",))
                eng.tensor_copy(idx_now[:, :], col)
                eng.drain()
                eng.wait_ge(x2_stored, 16 * NT)
                eng.indirect_dma_start(xg, None, x2_rows, bass.IndirectOffsetOnAxis(idx_now[:, 0:1], 0)
                                       ).then_inc(gathered, 16)

            eng.wait_ge(table_done, 1)
            gather(0)
            eng.wait_ge(xtrans_done, 1)
            gather(1)
            scale_residual("x2T")
            n = table(eng, T_N, NE, CMAX)
            with eng.Fori(2, CMAX) as c:
                with eng.If(c < n):
                    eng.wait_ge(gathered, c * 16)
                    eng.wait_ge(xtrans_done, c)
                    gather(c)
            eng.wait_ge(slot_done, 1)
            eng.wait_ge(all_stored, 1)
            for t in range(NT):
                for k in range(TOPK):
                    eng.indirect_dma_start(back[:, t * TOPK + k, :], None, moe_rows,
                                           bass.IndirectOffsetOnAxis(slot_i[:, t, k:k + 1], 0)
                                           ).then_inc(back_in[t * TOPK + k], 16)

        @block.scalar
        def _(eng):
            def split_hi(w):
                for h in range(2):
                    wait_landed(eng, w, h)
                    if w >= RING:
                        wait_full(eng, last_use(w - RING))
                    eng.activation(wring[:, w % RING, 0, h * 1024:(h + 1) * 1024], landed(w, h),
                                   ACT.Copy).then_inc(w_hi, 1)

            def actT_tiles(group, t):
                for k in range(2):
                    wait_full(eng, (group, t, k))
                    eng.activation(actT[:, 0, 4 * k:4 * k + 4, t * P:(t + 1) * P],
                                   bank((group, t, k)).rearrange("p (k t) -> p k t", t=P),
                                   ACT.Copy).then_inc(actT_hi, 1)

            def inverse_deviation(n, t):
                eng.wait_ge(var_ready, n * NT + t + 1)
                eng.activation(rstd[:, t:t + 1], rstd[:, t:t + 1], ACT.Sqrt).then_inc(rstd_ready, 1)

            for m in range(MT):
                for k in range(2):
                    wait_full(eng, ("memT", m, k))
                    eng.activation(memT[:, 0, 4 * k:4 * k + 4, m * P:(m + 1) * P],
                                   bank(("memT", m, k)).rearrange("p (k t) -> p k t", t=P),
                                   ACT.Copy).then_inc(memT_hi, 1)
            for w in range(RING):
                split_hi(w)
                inverse_deviation(0, w)
            for q in range(4):
                for n in (2 * q, 2 * q + 1):
                    wait_full(eng, ("mk", n))
                    i = eng.activation(mkT[:, n, :], bank(("mk", n))[:, 0:MEM], ACT.Copy)
                    free(i, ("mk", n))
                split_hi(mk0 + q + RING)
                if q == 0:
                    inverse_deviation(0, 3)
            for t in range(NT):
                actT_tiles("x0T", t)
            for q in range(4):
                for m in range(MT):
                    wait_full(eng, ("mv", q, m))
                    i = eng.activation(mvv[:, m, q * 256:(q + 1) * 256], bank(("mv", q, m))[:, 0:256], ACT.Copy)
                    free(i, ("mv", q, m))
                split_hi(mv0 + q + RING)
            eng.wait_ge(sp_abs, 1)
            eng.activation(sp[:, 1, :], sp[:, 0, :], ACT.Exp, scale=-1.0).then_inc(sp_exp, 1)
            eng.wait_ge(pad_zero, 3)
            for n, kind in enumerate(IN_KIND):
                wait_full(eng, ("in", n))
                if n == IN_KIND.index("q"):
                    eng.wait_ge(rows_zero, 16 * EXTRA)
                src = bank(("in", n))
                if kind == "xl":
                    i = eng.activation(xl[:, n, :], src, ACT.Copy)
                    free(i, ("in", n))
                elif kind == "g":
                    free(eng.activation(gel[:, n - 4, :], src, ACT.Gelu_apprx_tanh), ("in", n))
                else:
                    dst = kpad[0][:, CHUNK:] if kind == "k" else vpad[:, CHUNK:] if kind == "v" else qs[:, n - 10, :]
                    i = eng.activation(dst, src, ACT.Copy)
                    free(i, ("in", n))
                if n % 2:
                    split_hi(in0 + n // 2 + RING)

            for ft in range(FT):
                wait_full(eng, ("gate", ft, 0))
                i = eng.activation(ra[:, ft, :], bank(("gate", ft, 0)), ACT.Sigmoid, bias=fv("b_r", ft))
                free(i, ("gate", ft, 0))
                wait_full(eng, ("gate", ft, 1))
                eng.activation(bank(("gate", ft, 1)), bank(("gate", ft, 1)), ACT.Sigmoid,
                               bias=fv("b_i", ft)).then_inc(sig_i, 1)
            for b in range(2):
                wait_full(eng, ("vwin", b))
                i = eng.activation(vwin[:, 4 * b:4 * b + 4, :],
                                   bank(("vwin", b)).rearrange("p (c v) -> p c v", v=P), ACT.Copy)
                free(i, ("vwin", b))

            eng.wait_ge(sp_done, 1)
            wait_read(eng, *[("gate", ft, 0) for ft in range(FT)])

            def decays(ft):
                eng.activation(th[:, ft, :], ra[:, ft, :], ACT.Tanh, scale=sp[:, 6, ft:ft + 1]).then_inc(decay, 1)
                eng.wait_ge(decay, 2 * ft + 1)
                eng.activation(ra[:, ft, :], ra[:, ft, :], ACT.Exp, scale=sp[:, 7, ft:ft + 1]).then_inc(decay, 1)

            def soft_exp(t):
                b = t % 2
                eng.wait_ge(row_max, t + 1)
                if t >= 2:
                    for k in range(2):
                        wait_full(eng, ("PT", t - 2, k))
                for h in range(HEADS):
                    par, hp = h % 2, h // 2
                    i = eng.activation(prob[:, b, h, :], bank(("S", t, par))[:, hp * P:(hp + 1) * P], ACT.Exp,
                                       bias=nmx[:, b, h:h + 1], scale=HD ** -0.5, accum_out=psm[:, b, h:h + 1])
                    if hp == 3:
                        free(i, ("S", t, par))
                eng.activation(esk[:, b, :], esk[:, b, :], ACT.Exp).then_inc(exp_done, 1)

            def prob_T(t):
                for k in range(2):
                    wait_full(eng, ("PT", t, k))
                    if t >= 1:
                        wait_full(eng, ("O", t - 1))
                    i = eng.activation(probT[:, 4 * k:4 * k + 4, :],
                                       bank(("PT", t, k)).rearrange("p (h q) -> p h q", q=P), ACT.Copy)
                    free(i, ("PT", t, k))

            def att_split(t):
                s = slice(t * P, (t + 1) * P)
                eng.wait_ge(att_y, t + 1)
                eng.activation(actT[:, 0, 0:4, s], qs[:, :, s], ACT.Copy).then_inc(att_hi, 1)

            def att_square(t):
                g = ("O", t)
                eng.wait_ge(att_lo, t + 1)
                i = eng.activation(qs[:, :, t * P:(t + 1) * P], bank(g).rearrange("p (f t) -> p f t", t=P), ACT.Square)
                free(i, g)

            def lru_out(ft):
                eng.wait_ge(lru_y, ft + 1)
                eng.activation(actT[:, 0, FT + ft, :], xl[:, ft, :], ACT.Copy, scale=fv("g_lru", ft)
                               ).then_inc(lru_hi, 1)
                eng.activation(ra[:, ft, :], xl[:, ft, :], ACT.Square).then_inc(lru_sq, 1)

            soft_exp(0)
            for ft in range(FT):
                decays(ft)
            soft_exp(1)
            for ft in range(FT):
                eng.wait_ge(gain_sq, ft + 1)
                eng.activation(th[:, ft, :], th[:, ft, :], ACT.Sqrt).then_inc(gain, 1)
            for t in range(NT):
                prob_T(t)
                if t + 2 < NT:
                    soft_exp(t + 2)
                att_split(t)
                lru_out(t)
                if t >= 1:
                    att_square(t - 1)
            att_square(NT - 1)

            eng.wait_ge(ms_ready, 1)
            eng.activation(rms[:, :, :], rms[:, :, :], ACT.Sqrt).then_inc(rms_ready, 1)
            split_hi(o0 + 3)
            split_hi(o0 + 4)
            for t in range(NT):
                inverse_deviation(1, t)
                if t >= 2:
                    actT_tiles("x1T", t - 2)
            split_hi(o0 + 5)
            actT_tiles("x1T", 2)
            split_hi(o0 + 6)
            actT_tiles("x1T", 3)

            def m_exps(h):
                b = h % 2
                eng.wait_ge(m_max, h + 1)
                if h >= 2:
                    wait_full(eng, ("mPT", h - 2, 1))
                for t in range(NT):
                    i = eng.activation(mprob[:, b, t, :], bank(("mS", h, t // 2))[:, (t % 2) * MEM:(t % 2 + 1) * MEM],
                                       ACT.Exp, bias=nmx[:, b, t:t + 1], scale=MHD ** -0.5,
                                       accum_out=psm[:, b, t:t + 1])
                    if t % 2:
                        free(i, ("mS", h, t // 2))

            def m_queries(h):
                for n in range(2):
                    wait_full(eng, ("mq", h, n))
                    i = eng.activation(mq[:, 2 * h + n, :], bank(("mq", h, n)), ACT.Copy)
                    free(i, ("mq", h, n))

            def m_out_hi(h):
                for n in range(2):
                    wait_full(eng, ("mO", h, n))
                    eng.activation(actT[:, 0, 2 * h + n, :], bank(("mO", h, n)), ACT.Copy).then_inc(mo_hi, 1)

            def m_prob_T(h):
                for m in range(MT):
                    wait_full(eng, ("mPT", h, m))
                    if h >= 2:
                        wait_full(eng, ("mO", h - 2, 1))
                    i = eng.activation(mpT[:, h % 2, m, :], bank(("mPT", h, m)), ACT.Copy)
                    free(i, ("mPT", h, m))

            for h in range(MH + 2):
                if h < MH:
                    m_queries(h)
                    if q0 + h + 3 < len(pieces):
                        split_hi(q0 + h + 3)
                if 2 <= h:
                    m_prob_T(h - 2)
                if 1 <= h <= MH:
                    m_exps(h - 1)
                if h >= 4:
                    m_out_hi(h - 4)
            m_out_hi(2)
            m_out_hi(3)
            split_hi(len(pieces) - 1)

            for t in range(NT + 2):
                if t < NT:
                    inverse_deviation(2, t)
                for k in range(2 if t >= 2 else 0):
                    g = ("x2T", t - 2, k)
                    wait_full(eng, g)
                    wait_full(eng, ("mO", 3, 1))
                    i = eng.activation(x2T[:, 4 * k:4 * k + 4, (t - 2) * P:(t - 1) * P],
                                       bank(g).rearrange("p (k t) -> p k t", t=P), ACT.Copy)
                    free(i, g)

            def moe_split_hi(i, e=0, used=None):
                eng.wait_ge(moe_in[i], 16 * e + 16)
                if used is not None:
                    eng.wait_ge(*used)
                eng.activation(moe_w(i, 0), moe_landed(i), ACT.Copy).then_inc(moe_hi[i], 1)

            wait_full(eng, ("wo", 1, NT - 1))
            for i in range(6):
                moe_split_hi(i)
            eng.wait_ge(onehots, 1)
            eng.activation(below_exp, below, ACT.Exp).then_inc(onehots, 1)

            def silu(c):
                eng.wait_ge(gateup_done, c + 1)
                eng.activation(silu_g, psum[:, 2, :], ACT.Silu).then_inc(silu_done, 1)

            def evac_x(c):
                eng.wait_ge(xtrans_done, c + 1)
                eng.activation(xgT_hi, psum[:, 0:2, :].rearrange("p a b -> p (a b)"), ACT.Copy
                               ).then_inc(xgT_hi_done, 1)

            def evac_h(c):
                eng.wait_ge(htrans_done, c + 1)
                eng.activation(hT_hi, psum[:, 4, :], ACT.Copy).then_inc(hT_hi_done, 1)

            def evac_o(c, stored):
                eng.wait_ge(down_done, c + 1)
                if stored is not None:
                    eng.wait_ge(o_stored, stored)
                eng.activation(moe_o, psum[:, 5:7, :].rearrange("p a b -> p (a b)"), ACT.Copy).then_inc(o_read, 1)
                eng.wait_ge(o_read, c + 1)
                rows = moe_rows[c * P:(c + 1) * P, :] if isinstance(c, int) else moe_rows[bass.ds(c * P, P), :]
                eng.dma_start(rows, moe_o).then_inc(o_stored, 16)

            evac_x(0)
            eng.wait_ge(table_done, 1)
            n = table(eng, T_N, NE, CMAX)

            def new_hi(c, i, used):
                new = is_new(eng, c)
                with eng.If(new > 0):
                    e = expert_of(eng, c)
                    moe_split_hi(i, e, used)
                    moe_split_hi(i + 1, e)

            def act_chunk(c, first=False):
                new_hi(c, 0, (gu_half, c))
                silu(c - 1)
                evac_x(c)
                new_hi(c, 2, (gateup_done, c))
                if not first:
                    evac_o(c - 2, 16 * (c - 2))
                evac_h(c - 1)
                if not first:
                    new_hi(c - 1, 4, (down_done, c - 1))

            act_chunk(1, True)
            with eng.Fori(2, CMAX) as c:
                with eng.If(c < n):
                    act_chunk(c)
            last = table(eng, T_LAST, NE - 1, CMAX - 1)
            silu(last)
            previous = table(eng, T_PREV, NE - 2, CMAX - 2)
            evac_o(previous, 16 * previous)
            evac_h(last)
            new_hi(last, 4, (down_done, last))
            evac_o(last, 16 * last)
            eng.wait_ge(o_stored, 16 * n)
            eng.activation(esk[:, 0, 0:1], esk[:, 0, 1:2], ACT.Copy).then_inc(all_stored, 1)
            for t in range(NT):
                inverse_deviation(3, t)


        @block.vector
        def _(eng):
            steps = [0]

            def link(ins):
                steps[0] += 1
                ins.then_inc(dve_step, 1)
                eng.wait_ge(dve_step, steps[0])

            def split_lo(w):
                for h in range(2):
                    eng.wait_ge(w_hi, 2 * w + h + 1)
                    s = slice(h * 1024, (h + 1) * 1024)
                    eng.tensor_tensor(wring[:, w % RING, 1, s], landed(w, h),
                                      wring[:, w % RING, 0, s].bitcast(F32), ALU.subtract).then_inc(w_lo, 1)

            def layer_norm(n, t):
                x = xres[:, t, :]
                for h in range(2):
                    last = eng.bn_stats(stats[:, t, h, :], x[:, h * 512:(h + 1) * 512])
                link(last)
                link(eng.bn_aggr(mv[:, t, :], stats[:, t, :, :]))
                link(eng.tensor_scalar(rstd[:, t:t + 1], mv[:, t, 1:2], EPS, None, ALU.add))
                eng.reciprocal(rstd[:, t:t + 1], rstd[:, t:t + 1]).then_inc(var_ready, 1)
                eng.wait_ge(lngb_in, 32 * (n + 1))
                link(eng.scalar_tensor_tensor(x, x, mv[:, t, 0:1], lngb[:, 0, :], ALU.subtract, ALU.mult))
                eng.wait_ge(rstd_ready, n * NT + t + 1)
                i = eng.scalar_tensor_tensor(x, x, rstd[:, t:t + 1], lngb[:, 1, :], ALU.mult, ALU.add)
                i.then_inc(y_ready if n == 3 else ln_done, 1)

            actT_count = [0]

            def actT_lo_tile(group, t):
                for k in range(2):
                    actT_count[0] += 1
                    eng.wait_ge(actT_hi, actT_count[0])
                    d = slice(4 * k, 4 * k + 4)
                    s = slice(t * P, (t + 1) * P)
                    i = eng.tensor_tensor(actT[:, 1, d, s], bank((group, t, k)).rearrange("p (k t) -> p k t", t=P),
                                          actT[:, 0, d, s].bitcast(F32), ALU.subtract)
                    free(i, (group, t, k))

            for m in range(MT):
                for k in range(2):
                    eng.wait_ge(memT_hi, 2 * m + k + 1)
                    d = slice(4 * k, 4 * k + 4)
                    s = slice(m * P, (m + 1) * P)
                    i = eng.tensor_tensor(memT[:, 1, d, s], bank(("memT", m, k)).rearrange("p (k t) -> p k t", t=P),
                                          memT[:, 0, d, s].bitcast(F32), ALU.subtract)
                    free(i, ("memT", m, k))
            for w in range(NT):
                split_lo(w)
                eng.wait_ge(x_in[w], 16)
                layer_norm(0, w)
            for w in range(NT, mk0 + 4 + RING):
                split_lo(w)
            for t in range(NT):
                actT_lo_tile("x0T", t)
            for w in range(mv0 + RING, mv0 + 4 + RING):
                split_lo(w)

            lam = feat[:, FEAT["lam"], :]
            eng.wait_ge(small_in, 16 * 10)
            link(eng.tensor_scalar(sp[:, 5, :], lam, -1.0, None, ALU.mult))
            eng.tensor_tensor(sp[:, 0, :], sp[:, 5, :], lam, ALU.max).then_inc(sp_abs, 1)
            eng.wait_ge(sp_exp, 1)
            e1, z, z2, p = sp[:, 1, :], sp[:, 2, :], sp[:, 3, :], sp[:, 4, :]
            link(eng.tensor_scalar(z, e1, 2.0, None, ALU.add))
            link(eng.reciprocal(z, z))
            link(eng.tensor_tensor(z, z, e1, ALU.mult))
            link(eng.tensor_tensor(z2, z, z, ALU.mult))
            link(eng.tensor_scalar(p, z2, 1.0 / 15, None, ALU.mult))
            for k in (13, 11, 9, 7, 5, 3):
                link(eng.scalar_tensor_tensor(p, p, 1.0 / k, z2, ALU.add, ALU.mult))
            link(eng.scalar_tensor_tensor(p, p, 1.0, z, ALU.add, ALU.mult))
            link(eng.tensor_scalar(sp[:, 5, :], lam, -1.0, 0.0, ALU.mult, ALU.max))
            link(eng.scalar_tensor_tensor(p, p, 2.0, sp[:, 5, :], ALU.mult, ALU.add))
            link(eng.tensor_scalar(sp[:, 6, :], p, LRU_C, None, ALU.mult))
            eng.tensor_scalar(sp[:, 7, :], p, -LRU_C, None, ALU.mult).then_inc(sp_done, 1)

            def conv(ft):
                wait_read(eng, ("in", ft))
                x, y = xl[:, ft, :], xc[:, ft, :]
                link(eng.tensor_scalar(y, x, fv("conv3", ft), fv("conv_b", ft), ALU.mult, ALU.add))
                for s in (1, 2, 3):
                    i = eng.scalar_tensor_tensor(y[:, s:], x[:, :T - s], fv(f"conv{3 - s}", ft), y[:, s:],
                                                 ALU.mult, ALU.add)
                    if s < 3:
                        link(i)
                i.then_inc(xc_done, 1)

            for n in range(o0 - in0):
                if n < 2:
                    conv(2 * n)
                    conv(2 * n + 1)
                split_lo(in0 + n + RING)

            for ft in range(FT):
                eng.wait_ge(sig_i, ft + 1)
                i = eng.tensor_tensor(xc[:, ft, :], xc[:, ft, :], bank(("gate", ft, 1)), ALU.mult)
                free(i, ("gate", ft, 1))
            eng.wait_ge(rot_in, 16)
            for n in range(5):
                dst = kpad[0][:, CHUNK:] if n == 0 else qs[:, n - 1, :]
                b = bank(("rope", n))
                wait_full(eng, ("rope", n))
                eng.tensor_tensor(b, b, rot[:, 1, :], ALU.mult)
                link(eng.tensor_tensor(dst, dst, rot[:, 0, :], ALU.mult))
                i = eng.tensor_tensor(dst, dst, b, ALU.add)
                free(i, ("rope", n))
                if n == 0:
                    wait_read(eng, ("rope", 0))
                    eng.wait_ge(pad_zero, 3)
                    eng.tensor_copy(kpad[1][0:64, CHUNK:], kpad[0][64:128, CHUNK:])
                    eng.tensor_copy(kpad[1][64:128, CHUNK:], kpad[0][0:64, CHUNK:]).then_inc(kswap, 1)

            eng.wait_ge(sink_in, 16)

            def soft_max(t):
                b = t % 2
                for par in range(2):
                    g = ("S", t, par)
                    wait_full(eng, g)
                    s = bank(g).rearrange("p (h k) -> p h k", k=P)
                    if t == 0:
                        link(eng.tensor_tensor(s, s, mask0.unsqueeze(1).to_broadcast([P, 4, P]), ALU.add))
                    i = eng.tensor_reduce(mx[:, b, par::2], s, AX, ALU.max)
                link(i)
                link(eng.scalar_tensor_tensor(mx[:, b, :], mx[:, b, :], HD ** -0.5, sink[:, :], ALU.mult, ALU.max))
                eng.tensor_scalar(nmx[:, b, :], mx[:, b, :], -1.0, None, ALU.mult)
                eng.tensor_tensor(esk[:, b, :], sink[:, :], mx[:, b, :], ALU.subtract).then_inc(row_max, 1)

            def soft_norm(t):
                b = t % 2
                eng.wait_ge(exp_done, t + 1)
                link(eng.tensor_tensor(rden[:, b, :], psm[:, b, :], esk[:, b, :], ALU.add))
                link(eng.reciprocal(rden[:, b, :], rden[:, b, :]))
                eng.tensor_tensor(prob[:, b], prob[:, b], rden[:, b, :].unsqueeze(2).to_broadcast([P, HEADS, P]),
                                  ALU.mult).then_inc(prob_done, 1)

            def att_out(t):
                g = ("O", t)
                wait_full(eng, g)
                eng.tensor_tensor(qs[:, :, t * P:(t + 1) * P], bank(g).rearrange("p (f t) -> p f t", t=P),
                                  feat[:, FEAT["g_att"], :].unsqueeze(2).to_broadcast([P, FT, P]), ALU.mult
                                  ).then_inc(att_y, 1)

            def att_lo_t(t):
                s = slice(t * P, (t + 1) * P)
                eng.wait_ge(att_hi, t + 1)
                eng.tensor_tensor(actT[:, 1, 0:4, s], qs[:, :, s], actT[:, 0, 0:4, s].bitcast(F32),
                                  ALU.subtract).then_inc(att_lo, 1)

            def lru(ft):
                eng.wait_ge(decay, 2 * ft + 2)
                a, h, y = ra[:, ft, :], th[:, ft, :], xl[:, ft, :]
                link(eng.tensor_tensor(y, a, a, ALU.mult))
                link(eng.scalar_tensor_tensor(h, y, 1.0, h, ALU.add, ALU.mult))
                eng.tensor_scalar(h, h, 0.0, None, ALU.max).then_inc(gain_sq, 1)

            def lru_scan(ft):
                a, h, y = ra[:, ft, :], th[:, ft, :], xl[:, ft, :]
                eng.wait_ge(gain, ft + 1)
                link(eng.tensor_tensor(h, h, xc[:, ft, :], ALU.mult))
                link(eng.tensor_tensor_scan(y, a, h, 0.0, ALU.mult, ALU.add))
                eng.tensor_tensor(y, y, gel[:, ft, :], ALU.mult).then_inc(lru_y, 1)

            def lru_lo_t(ft):
                eng.wait_ge(lru_hi, ft + 1)
                eng.scalar_tensor_tensor(actT[:, 1, FT + ft, :], xl[:, ft, :], fv("g_lru", ft),
                                         actT[:, 0, FT + ft, :].bitcast(F32), ALU.mult, ALU.subtract
                                         ).then_inc(lru_lo, 1)

            soft_max(0)
            soft_norm(0)
            soft_max(1)
            for ft in range(FT):
                lru(ft)
            soft_norm(1)
            for t in range(NT):
                if t + 2 < NT:
                    soft_max(t + 2)
                att_out(t)
                lru_scan(t)
                if t + 2 < NT:
                    soft_norm(t + 2)
                att_lo_t(t)
                lru_lo_t(t)

            for b in range(2):
                g = ("sq", b)
                wait_full(eng, g)
                free(eng.tensor_scalar(rms[:, b, :], bank(g)[:, 0:NT], 1.0 / D_ATT, EPS, ALU.mult, ALU.add), g)
            wait_read(eng, ("sq", 0), ("sq", 1))
            eng.reciprocal(rms[:, :, :], rms[:, :, :]).then_inc(ms_ready, 1)
            eng.wait_ge(rms_ready, 1)
            eng.wait_ge(scaled, NT)
            for h in range(2):
                for t in range(NT):
                    x = xres[:, t, h * 512:(h + 1) * 512]
                    for b in range(2):
                        g = ("out", h, t, b)
                        wait_full(eng, g)
                        i = eng.scalar_tensor_tensor(x, bank(g), rms[:, b, t:t + 1], x, ALU.mult, ALU.add)
                        free(i, g)
                        wait_read(eng, g)
                    if h == 1:
                        layer_norm(1, t)
                        if t >= 2:
                            actT_lo_tile("x1T", t - 2)
                if h == 0:
                    split_lo(o0 + 3)
                    split_lo(o0 + 4)
            split_lo(o0 + 5)
            actT_lo_tile("x1T", 2)
            split_lo(o0 + 6)
            actT_lo_tile("x1T", 3)

            def m_maxes(h):
                b = h % 2
                for n in range(2):
                    g = ("mS", h, n)
                    wait_full(eng, g)
                    i = eng.tensor_reduce(mx[:, b, 2 * n:2 * n + 2], bank(g).rearrange("p (t m) -> p t m", m=MEM),
                                          AX, ALU.max)
                link(i)
                eng.tensor_scalar(nmx[:, b, 0:NT], mx[:, b, 0:NT], -(MHD ** -0.5), None, ALU.mult
                                  ).then_inc(m_max, 1)

            def m_norm(h):
                b = h % 2
                wait_read(eng, ("mS", h, 0), ("mS", h, 1))
                link(eng.reciprocal(rden[:, b, 0:NT], psm[:, b, 0:NT]))
                eng.tensor_tensor(mprob[:, b], mprob[:, b], rden[:, b, 0:NT].unsqueeze(2).to_broadcast([P, NT, MEM]),
                                  ALU.mult).then_inc(m_prob, 1)

            def m_out_lo(h):
                for n in range(2):
                    eng.wait_ge(mo_hi, 2 * h + n + 1)
                    i = eng.tensor_tensor(actT[:, 1, 2 * h + n, :], bank(("mO", h, n)),
                                          actT[:, 0, 2 * h + n, :].bitcast(F32), ALU.subtract)
                    free(i, ("mO", h, n))

            for h in range(MH + 2):
                if h < MH and q0 + h + 3 < len(pieces):
                    split_lo(q0 + h + 3)
                if 1 <= h <= MH:
                    m_maxes(h - 1)
                    m_norm(h - 1)
                if h >= 4:
                    m_out_lo(h - 4)
            m_out_lo(2)
            m_out_lo(3)
            split_lo(len(pieces) - 1)
            eng.wait_ge(w_lo, 2 * len(pieces))
            eng.tensor_copy(tri_h, tri)
            eng.tensor_copy(ones_h, ones)

            eng.wait_ge(scaled, 2 * NT)
            for h in range(2):
                for t in range(NT):
                    x = xres[:, t, h * 512:(h + 1) * 512]
                    g = ("wo", h, t)
                    wait_full(eng, g)
                    i = eng.tensor_tensor(x, bank(g), x, ALU.add)
                    free(i, g)
                    wait_read(eng, g)
                    if h == 1:
                        layer_norm(2, t)

            def moe_split_lo(i, e=0):
                eng.wait_ge(moe_hi[i], e + 1)
                eng.tensor_tensor(moe_w(i, 1), moe_landed(i), moe_w(i, 0).bitcast(F32), ALU.subtract
                                  ).then_inc(moe_lo[i], 1)

            moe_split_lo(0)

            lg = rtmp(NT, NG + NE)
            eng.wait_ge(router_in, 16 * (3 + NG))
            g = ("logits",)
            wait_full(eng, g)
            i = eng.tensor_tensor(lg, bank(g)[:, 0:NT * (NG + NE)].rearrange("p (t e) -> p t e", t=NT),
                                  b_rt[:, :].unsqueeze(1).to_broadcast([P, NT, NG + NE]), ALU.add)
            free(i, g)
            wait_read(eng, g)
            wgt = cst[:, C_WG:C_WG + EPG].unsqueeze(1).to_broadcast([P, NT, EPG])
            tmp4 = rtmp(NT, 4)
            m1 = rtmp(NT)

            def first_hot(dst, v, m):
                link(eng.tensor_tensor(tmp4, v, m.unsqueeze(2).to_broadcast([P, NT, 4]), ALU.is_equal))
                link(eng.tensor_tensor(tmp4, tmp4, wgt, ALU.mult))
                link(eng.tensor_reduce(m1, tmp4, AX, ALU.max))
                link(eng.tensor_tensor(dst, tmp4, m1.unsqueeze(2).to_broadcast([P, NT, 4]), ALU.is_equal))

            gl = lg[:, :, 0:NG]
            gm, gh = rtmp(NT), rtmp(NT, NG)
            gx = rtmp(NT, NG)
            link(eng.tensor_reduce(gm, gl, AX, ALU.max))
            first_hot(gh, gl, gm)
            link(eng.tensor_tensor(gx, gl, gm.unsqueeze(2).to_broadcast([P, NT, NG]), ALU.subtract))
            pick = rtmp(NT, NG, EPG)
            link(eng.tensor_tensor(pick, lg[:, :, NG:].rearrange("p t (g e) -> p t g e", g=NG),
                                   gh.unsqueeze(3).to_broadcast([P, NT, NG, EPG]), ALU.mult))
            el = rtmp(NT, EPG)
            link(eng.tensor_reduce(el, pick.rearrange("p t g e -> p t e g"), AX, ALU.add))
            em1, em2, eh1, eh2, el2 = rtmp(NT), rtmp(NT), rtmp(NT, EPG), rtmp(NT, EPG), rtmp(NT, EPG)
            link(eng.tensor_reduce(em1, el, AX, ALU.max))
            first_hot(eh1, el, em1)
            link(eng.scalar_tensor_tensor(el2, eh1, 2 * NEG, el, ALU.mult, ALU.add))
            link(eng.tensor_reduce(em2, el2, AX, ALU.max))
            first_hot(eh2, el2, em2)
            eng.tensor_tensor(below[:, :, 0], em2, em1, ALU.subtract)
            link(eng.tensor_copy(below[:, :, 1:], gx))
            for k, eh in enumerate((eh1, eh2)):
                m = moh[:, k].rearrange("p t (g e) -> p t g e", g=NG)
                i = eng.tensor_tensor(m, eh.unsqueeze(2).to_broadcast([P, NT, NG, EPG]),
                                      gh.unsqueeze(3).to_broadcast([P, NT, NG, EPG]), ALU.mult)
            link(i)
            eng.tensor_tensor(moh_h, moh[:, 0], moh[:, 1], ALU.add).then_inc(onehots, 1)

            g = ("rank",)
            wait_full(eng, g)
            rk_all = rtmp(NT + 1, NE)
            i = eng.tensor_copy(rk_all, bank(g)[:, 0:(NT + 1) * NE].rearrange("p (t e) -> p t e", e=NE))
            free(i, g)
            wait_read(eng, g)
            cnt = rk_all[:, NT, :]
            xe, xs, end, start = rtmp(NE), rtmp(NE), rtmp(NE), rtmp(NE)
            big = rtmp(3, NE)
            thr = cst[:, C_THR:C_THR + 3]
            experts = cst[:, C_EXP:C_EXP + NE]
            link(eng.tensor_tensor(big, cnt.unsqueeze(1).to_broadcast([P, 3, NE]),
                                   thr.unsqueeze(2).to_broadcast([P, 3, NE]), ALU.is_gt))
            link(eng.tensor_reduce(xe, big.rearrange("p j e -> p e j"), AX, ALU.add))
            one_row = cst[:, C_ONES:C_ONES + NE]
            link(eng.tensor_tensor_scan(xs, one_row, xe, 0.0, ALU.mult, ALU.add))
            link(eng.tensor_tensor(end, xs, experts, ALU.add))
            link(eng.tensor_tensor(start, end, xe, ALU.subtract))
            prod = rtmp(2, TOPK * NT, NE)
            vals = rtmp(2, TOPK * NT)
            for v, src in enumerate((rk_all[:, 0:NT, :], start.unsqueeze(1).to_broadcast([P, NT, NE]))):
                for k in range(TOPK):
                    i = eng.tensor_tensor(prod[:, v, k * NT:(k + 1) * NT, :], moh[:, k], src, ALU.mult)
            link(i)
            link(eng.tensor_reduce(vals, prod, AX, ALU.add))
            rank, first = vals[:, 0, :], vals[:, 1, :]
            over = rtmp(TOPK * NT, 3)
            jv, cv, row = rtmp(TOPK * NT), rtmp(TOPK * NT), rtmp(TOPK * NT)
            link(eng.tensor_tensor(over, rank.unsqueeze(2).to_broadcast([P, TOPK * NT, 3]),
                                   thr.unsqueeze(1).to_broadcast([P, TOPK * NT, 3]), ALU.is_ge))
            link(eng.tensor_reduce(jv, over, AX, ALU.add))
            eng.scalar_tensor_tensor(row, jv, -float(P), rank, ALU.mult, ALU.add)
            link(eng.tensor_tensor(cv, first, jv, ALU.add))
            iota_r = cst[:, C_ROW:C_ROW + P]
            iota_c = cst[:, C_CHK:C_CHK + CMAX]
            in_c = rtmp(TOPK * NT, CMAX)
            J = TOPK * NT
            eng.tensor_tensor(in_c, iota_c.unsqueeze(1).to_broadcast([P, J, CMAX]),
                              cv.unsqueeze(2).to_broadcast([P, J, CMAX]), ALU.is_equal)
            link(eng.tensor_tensor(selT, iota_r.unsqueeze(1).to_broadcast([P, J, P]),
                                   row.unsqueeze(2).to_broadcast([P, J, P]), ALU.is_equal))
            token = cst[:, C_TOK:C_TOK + NT]
            for k in range(TOPK):
                i = eng.tensor_tensor(sel_c[:, k * NT:(k + 1) * NT, :], in_c[:, k * NT:(k + 1) * NT, :],
                                      token.unsqueeze(2).to_broadcast([P, NT, CMAX]), ALU.mult)
            i.then_inc(selected, 1)
            endb = kvm[:, 3, 0:CMAX * NE].rearrange("p (c e) -> p c e", e=NE)
            ctf = rtmp(TAB_W)
            ef = ctf[:, T_EXP:T_EXP + CMAX]
            link(eng.tensor_tensor(endb, end.unsqueeze(1).to_broadcast([P, CMAX, NE]),
                                   iota_c.unsqueeze(2).to_broadcast([P, CMAX, NE]), ALU.is_lt))
            link(eng.tensor_reduce(ef, endb, AX, ALU.add))
            link(eng.tensor_scalar(ef, ef, float(NE - 1), None, ALU.min))
            eng.tensor_tensor(ctf[:, T_NEW + 1:T_NEW + CMAX], ef[:, 1:], ef[:, :CMAX - 1], ALU.is_gt)
            eng.tensor_scalar(ctf[:, T_NEW:T_NEW + 1], xs[:, 0:1], 0.0, 1.0, ALU.mult, ALU.add)
            eng.tensor_scalar(ctf[:, T_N:T_N + 1], xs[:, NE - 1:NE], float(NE), None, ALU.add)
            eng.tensor_scalar(ctf[:, T_LAST:T_LAST + 1], xs[:, NE - 1:NE], float(NE - 1), None, ALU.add)
            link(eng.tensor_scalar(ctf[:, T_PREV:T_PREV + 1], xs[:, NE - 1:NE], float(NE - 2), None, ALU.add))
            eng.tensor_copy(ctab[0:1, :], ctf[0:1, :]).then_inc(table_done, 1)
            g = ("table",)
            wait_full(eng, g)
            i = eng.tensor_copy(tokidx[:, :], bank(g)[:, 0:CMAX])
            free(i, g)
            for i in range(1, 4):
                moe_split_lo(i)
            slot_f = rtmp(TOPK * NT)
            link(eng.scalar_tensor_tensor(slot_f, cv, float(P), row, ALU.mult, ALU.add))
            eng.tensor_copy(slot_i[:, :, :], slot_f.rearrange("p (k t) -> p t k", k=TOPK)).then_inc(slot_done, 1)
            def evac_x(c):
                eng.wait_ge(xgT_hi_done, c + 1)
                eng.tensor_tensor(xgT_lo, psum[:, 0:2, :].rearrange("p a b -> p (a b)"), xgT_hi.bitcast(F32),
                                  ALU.subtract).then_inc(xgT_ready, 1)

            def h_mul(c):
                eng.wait_ge(silu_done, c + 1)
                eng.tensor_tensor(h_act, silu_g, psum[:, 3, :], ALU.mult).then_inc(h_ready, 1)

            def evac_h(c):
                eng.wait_ge(hT_hi_done, c + 1)
                eng.tensor_tensor(hT_lo, psum[:, 4, :], hT_hi.bitcast(F32), ALU.subtract).then_inc(hT_ready, 1)

            evac_x(0)
            moe_split_lo(4)
            moe_split_lo(5)
            eng.wait_ge(onehots, 2)
            den, dg = rtmp(NT), rtmp(NT)
            link(eng.tensor_reduce(dg, below_exp[:, :, 1:], AX, ALU.add))
            link(eng.scalar_tensor_tensor(den, below_exp[:, :, 0], 1.0, dg, ALU.add, ALU.mult))
            link(eng.reciprocal(gates[:, :, 0], den))
            link(eng.tensor_tensor(gates[:, :, 1], gates[:, :, 0], below_exp[:, :, 0], ALU.mult))
            n = table(eng, T_N, NE, CMAX)

            def new_lo(c, i):
                new = is_new(eng, c)
                with eng.If(new > 0):
                    e = expert_of(eng, c)
                    moe_split_lo(i, e)
                    moe_split_lo(i + 1, e)

            def dve_chunk(c, first=False):
                new_lo(c, 0)
                h_mul(c - 1)
                evac_x(c)
                new_lo(c, 2)
                evac_h(c - 1)
                if not first:
                    new_lo(c - 1, 4)

            dve_chunk(1, True)
            with eng.Fori(2, CMAX) as c:
                with eng.If(c < n):
                    dve_chunk(c)
            last = table(eng, T_LAST, NE - 1, CMAX - 1)
            h_mul(last)
            evac_h(last)
            new_lo(last, 4)

            eng.wait_ge(scaled, 3 * NT)
            for t in range(NT):
                for k in range(TOPK):
                    eng.wait_ge(back_in[t * TOPK + k], 16)
                    link(eng.scalar_tensor_tensor(xres[:, t, :], back[:, t * TOPK + k, :], gates[:, t, k:k + 1],
                                                  xres[:, t, :], ALU.mult, ALU.add))
                layer_norm(3, t)

        @block.tensor
        def _(eng):
            def mm3(out, s, m, first, last):
                eng.matmul(out, s[0], m[0], start=first, stop=False)
                eng.matmul(out, s[0], m[1], start=False, stop=False)
                return eng.matmul(out, s[1], m[0], start=False, stop=last)

            def wpiece(w, width):
                return [wring[:, w % RING, i, :].rearrange("p (k n) -> p k n", n=width) for i in range(2)]

            def transposes(g, srcs, width=P):
                wait_free(eng, g)
                for j, s in enumerate(srcs):
                    i = eng.transpose(bank(g)[:, j * width:(j + 1) * width], s, ident)
                full(i, g)

            def rows_T(group, t):
                for k in range(2):
                    transposes((group, t, k), [xres[:, t, (4 * k + j) * P:(4 * k + j + 1) * P] for j in range(4)])

            eng.wait_ge(mem_in, 16)
            eng.wait_ge(const_in, 16)
            for m in range(MT):
                for k in range(2):
                    transposes(("memT", m, k), [memr[:, m, (4 * k + j) * P:(4 * k + j + 1) * P] for j in range(4)])
            wait_read(eng, *[("memT", m, k) for m in range(MT) for k in range(2)])
            for n in range(KT):
                w = mk0 + n // 2
                c0 = (n % 2) * P
                eng.wait_ge(w_lo, 2 * w + 2)
                wait_free(eng, ("mk", n))
                wp = wpiece(w, 256)
                for k in range(KT):
                    i = mm3(bank(("mk", n))[:, 0:MEM], [q[:, k, c0:c0 + P] for q in wp],
                            [memT[:, j, k, :] for j in range(2)], k == 0, k == KT - 1)
                full(i, ("mk", n))
            for t in range(NT):
                eng.wait_ge(ln_done, t + 1)
                rows_T("x0T", t)
            for q in range(4):
                w = mv0 + q
                eng.wait_ge(w_lo, 2 * w + 2)
                wp = wpiece(w, 256)
                for m in range(MT):
                    wait_free(eng, ("mv", q, m))
                    for k in range(KT):
                        i = mm3(bank(("mv", q, m))[:, 0:256], [memT[:, j, k, m * P:(m + 1) * P] for j in range(2)],
                                [x[:, k, :] for x in wp], k == 0, k == KT - 1)
                    full(i, ("mv", q, m))

            wait_read(eng, *[("x0T", t, k) for t in range(NT) for k in range(2)])
            for n in range(D_IN // P):
                w, c0 = in_slices(n)
                eng.wait_ge(w_lo, 2 * w + 2)
                wait_free(eng, ("in", n))
                wp = wpiece(w, 256)
                for k in range(KT):
                    i = mm3(bank(("in", n)), [q[:, k, c0:c0 + P] for q in wp],
                            [actT[:, j, k, :] for j in range(2)], k == 0, k == KT - 1)
                full(i, ("in", n))
            eng.wait_ge(bd_in, 64)
            for ft in range(FT):
                eng.wait_ge(xc_done, ft + 1)
                for w in range(2):
                    g = ("gate", ft, w)
                    wait_free(eng, g)
                    full(eng.matmul(bank(g), gate_bd[:, w, ft, :], xc[:, ft, :], start=True, stop=True), g)
            for n in range(5):
                wait_read(eng, ("in", 8 if n == 0 else 9 + n))
                wait_free(eng, ("rope", n))
                src = kpad[0][:, CHUNK:] if n == 0 else qs[:, n - 1, :]
                full(eng.matmul(bank(("rope", n)), perm, src, start=True, stop=True), ("rope", n))
            eng.wait_ge(pad_zero, 3)
            wait_read(eng, ("in", 9))
            for b in range(2):
                transposes(("vwin", b), [vpad[:, c * CHUNK:c * CHUNK + P] for c in range(4 * b, 4 * b + 4)])

            def scores(t):
                for par in range(2):
                    g = ("S", t, par)
                    wait_free(eng, g)
                    ps = slice(par * 64, par * 64 + 64)
                    for hp in range(4):
                        kk = kpad[0 if hp // 2 == par else 1]
                        for c in range(2):
                            ch = 2 * t + c
                            i = eng.matmul(psum[c * 64:c * 64 + 64, G[g] % 8, hp * P:(hp + 1) * P],
                                           qs[ps, hp, ch * CHUNK:(ch + 1) * CHUNK],
                                           kk[ps, ch * CHUNK:ch * CHUNK + P], start=True, stop=True)
                    full(i, g)

            def prob_T(t):
                eng.wait_ge(prob_done, t + 1)
                for k in range(2):
                    transposes(("PT", t, k), [prob[:, t % 2, 4 * k + j, :] for j in range(4)])

            def att_out(t):
                g = ("O", t)
                wait_read(eng, ("PT", t, 0), ("PT", t, 1), ("vwin", 0), ("vwin", 1))
                wait_free(eng, g)
                for c in range(2):
                    for kv in range(2):
                        for par in range(2):
                            dst = psum[par * 64:par * 64 + 64, G[g] % 8, :].rearrange("p (f t) -> p f t", t=P)
                            i = eng.matmul(dst[:, 2 * kv:2 * kv + 2, c * 64:c * 64 + 64],
                                           vwin[:, 2 * t + c, kv * 64:kv * 64 + 64],
                                           probT[:, 4 * kv + par:4 * kv + par + 3:2, c * 64:c * 64 + 64],
                                           start=True, stop=True)
                full(i, g)

            wait_read(eng, *[("rope", n) for n in range(5)])
            eng.wait_ge(kswap, 1)
            scores(0)
            scores(1)
            for t in range(NT):
                prob_T(t)
                att_out(t)
                if t + 2 < NT:
                    scores(t + 2)

            wait_read(eng, *[("O", t) for t in range(NT)])
            eng.wait_ge(lru_sq, FT)
            for b in range(2):
                g = ("sq", b)
                wait_free(eng, g)
                for t in range(NT):
                    for f in range(FT):
                        src = qs[:, f, t * P:(t + 1) * P] if b == 0 else ra[:, f, t * P:(t + 1) * P]
                        i = eng.matmul(bank(g)[:, t:t + 1], src, ones[:, 0:1], start=f == 0, stop=f == FT - 1)
                full(i, g)

            def norm_T(n, t):
                eng.wait_ge(ln_done, n * NT + t + 1)
                rows_T(f"x{n}T", t)

            eng.wait_ge(att_lo, NT)
            eng.wait_ge(lru_lo, FT)
            w0 = o0
            for h in range(2):
                for t in range(NT):
                    for b in range(2):
                        w = w0 + 2 * h + b
                        eng.wait_ge(w_lo, 2 * w + 2)
                        g = ("out", h, t, b)
                        wait_free(eng, g)
                        wp = wpiece(w, 512)
                        for k in range(4):
                            i = mm3(bank(g), [actT[:, j, 4 * b + k, t * P:(t + 1) * P] for j in range(2)],
                                    [x[:, k, :] for x in wp], k == 0, k == 3)
                        full(i, g)
                    if h == 1 and t >= 2:
                        norm_T(1, t - 2)
            norm_T(1, 2)
            norm_T(1, 3)

            def m_query(h):
                w = q0 + h
                eng.wait_ge(w_lo, 2 * w + 2)
                wp = wpiece(w, 256)
                for n in range(2):
                    wait_free(eng, ("mq", h, n))
                    for k in range(KT):
                        i = mm3(bank(("mq", h, n)), [x[:, k, n * P:(n + 1) * P] for x in wp],
                                [actT[:, j, k, :] for j in range(2)], k == 0, k == KT - 1)
                    full(i, ("mq", h, n))

            def m_scores(h):
                wait_read(eng, ("mq", h, 0), ("mq", h, 1))
                for n in range(2):
                    g = ("mS", h, n)
                    wait_free(eng, g)
                    for u in range(2):
                        t = 2 * n + u
                        for k in range(2):
                            i = eng.matmul(bank(g)[:, u * MEM:(u + 1) * MEM],
                                           mq[:, 2 * h + k, t * P:(t + 1) * P], mkT[:, 2 * h + k, :],
                                           start=k == 0, stop=k == 1)
                    full(i, g)

            def m_prob_T(h):
                eng.wait_ge(m_prob, h + 1)
                for m in range(MT):
                    transposes(("mPT", h, m), [mprob[:, h % 2, t, m * P:(m + 1) * P] for t in range(NT)])

            def m_out(h):
                wait_read(eng, ("mPT", h, 0), ("mPT", h, 1))
                for n in range(2):
                    g = ("mO", h, n)
                    wait_free(eng, g)
                    for m in range(MT):
                        i = eng.matmul(bank(g), mvv[:, m, (2 * h + n) * P:(2 * h + n + 1) * P],
                                       mpT[:, h % 2, m, :], start=m == 0, stop=m == 1)
                    full(i, g)

            wait_read(eng, *[("x1T", t, k) for t in range(NT) for k in range(2)])
            wait_read(eng, *[("mk", n) for n in range(KT)])
            wait_read(eng, *[("mv", q, m) for q in range(4) for m in range(MT)])
            for h in range(MH + 2):
                if h < MH:
                    m_query(h)
                if 2 <= h:
                    m_prob_T(h - 2)
                if 1 <= h <= MH:
                    m_scores(h - 1)
                if h >= 4:
                    m_out(h - 4)
            m_out(2)
            m_out(3)

            wait_read(eng, *[("mO", h, n) for h in range(MH) for n in range(2)])
            w0 = wo0
            for h in range(2):
                for t in range(NT):
                    g = ("wo", h, t)
                    wait_free(eng, g)
                    for b in range(2):
                        w = w0 + 2 * h + b
                        eng.wait_ge(w_lo, 2 * w + 2)
                        wp = wpiece(w, 512)
                        for k in range(4):
                            i = mm3(bank(g), [actT[:, j, 4 * b + k, t * P:(t + 1) * P] for j in range(2)],
                                    [x[:, k, :] for x in wp], b + k == 0, b == 1 and k == 3)
                    full(i, g)
                    if h == 1 and t >= 2:
                        norm_T(2, t - 2)

            W = NG + NE

            def logits(t):
                g = ("logits",)
                wait_read(eng, ("x2T", t, 0), ("x2T", t, 1))
                if t == 0:
                    eng.wait_ge(router_in, 16 * (3 + NG))
                    wait_free(eng, g)
                for k in range(KT):
                    i = eng.matmul(bank(g)[:, t * W:(t + 1) * W], x2T[:, k, t * P:(t + 1) * P], w_rt[:, k, :],
                                   start=k == 0, stop=k == KT - 1)
                if t == NT - 1:
                    full(i, g)

            logits(0)
            norm_T(2, 2)
            logits(1)
            norm_T(2, 3)
            logits(2)
            logits(3)
            g = ("rank",)
            eng.wait_ge(onehots, 1)
            wait_free(eng, g)
            for t in range(NT + 1):
                dst = bank(g)[:, t * NE:(t + 1) * NE]
                for s in range(min(t + 1, NT)):
                    i = eng.matmul(dst, tri_h if s == t else ones_h, moh_h[:, s, :], start=s == 0,
                                   stop=s == min(t, NT - 1))
            full(i, g)
            g = ("table",)
            eng.wait_ge(selected, 1)
            wait_free(eng, g)
            for j in range(TOPK * NT):
                i = eng.matmul(bank(g)[:, 0:CMAX], selT[:, j, :], sel_c[:, j, :], start=j == 0,
                               stop=j == TOPK * NT - 1)
            full(i, g)

            def x_T(c):
                eng.wait_ge(gathered, 16 * c + 16)
                for k in range(KT):
                    i = eng.transpose(psum[:, k // 4, (k % 4) * P:(k % 4 + 1) * P], xg[:, k * P:(k + 1) * P], ident)
                i.then_inc(xtrans_done, 1)

            def gate_up(c):
                e = expert_of(eng, c)
                eng.wait_ge(xgT_ready, c + 1)
                for k in range(KT):
                    if k % 4 == 0:
                        for i in (k // 2, k // 2 + 1):
                            eng.wait_ge(moe_lo[i], e + 1)
                    s = slice((k % 4) * F, (k % 4 + 1) * F)
                    cols = slice(k * P, (k + 1) * P)
                    first, final = k == 0, k == KT - 1
                    for b in range(2):
                        for part in range(2):
                            eng.matmul(psum[:, 2 + b, :], xgT_hi[:, cols], moe_w(k // 4 * 2 + b, part)[:, s],
                                       start=first and part == 0, stop=False)
                    for b in range(2):
                        i = eng.matmul(psum[:, 2 + b, :], xgT_lo[:, cols], moe_w(k // 4 * 2 + b, 0)[:, s],
                                       start=False, stop=final)
                    if k == 3:
                        i.then_inc(gu_half, 1)
                i.then_inc(gateup_done, 1)

            def h_T(c):
                eng.wait_ge(h_ready, c + 1)
                for f in range(FFT):
                    i = eng.transpose(psum[:, 4, f * P:(f + 1) * P], h_act[:, f * P:(f + 1) * P], ident)
                i.then_inc(htrans_done, 1)

            def down(c):
                e = expert_of(eng, c)
                eng.wait_ge(hT_ready, c + 1)
                if not isinstance(c, int):
                    eng.wait_ge(o_read, c)
                for f in range(FFT):
                    if f % 2 == 0:
                        eng.wait_ge(moe_lo[4 + f // 2], e + 1)
                    cols = slice(f * P, (f + 1) * P)
                    first, final = f == 0, f == FFT - 1
                    for hf in range(2):
                        s = slice((f % 2) * D + hf * 512, (f % 2) * D + hf * 512 + 512)
                        for part in range(2):
                            eng.matmul(psum[:, 5 + hf, :], hT_hi[:, cols], moe_w(4 + f // 2, part)[:, s],
                                       start=first and part == 0, stop=False)
                    for hf in range(2):
                        s = slice((f % 2) * D + hf * 512, (f % 2) * D + hf * 512 + 512)
                        i = eng.matmul(psum[:, 5 + hf, :], hT_lo[:, cols], moe_w(4 + f // 2, 0)[:, s],
                                       start=False, stop=final)
                i.then_inc(down_done, 1)

            for b in range(8):
                last = max(v for v in G.values() if v % 8 == b)
                eng.wait_ge(psum_read[b], last // 8 + 1)
            x_T(0)
            eng.wait_ge(table_done, 1)
            gate_up(0)
            x_T(1)
            h_T(0)
            gate_up(1)
            n = table(eng, T_N, NE, CMAX)
            with eng.Fori(2, CMAX) as c:
                with eng.If(c < n):
                    x_T(c)
                    down(c - 2)
                    h_T(c - 1)
                    gate_up(c)
            last = table(eng, T_LAST, NE - 1, CMAX - 1)
            down(table(eng, T_PREV, NE - 2, CMAX - 2))
            h_T(last)
            down(last)


_INS = ['x', 'mem', 'ln_in_g', 'ln_in_b', 'w_in', 'attn_sink', 'conv_w', 'conv_b', 'w_rgate', 'b_rgate',
        'w_igate', 'b_igate', 'lru_lambda', 'norm_attn_g', 'norm_lru_g', 'w_out', 'ln1_g', 'ln1_b', 'wq_mem',
        'wk_mem', 'wv_mem', 'wo_mem', 'ln2_g', 'ln2_b', 'w_router_group', 'b_router_group', 'w_router_expert',
        'b_router_expert', 'w_gate_e', 'w_up_e', 'w_down_e', 'ln3_g', 'ln3_b']


def kernel(**inputs):
    import concourse.bacc as bacc
    from concourse.bass_utils import run_bass_kernel_spmd

    nc = bacc.Bacc("TRN2", target_bir_lowering=False, num_devices=1)
    arrays, args = {}, {}
    for name in _INS:
        a = np.ascontiguousarray(inputs[name])
        arrays[f"in_{name}"] = a
        args[name] = nc.dram_tensor(f"in_{name}", a.shape, mybir.dt.from_np(a.dtype), kind="ExternalInput").ap()
    cst, rot = constants()
    aps = []
    for name, a in (("consts", cst), ("rots", rot)):
        arrays[name] = a
        aps.append(nc.dram_tensor(name, a.shape, F32, kind="ExternalInput").ap())
    y = nc.dram_tensor("y_out", (1, T, D), F32, kind="ExternalOutput").ap()
    encoder_layer(nc, args, aps[0], aps[1], y)
    r = run_bass_kernel_spmd(nc, [arrays], core_ids=[0])
    return r.results[0]["y_out"]
```

```python
from contextlib import ExitStack

import numpy as np

import concourse.bass as bass
from concourse import mybir

F32 = mybir.dt.float32
F32R = mybir.dt.float32r
F16 = mybir.dt.float16
I32 = mybir.dt.int32
U32 = mybir.dt.uint32
ALU = mybir.AluOpType
ACT = mybir.ActivationFunctionType
AX = mybir.AxisListType.X

P = 128
D = 1024
T = 512
NT = T // P
KT = D // P
CHUNK = 64
HD = 64
HEADS = 8
KVH = 2
D_ATT = HEADS * HD
D_KV = KVH * HD
D_LRU = 512
FT = D_LRU // P
TAPS = 4
LRU_C = 8.0
D_IN = D_ATT + 2 * D_KV + 2 * D_LRU
MEM = 256
MT = MEM // P
MH = 4
MHD = D // MH
NG = 4
EPG = 4
NE = NG * EPG
TOPK = 2
F = 512
FFT = F // P
ALPHA = 2.0 ** 0.25
EPS = 1e-5
NEG = -1e30
EXTRA = (TOPK * T - 1) // P
CMAX = NE + EXTRA
T_N, T_LAST, T_PREV, T_EXP = 0, 1, 2, 3
T_NEW = T_EXP + CMAX
TAB_W = T_NEW + CMAX

C_ID, C_TRI, C_ONES, C_PERM, C_MASK, C_ROW = (P * i for i in range(6))
C_CHK = 6 * P
C_EXP = C_CHK + CMAX
C_THR = C_EXP + NE
C_WG = C_THR + 3
C_TOK = C_WG + EPG
CONST_W = C_TOK + NT


def constants():
    c = np.zeros((P, CONST_W), np.float32)
    i = np.arange(P)
    c[:, C_ID:C_ID + P] = i[:, None] == i[None, :]
    c[:, C_TRI:C_TRI + P] = i[:, None] < i[None, :]
    c[:, C_ONES:C_ONES + P] = 1.0
    src = (i // HD) * HD + (i % HD + HD // 2) % HD
    c[:, C_PERM:C_PERM + P] = i[:, None] == src[None, :]
    c[:CHUNK, C_MASK:C_MASK + CHUNK] = NEG
    c[:, C_ROW:C_ROW + P] = i[None, :]
    c[:, C_CHK:C_CHK + CMAX] = np.arange(CMAX)[None, :]
    c[:, C_EXP:C_EXP + NE] = np.arange(NE)[None, :]
    c[:, C_THR:C_THR + 3] = P * np.arange(1, 4)[None, :]
    c[:, C_WG:C_WG + EPG] = EPG - np.arange(EPG)[None, :]
    c[:, C_TOK:C_TOK + NT] = i[:, None] + P * np.arange(NT)[None, :]
    inv = np.float32(10000.0) ** (-np.arange(0, HD, 2, dtype=np.float32) / np.float32(HD))
    ang = np.arange(T, dtype=np.float32)[None, :] * inv[i % (HD // 2)][:, None].astype(np.float32)
    sign = np.where(i % HD < HD // 2, -1.0, 1.0).astype(np.float32)[:, None]
    rot = np.stack([np.cos(ang), np.sin(ang) * sign], 1).astype(np.float32)
    return c, rot


ATTENTION = [("mv", 0), ("S", 0), ("S", 1), ("PT", 0), ("mv", 1), ("mv", 2), ("S", 2), ("O", 0), ("PT", 1),
             ("mv", 3), ("O", 1), ("S", 3), ("PT", 2), ("O", 2), ("out", 0), ("PT", 3), ("out", 1), ("O", 3),
             ("out", 2), ("sq1", 0), ("sq0", 0), ("out", 3)]
M_TAIL = [("mO", 0), ("mS", 3), ("mPT", 2), ("mO", 1), ("mO", 2), ("mPT", 3), ("mO", 3)]


def psum_groups():
    g = [("memT", m, k) for m in range(MT) for k in range(2)]
    g += [("mk", n) for n in range(KT - 2)]
    g += [("x0T", t, k) for t in range(NT) for k in range(2)]
    g += [("mk", KT - 2), ("mk", KT - 1)]
    g += [("in", n) for n in range(D_IN // P)]
    g += [("gate", ft, w) for ft in range(FT) for w in range(2)]
    g += [("rope", n) for n in range(5)] + [("vwin", 0), ("vwin", 1)]
    for name, t in ATTENTION:
        g += {"sq1": [("sq",)], "sq0": [], "out": [("out", 0, t, 0)], "O": [("O", t)]}.get(
            name, [(name, t, k) for k in range(2)])
    g += [("out", 0, t, 1) for t in range(NT)]
    for t in range(NT):
        g += [("out", 1, t, 0), ("out", 1, t, 1)]
        if t >= 2:
            g += [("x1T", t - 2, 0), ("x1T", t - 2, 1)]
    g += [("x1T", 2, 0), ("x1T", 2, 1), ("mq", 0, 0), ("x1T", 3, 0), ("x1T", 3, 1), ("mq", 0, 1)]
    for h in range(1, MH):
        g += [("mq", h, n) for n in range(2)]
        if h >= 2:
            g += [("mPT", h - 2, m) for m in range(MT)]
        g += [("mS", h - 1, n) for n in range(2)]
    for name, h in M_TAIL:
        g += [(name, h, n) for n in range(2)]
    g += [("wo", 0, t) for t in range(NT)]
    for t in range(NT):
        g += [("wo", 1, t)]
        if t >= 2:
            g += [("x2T", t - 2, 0), ("x2T", t - 2, 1)]
    g += [("logitsT", 0), ("x2T", 2, 0), ("x2T", 2, 1), ("logitsT", 1), ("x2T", 3, 0), ("x2T", 3, 1)]
    g += [("logitsT", 2), ("logitsT", 3)]
    g += [("logits",), ("rank",), ("table",)]
    return {name: n for n, name in enumerate(g)}


def weight_pieces(w_in, wk, wv, w_out, wq, wo):
    cols = [("mk", wk, 256 * c) for c in range(4)]
    cols += [("in", w_in, 256 * c) for c in (3, 4, 5, 6, 2, 0, 1)]
    cols += [("mv", wv, 256 * c) for c in range(4)]
    out = []
    for name, w, c0 in cols:
        if name == "mk":
            out.append((name, [w[:, c0:c0 + 256]], 256))
        else:
            out.append((name, [w[h * 512:(h + 1) * 512, c0:c0 + 256] for h in range(2)], 256))
    for name, w in (("out", w_out), ("mq", wq), ("wo", wo)):
        for q in range(4):
            if name == "mq":
                out.append((name, [w[h * 512:(h + 1) * 512, q * 256:(q + 1) * 256] for h in range(2)], 256))
            else:
                n, k = q // 2, q % 2
                out.append((name, [w[k * 512 + h * 256:k * 512 + (h + 1) * 256, n * 512:(n + 1) * 512]
                                   for h in range(2)], 512))
    return out


def encoder_layer(nc, A, consts, rots, y_out):
    G = psum_groups()
    pieces = weight_pieces(A["w_in"][0], A["wk_mem"][0], A["wv_mem"][0], A["w_out"][0],
                           A["wq_mem"][0], A["wo_mem"][0])
    first_piece = {}
    for n, (name, _, _) in enumerate(pieces):
        first_piece.setdefault(name, n)
    mk0, mv0, in0, o0, q0, wo0 = (first_piece[n] for n in ("mk", "mv", "in", "out", "mq", "wo"))
    RING = 3
    EARLY = {0: 0, 1: 1, 2: 2, 3: 3, 5: 1, 6: 2}
    EARLY_AFTER = {5: 1, 6: 2}
    STAGED = [w for w in range(len(pieces)) if w not in EARLY]

    def last_use(w):
        name = pieces[w][0]
        q = w - first_piece[name]
        return {"in": ("in", 2 * q + 1), "mk": ("mk", 2 * q + 1), "mv": ("mv", q, MT - 1), "mq": ("mq", q, 1),
                "out": ("out", q // 2, NT - 1, q % 2), "wo": ("wo", q // 2, NT - 1)}[name]

    ctx = ExitStack()
    with ctx:
        def sb(name, shape, dt=F32):
            return ctx.enter_context(nc.sbuf_tensor(name, shape, dt))

        offset = {}

        def sb_at(name, shape, dt=F32):
            offset[name] = nc.sbuf_base
            return sb(name, shape, dt)

        def alias(name, of, shape, dt):
            return nc.alloc_sbuf_tensor_at(name, shape, dt, offset=offset[of])

        def sem(name):
            return ctx.enter_context(nc.semaphore(name))

        xres = sb("xres", [P, NT, D])
        actT = sb_at("actT", [P, 2, KT, T], F32R)
        memT = sb_at("memT", [P, 2, KT, MEM], F32R)
        qs = sb_at("qs", [P, 4, T])
        wring = sb("wring", [P, RING, 2, 2048], F32R)
        stage = sb_at("stage", [P, 2, 1024])
        kvm = sb_at("kvm", [P, 4, 1024])
        scr = sb_at("scr", [P, 6, 2048])
        lngb = sb("lngb", [P, 2, D])
        cst = sb("cst", [P, CONST_W])
        w_rt = sb("w_rt", [P, KT, NG + NE])
        b_rt = sb("b_rt", [P, NG + NE])
        sink = sb("sink", [P, HEADS])
        feat = sb("feat", [P, 11, FT])
        sp = sb("sp", [P, 8, FT])
        stats = sb("stats", [P, NT, 2, 6])
        mv = sb("mv", [P, NT, 2])
        sums = sb("sums", [P, NT, 2])
        nmean = sb("nmean", [P, NT])
        ssq = sb("ssq", [P, NT])
        eps = sb("eps", [P, 1])
        rstd = sb("rstd", [P, NT])
        rms = sb("rms", [P, 2, NT])
        mx = sb("mx", [P, 2, HEADS])
        nmx = sb("nmx", [P, 2, HEADS])
        psm = sb("psm", [P, 2, HEADS])
        esk = sb("esk", [P, 2, HEADS])
        rden = sb("rden", [P, 2, HEADS])
        gates = sb("gates", [P, NT, TOPK])
        slot_i = sb("slot_i", [P, NT, TOPK], U32)
        tokidx = sb("tokidx", [P, CMAX], U32)
        idx_now = sb("idx_now", [P, 1], U32)
        ctab = sb("ctab", [1, TAB_W], I32)

        ident = cst[:, C_ID:C_ID + P]
        tri = cst[:, C_TRI:C_TRI + P]
        ones = cst[:, C_ONES:C_ONES + P]
        perm = cst[:, C_PERM:C_PERM + P]
        mask0 = cst[:, C_MASK:C_MASK + P]

        att = alias("att", "actT", [P, 2, 4096], F32)
        prob = att[:, 0, 2048:].rearrange("p (b h k) -> p b h k", b=2, h=HEADS)
        probT = att[:, 1, 2048:3072].rearrange("p (h q) -> p h q", h=HEADS)
        vwin = att[:, 1, 3072:].rearrange("p (c v) -> p c v", c=T // CHUNK)
        rot = lngb[:, 0, :].rearrange("p (a t) -> p a t", a=2)
        gate_bd = lngb[:, 1, :].rearrange("p (g f j) -> p g f j", g=2, f=FT)
        mkT = kvm[:, 0:2, :].rearrange("p a (k m) -> p (a k) m", m=MEM)
        mvv = kvm[:, 2:4, :]
        mprob = scr[:, 3, :].rearrange("p (b t m) -> p b t m", b=2, t=NT)
        mq = scr[:, 4:6, :].rearrange("p a (k t) -> p (a k) t", t=T)
        mpT = qs[:, :, :].rearrange("p (b m) t -> p b m t", b=2)
        x2T = kvm[:, :, :].rearrange("p a (k t) -> p (a k) t", t=T)
        xl, xc, gel, ra, th = (scr[:, i, :].rearrange("p (f t) -> p f t", f=FT) for i in range(5))
        KP = CHUNK + T
        kpad = [scr[:, 5, i * KP:(i + 1) * KP] for i in range(2)]
        vpad = scr[:, 5, 2 * KP:3 * KP]
        squares_out = {0: qs[:, 2:4, :].rearrange("p a b -> p (a b)"), 1: scr[:, 4, 0:D], 3: kvm[:, 3, :]}
        memr = scr[:, 4, :].rearrange("p (m d) -> p m d", m=MT)
        moe_land = alias("moe_land", "actT", [P, 4, 2048], F32)
        moe_split = alias("moe_split", "scr", [P, 3, 2, 2048], F32R)
        xg = kvm[:, 0, :]
        logT = qs[:, 3, :]
        xgT_hi = alias("kvm_r", "kvm", [P, 4, 1024], F32R)[:, 1, :]
        moe_o = kvm[:, 2, :]
        silu_g = kvm[:, 3, 0:512]
        h_act = kvm[:, 3, 512:1024]
        hT_hi = alias("qs_r", "qs", [P, 4, T], F32R)[:, 3, :]
        stage_r = alias("stage_r", "stage", [P, 2, 1024], F32R)
        xgT_lo, hT_lo = stage_r[:, 1, :], stage_r[:, 0, 0:512]
        moe_land_early = alias("moe_land_early", "memT", [P, 2, 2048], F32)

        FIRST_AT = {2: 2, 3: 2, 5: 3}

        def moe_landed(i, first=False):
            if first and i in FIRST_AT:
                return scr[:, FIRST_AT[i], :]
            return moe_land_early[:, i, :] if i < 2 else moe_land[:, i - 2, :]

        def moe_w(i, part):
            return wring[:, i, part, :] if i < 3 else moe_split[:, i - 3, part, :]

        back = scr[:, 0:4, :].rearrange("p a (b n) -> p (a b) n", n=D)

        rt = qs[:, 0:3, :].rearrange("p a b -> p (a b)")
        rt_at = [0]

        def rtmp(*shape):
            n = int(np.prod(shape))
            a = rt[:, rt_at[0]:rt_at[0] + n]
            rt_at[0] += n
            assert rt_at[0] <= 3 * T
            if len(shape) == 1:
                return a
            names = "abc"[:len(shape)]
            return a.rearrange(f"p ({' '.join(names)}) -> p {' '.join(names)}",
                               **{k: s for k, s in zip(names, shape)})

        below, below_exp = rtmp(NT, 1 + NG), rtmp(NT, 1 + NG)
        moh = rtmp(2, NT, NE)
        half = alias("half", "stage", [P, 4096], F16)
        selT = half[:, 0:1024].rearrange("p (j r) -> p j r", r=P)
        sel_c = half[:, 1024:1024 + 8 * CMAX].rearrange("p (j c) -> p j c", c=CMAX)
        moh_h = half[:, 1280:1280 + NT * NE].rearrange("p (t e) -> p t e", t=NT)
        tri_h, ones_h = half[:, 1408:1408 + P], half[:, 1536:1536 + P]

        psum = ctx.enter_context(nc.psum_tensor("psum", [P, 8, 512], F32))

        x2_rows = nc.dram_tensor("x2_rows", (T, D), F32, kind="Internal").ap()
        moe_rows = nc.dram_tensor("moe_rows", (CMAX * P, D), F32, kind="Internal").ap()

        psum_full = [sem(f"psum_full{b}") for b in range(8)]
        psum_read = [sem(f"psum_read{b}") for b in range(8)]
        x_in = [sem(f"x_in{t}") for t in range(NT)]
        const_in = sem("const_in")
        small_in = sem("small_in")
        router_in = sem("router_in")
        sink_in = sem("sink_in")
        rot_in = sem("rot_in")
        cos_done = sem("cos_done")
        bd_in = sem("bd_in")
        bd_zero = sem("bd_zero")
        pad_zero = sem("pad_zero")
        rows_src = sem("rows_src")
        rows_zero = sem("rows_zero")
        lngb_in = sem("lngb_in")
        ident_in = sem("ident_in")
        mem_in = [sem(f"mem_in{m}") for m in range(MT)]
        early_in = {w: sem(f"early_in{w}") for w in EARLY}
        stage_in = [sem(f"stage_in{h}") for h in range(2)]
        w_hi = sem("w_hi")
        w_lo = sem("w_lo")
        dve_step = sem("dve_step")
        ln_done = sem("ln_done")
        eps_set = sem("eps_set")
        sum_ready = sem("sum_ready")
        mean_ready = sem("mean_ready")
        ssq_ready = sem("ssq_ready")
        deviation = sem("deviation")
        actT_hi = sem("actT_hi")
        scaled = sem("scaled")
        xc_done = sem("xc_done")
        kswap = sem("kswap")
        sig_i = sem("sig_i")
        sp_abs = sem("sp_abs")
        sp_exp = sem("sp_exp")
        sp_done = sem("sp_done")
        decay = sem("decay")
        lru_y = sem("lru_y")
        lru_sq = sem("lru_sq")
        lru_hi = sem("lru_hi")
        lru_lo = sem("lru_lo")
        row_max = sem("row_max")
        exp_done = sem("exp_done")
        prob_done = sem("prob_done")
        att_y = sem("att_y")
        att_hi = sem("att_hi")
        att_lo = sem("att_lo")
        memT_hi = sem("memT_hi")
        m_max = sem("m_max")
        m_prob = sem("m_prob")
        mo_hi = sem("mo_hi")
        var_ready = sem("var_ready")
        rstd_ready = sem("rstd_ready")
        ms_ready = sem("ms_ready")
        rms_ready = sem("rms_ready")
        gain_sq = sem("gain_sq")
        gain = sem("gain")
        x2_stored = sem("x2_stored")
        onehots = sem("onehots")
        selected = sem("selected")
        table_done = sem("table_done")
        slot_done = sem("slot_done")
        moe_in = [sem(f"moe_in{i}") for i in range(6)]
        moe_hi = [sem(f"moe_hi{i}") for i in range(6)]
        moe_lo = [sem(f"moe_lo{i}") for i in range(6)]
        gu_half = sem("gu_half")
        gateup_done = sem("gateup_done")
        silu_done = sem("silu_done")
        h_ready = sem("h_ready")
        htrans_done = sem("htrans_done")
        hT_hi_done = sem("hT_hi_done")
        hT_ready = sem("hT_ready")
        down_done = sem("down_done")
        o_read = sem("o_read")
        o_stored = sem("o_stored")
        xtrans_done = sem("xtrans_done")
        xgT_hi_done = sem("xgT_hi_done")
        xgT_ready = sem("xgT_ready")
        all_stored = sem("all_stored")
        gathered = sem("gathered")
        back_in = [sem(f"back_in{i}") for i in range(NT * TOPK)]
        centred = sem("centred")
        normed = sem("normed")
        y_ready = sem("y_ready")
        y_stored = sem("y_stored")

        def bank(g):
            return psum[:, G[g] % 8, :]

        def wait_full(eng, g):
            eng.wait_ge(psum_full[G[g] % 8], G[g] // 8 + 1)

        def wait_free(eng, g):
            if G[g] >= 8:
                eng.wait_ge(psum_read[G[g] % 8], G[g] // 8)

        def full(ins, g):
            ins.then_inc(psum_full[G[g] % 8], 1)

        def free(ins, g):
            ins.then_inc(psum_read[G[g] % 8], 1)

        def wait_read(eng, *groups):
            for g in groups:
                eng.wait_ge(psum_read[G[g] % 8], G[g] // 8 + 1)

        def table(eng, at, lo=0, hi=CMAX):
            return eng.value_load(ctab[0:1, at:at + 1] if isinstance(at, int) else ctab[0:1, bass.ds(at, 1)],
                                  min_val=lo, max_val=hi)

        def expert_of(eng, c):
            return table(eng, c + T_EXP, 0, NE - 1)

        def is_new(eng, c):
            return table(eng, c + T_NEW, 0, 1)

        FEAT = {n: i for i, n in enumerate(("conv0", "conv1", "conv2", "conv3", "conv_b", "b_r", "b_i",
                                            "lam", "g_att", "g_lru"))}

        def fv(name, ft):
            return feat[:, FEAT[name], ft:ft + 1]

        NORM_NTH = {0: 0, 1: 1, 3: 2}

        def in_slices(n):
            return in0 + n // 2, (n % 2) * P

        def landed(w, h):
            if w in EARLY:
                return scr[:, EARLY[w], h * 1024:(h + 1) * 1024]
            return stage[:, h, :]

        def wait_landed(eng, w, h):
            if w in EARLY:
                eng.wait_ge(early_in[w], 16 * len(pieces[w][1]))
            else:
                eng.wait_ge(stage_in[h], 16 * (STAGED.index(w) + 1))

        IN_KIND = ["xl"] * 4 + ["g"] * 4 + ["k", "v"] + ["q"] * 4
        block = ctx.enter_context(nc.Block())

        @block.sync
        def _(eng):
            def load_ln(name):
                for i, part in enumerate("gb"):
                    v = A[f"{name}_{part}"]
                    v = v if name == "ln_in" else v[0]
                    eng.dma_start(lngb[:, i, :], v.partition_broadcast(P)).then_inc(lngb_in, 16)

            def load_piece(w):
                _, parts, width = pieces[w]
                if w in EARLY:
                    if w in EARLY_AFTER:
                        eng.wait_ge(w_lo, 2 * EARLY_AFTER[w] + 2)
                    n = 2048 // len(parts)
                    for h, part in enumerate(parts):
                        eng.dma_start(scr[:, EARLY[w], h * n:(h + 1) * n].rearrange("p (k n) -> p k n", n=width),
                                      part.rearrange("(k p) n -> p k n", p=P)).then_inc(early_in[w], 16)
                    return
                for h in range(2):
                    nth = STAGED.index(w)
                    if nth > 0:
                        eng.wait_ge(w_lo, 2 * STAGED[nth - 1] + h + 1)
                    eng.dma_start(stage[:, h, :].rearrange("p (k n) -> p k n", n=width),
                                  parts[h].rearrange("(k p) n -> p k n", p=P)).then_inc(stage_in[h], 16)

            eng.dma_start(ident, consts[:, C_ID:C_ID + P]).then_inc(ident_in, 16)
            for m in range(MT):
                eng.dma_start(memr[:, m, :], A["mem"][0, m * P:(m + 1) * P, :]).then_inc(mem_in[m], 16)
            load_piece(0)
            eng.dma_start(xres[:, 0, :], A["x"][0, 0:P, :]).then_inc(x_in[0], 16)
            load_ln("ln_in")
            load_piece(1)
            for t in range(1, NT):
                eng.dma_start(xres[:, t, :], A["x"][0, t * P:(t + 1) * P, :]).then_inc(x_in[t], 16)
                if t + 1 < in0:
                    load_piece(t + 1)
            eng.dma_start(cst[:, C_ID + P:], consts[:, C_ID + P:]).then_inc(const_in, 16)
            for w in range(in0, in0 + 3):
                load_piece(w)
            for i in range(TAPS):
                eng.dma_start(feat[:, i, :], A["conv_w"][0, i].rearrange("(f p) -> p f", p=P),
                              allow_slow_non_contiguous=True).then_inc(small_in, 16)
            for name, key in (("conv_b", "conv_b"), ("b_r", "b_rgate"), ("b_i", "b_igate"),
                              ("lam", "lru_lambda"), ("g_att", "norm_attn_g"), ("g_lru", "norm_lru_g")):
                eng.dma_start(feat[:, FEAT[name], :], A[key][0].rearrange("(f p) -> p f", p=P),
                              allow_slow_non_contiguous=True).then_inc(small_in, 16)
            eng.wait_ge(ln_done, NT)
            eng.dma_start(rot, rots).then_inc(rot_in, 16)
            eng.wait_ge(bd_zero, 1)
            for g, key in enumerate(("w_rgate", "w_igate")):
                w = A[key][0].rearrange("(f two) i j -> two i f j", two=2)
                for par in range(2):
                    s = slice(par * 64, par * 64 + 64)
                    eng.dma_start(gate_bd[s, g, :, s], w[par]).then_inc(bd_in, 16)
            for w in range(in0 + 3, o0):
                load_piece(w)
            eng.dma_start(b_rt[:, 0:NG], A["b_router_group"][0].partition_broadcast(P)).then_inc(router_in, 16)
            eng.dma_start(b_rt[:, NG:], A["b_router_expert"][0].rearrange("g e -> (g e)")
                          .partition_broadcast(P)).then_inc(router_in, 16)
            eng.dma_start(w_rt[:, :, 0:NG], A["w_router_group"][0].rearrange("(k p) g -> p k g", p=P),
                          allow_slow_non_contiguous=True).then_inc(router_in, 16)
            for g in range(NG):
                eng.dma_start(w_rt[:, :, NG + g * EPG:NG + (g + 1) * EPG],
                              A["w_router_expert"][0, g].rearrange("(k p) e -> p k e", p=P),
                              allow_slow_non_contiguous=True).then_inc(router_in, 16)
            for w in range(o0, o0 + 4):
                load_piece(w)
            wait_read(eng, *[("rope", n) for n in range(5)])
            wait_full(eng, ("gate", FT - 1, 1))
            load_ln("ln1")
            for w in range(o0 + 4, wo0):
                load_piece(w)
            def load_moe(i, e):
                key, rows = (("w_gate_e", 0), ("w_up_e", 0), ("w_gate_e", 512), ("w_up_e", 512),
                             ("w_down_e", 0), ("w_down_e", 256))[i]
                w = A[key][0, e] if isinstance(e, int) else A[key][0, bass.ds(e, 1)].rearrange("a k f -> (a k) f")
                n = D if key == "w_down_e" else F
                w = w[rows:rows + P * 2048 // n, :]
                eng.dma_start(moe_landed(i, isinstance(e, int) and e == 0).rearrange("p (k n) -> p k n", n=n),
                              w.rearrange("(k p) n -> p k n", p=P)).then_inc(moe_in[i], 16)

            eng.wait_ge(lru_y, FT)
            for i in (3, 0, 1):
                load_moe(i, 0)
            eng.wait_ge(ln_done, 2 * NT)
            load_ln("ln2")
            for w in range(wo0, len(pieces)):
                load_piece(w)
            wait_full(eng, ("mPT", MH - 1, MT - 1))
            load_moe(5, 0)
            eng.wait_ge(moe_lo[3], 1)
            load_moe(2, 0)
            wait_full(eng, ("wo", 1, NT - 1))
            load_moe(4, 0)
            load_moe(3, 1)
            for t in range(NT):
                eng.wait_ge(ln_done, 2 * NT + t + 1)
                eng.dma_start(x2_rows[t * P:(t + 1) * P, :], xres[:, t, :]).then_inc(x2_stored, 16)
            eng.wait_ge(ln_done, 3 * NT)
            load_ln("ln3")
            for i in (0, 1, 2):
                eng.wait_ge(moe_lo[i], 1)
                load_moe(i, 1)
            load_moe(5, 1)
            eng.wait_ge(moe_lo[4], 1)
            load_moe(4, 1)

            def next_expert(e, first=False):
                for i in range(4):
                    eng.wait_ge(moe_lo[i], e)
                    load_moe(i, e)
                if not first:
                    for i in (4, 5):
                        eng.wait_ge(moe_lo[i], e - 1)
                        load_moe(i, e - 1)

            next_expert(2, True)
            with eng.Fori(3, NE) as e:
                next_expert(e)
            for i in (4, 5):
                eng.wait_ge(moe_lo[i], NE - 1)
                load_moe(i, NE - 1)
            for t in range(NT):
                if t < NT - 1:
                    eng.wait_ge(y_ready, t + 1)
                else:
                    eng.wait_ge(ln_done, 3 * NT + 1)
                eng.dma_start(y_out[0, t * P:(t + 1) * P, :], xres[:, t, :]).then_inc(y_stored, 16)
            eng.wait_ge(y_stored, NT * 16)

        @block.gpsimd
        def _(eng):
            for k in (kpad[0], kpad[1], vpad):
                eng.memset(k[:, 0:CHUNK], 0.0).then_inc(pad_zero, 1)
            eng.memset(qs[:, 0:2, :], 0.0).then_inc(rows_src, 1)
            eng.memset(eps[:, :], EPS).then_inc(eps_set, 1)
            eng.dma_start(sink[:, :], A["attn_sink"][0].partition_broadcast(P)).then_inc(sink_in, 16)
            eng.wait_ge(ln_done, NT)
            eng.memset(lngb[:, 1, :], 0.0).then_inc(bd_zero, 1)

            eng.wait_ge(rows_src, 1)
            wait_full(eng, ("in", 3))
            for c in range(NE, CMAX):
                eng.dma_start(moe_rows[c * P:(c + 1) * P, :], qs[:, 0:2, :]).then_inc(rows_zero, 16)

            def scale_residual(group):
                for t in range(NT):
                    for k in range(2):
                        wait_full(eng, (group, t, k))
                    if group == "x2T":
                        eng.wait_ge(x2_stored, 16 * NT)
                    eng.tensor_scalar(xres[:, t, :], xres[:, t, :], ALPHA, None, ALU.mult).then_inc(scaled, 1)

            scale_residual("x0T")
            eng.wait_ge(rot_in, 16)
            for n in range(5):
                dst = kpad[0][:, CHUNK:] if n == 0 else qs[:, n - 1, :]
                wait_full(eng, ("rope", n))
                eng.tensor_tensor(dst, dst, rot[:, 0, :], ALU.mult).then_inc(cos_done, 1)
            scale_residual("x1T")

            def gather(c):
                col = tokidx[:, c:c + 1] if isinstance(c, int) else tokidx[:, bass.ds(c, 1)]
                wait_read(eng, ("table",))
                eng.tensor_copy(idx_now[:, :], col)
                eng.drain()
                eng.wait_ge(x2_stored, 16 * NT)
                eng.indirect_dma_start(xg, None, x2_rows, bass.IndirectOffsetOnAxis(idx_now[:, 0:1], 0)
                                       ).then_inc(gathered, 16)

            gather(0)
            eng.wait_ge(xtrans_done, 1)
            gather(1)
            scale_residual("x2T")
            eng.wait_ge(table_done, 1)
            n = table(eng, T_N, NE, CMAX)
            with eng.Fori(2, CMAX) as c:
                with eng.If(c < n):
                    eng.wait_ge(gathered, c * 16)
                    eng.wait_ge(xtrans_done, c)
                    gather(c)
            eng.wait_ge(slot_done, 1)
            eng.wait_ge(all_stored, 1)
            for t in range(NT):
                for k in range(TOPK):
                    eng.indirect_dma_start(back[:, t * TOPK + k, :], None, moe_rows,
                                           bass.IndirectOffsetOnAxis(slot_i[:, t, k:k + 1], 0)
                                           ).then_inc(back_in[t * TOPK + k], 16)
            for t in range(NT - 1):
                eng.wait_ge(normed, t + 1)
                eng.tensor_tensor(xres[:, t, :], xres[:, t, :], lngb[:, 1, :], ALU.add).then_inc(y_ready, 1)

        @block.scalar
        def _(eng):
            def split_hi(w):
                for h in range(2):
                    wait_landed(eng, w, h)
                    if w >= RING:
                        wait_full(eng, last_use(w - RING))
                    eng.activation(wring[:, w % RING, 0, h * 1024:(h + 1) * 1024], landed(w, h),
                                   ACT.Copy).then_inc(w_hi, 1)

            def actT_tiles(group, t):
                for k in range(2):
                    wait_full(eng, (group, t, k))
                    eng.activation(actT[:, 0, 4 * k:4 * k + 4, t * P:(t + 1) * P],
                                   bank((group, t, k)).rearrange("p (k t) -> p k t", t=P),
                                   ACT.Copy).then_inc(actT_hi, 1)

            def inverse_deviation(n, t):
                eng.wait_ge(var_ready, t + 1)
                eng.activation(rstd[:, t:t + 1], rstd[:, t:t + 1], ACT.Sqrt).then_inc(rstd_ready, 1)

            def norm_deviation(n, t):
                if n == 0 and t == 0:
                    eng.wait_ge(eps_set, 1)
                if n == 0:
                    eng.wait_ge(x_in[t], 16)
                    eng.activation(squares_out[n], xres[:, t, :], ACT.Copy, accum_out=sums[:, t, 0:1]
                                   ).then_inc(sum_ready, 1)
                    eng.wait_ge(sum_ready, t + 1)
                    eng.activation(nmean[:, t:t + 1], sums[:, t, 0:1], ACT.Copy, scale=-1.0 / D).then_inc(mean_ready, 1)
                nth = NORM_NTH[n] * NT + t + 1
                eng.wait_ge(mean_ready, nth)
                eng.activation(squares_out[n], xres[:, t, :], ACT.Square, bias=nmean[:, t:t + 1],
                               accum_out=ssq[:, t:t + 1]).then_inc(ssq_ready, 1)
                eng.wait_ge(ssq_ready, nth)
                eng.activation(rstd[:, t:t + 1], ssq[:, t:t + 1], ACT.Sqrt, scale=1.0 / D,
                               bias=eps[:, :]).then_inc(deviation, 1)

            for m in range(MT):
                for k in range(2):
                    wait_full(eng, ("memT", m, k))
                    eng.activation(memT[:, 0, 4 * k:4 * k + 4, m * P:(m + 1) * P],
                                   bank(("memT", m, k)).rearrange("p (k t) -> p k t", t=P),
                                   ACT.Copy).then_inc(memT_hi, 1)
            for w in range(RING):
                split_hi(w)
                norm_deviation(0, w)
            def mem_keys(q):
                for n in (2 * q, 2 * q + 1):
                    wait_full(eng, ("mk", n))
                    i = eng.activation(mkT[:, n, :], bank(("mk", n))[:, 0:MEM], ACT.Copy)
                    free(i, ("mk", n))

            mem_keys(0)
            split_hi(RING)
            norm_deviation(0, 3)
            mem_keys(1)
            mem_keys(2)
            for t in range(NT):
                actT_tiles("x0T", t)
            split_hi(RING + 1)
            mem_keys(3)
            split_hi(RING + 2)
            split_hi(RING + 3)
            eng.wait_ge(sp_abs, 1)
            eng.activation(sp[:, 1, :], sp[:, 0, :], ACT.Exp, scale=-1.0).then_inc(sp_exp, 1)
            eng.wait_ge(pad_zero, 3)
            for n, kind in enumerate(IN_KIND):
                wait_full(eng, ("in", n))
                if n == IN_KIND.index("q"):
                    eng.wait_ge(rows_zero, 16 * EXTRA)
                src = bank(("in", n))
                if kind == "xl":
                    i = eng.activation(xl[:, n, :], src, ACT.Copy)
                    free(i, ("in", n))
                elif kind == "g":
                    free(eng.activation(gel[:, n - 4, :], src, ACT.Gelu_apprx_tanh), ("in", n))
                else:
                    dst = kpad[0][:, CHUNK:] if kind == "k" else vpad[:, CHUNK:] if kind == "v" else qs[:, n - 10, :]
                    i = eng.activation(dst, src, ACT.Copy)
                    free(i, ("in", n))
                if n % 2:
                    split_hi(in0 + n // 2 + RING)

            for ft in range(FT):
                wait_full(eng, ("gate", ft, 0))
                i = eng.activation(ra[:, ft, :], bank(("gate", ft, 0)), ACT.Sigmoid, bias=fv("b_r", ft))
                free(i, ("gate", ft, 0))
                wait_full(eng, ("gate", ft, 1))
                eng.activation(bank(("gate", ft, 1)), bank(("gate", ft, 1)), ACT.Sigmoid,
                               bias=fv("b_i", ft)).then_inc(sig_i, 1)
            for b in range(2):
                wait_full(eng, ("vwin", b))
                i = eng.activation(vwin[:, 4 * b:4 * b + 4, :],
                                   bank(("vwin", b)).rearrange("p (c v) -> p c v", v=P), ACT.Copy)
                free(i, ("vwin", b))

            eng.wait_ge(sp_done, 1)
            wait_read(eng, *[("gate", ft, 0) for ft in range(FT)])

            def decays(ft):
                eng.activation(th[:, ft, :], ra[:, ft, :], ACT.Tanh, scale=sp[:, 6, ft:ft + 1]).then_inc(decay, 1)
                eng.wait_ge(decay, 2 * ft + 1)
                eng.activation(ra[:, ft, :], ra[:, ft, :], ACT.Exp, scale=sp[:, 7, ft:ft + 1]).then_inc(decay, 1)

            def soft_exp(t):
                b = t % 2
                eng.wait_ge(row_max, t + 1)
                if t >= 2:
                    for k in range(2):
                        wait_full(eng, ("PT", t - 2, k))
                for h in range(HEADS):
                    par, hp = h % 2, h // 2
                    i = eng.activation(prob[:, b, h, :], bank(("S", t, par))[:, hp * P:(hp + 1) * P], ACT.Exp,
                                       bias=nmx[:, b, h:h + 1], scale=HD ** -0.5, accum_out=psm[:, b, h:h + 1])
                    if hp == 3:
                        free(i, ("S", t, par))
                eng.activation(esk[:, b, :], esk[:, b, :], ACT.Exp).then_inc(exp_done, 1)

            def prob_T(t):
                for k in range(2):
                    wait_full(eng, ("PT", t, k))
                    if t >= 1:
                        wait_full(eng, ("O", t - 1))
                    i = eng.activation(probT[:, 4 * k:4 * k + 4, :],
                                       bank(("PT", t, k)).rearrange("p (h q) -> p h q", q=P), ACT.Copy)
                    free(i, ("PT", t, k))

            def att_split(t):
                s = slice(t * P, (t + 1) * P)
                eng.wait_ge(att_y, t + 1)
                eng.activation(actT[:, 0, 0:4, s], qs[:, :, s], ACT.Copy).then_inc(att_hi, 1)

            def att_square(t):
                g = ("O", t)
                eng.wait_ge(att_lo, t + 1)
                i = eng.activation(qs[:, :, t * P:(t + 1) * P], bank(g).rearrange("p (f t) -> p f t", t=P), ACT.Square)
                free(i, g)

            def lru_square(ft):
                eng.wait_ge(lru_y, ft + 1)
                eng.activation(ra[:, ft, :], xl[:, ft, :], ACT.Square).then_inc(lru_sq, 1)

            def lru_out(ft):
                eng.activation(actT[:, 0, FT + ft, :], xl[:, ft, :], ACT.Copy, scale=fv("g_lru", ft)
                               ).then_inc(lru_hi, 1)

            def mem_values(q):
                for m in range(MT):
                    wait_full(eng, ("mv", q, m))
                    i = eng.activation(mvv[:, m, q * 256:(q + 1) * 256], bank(("mv", q, m))[:, 0:256], ACT.Copy)
                    free(i, ("mv", q, m))

            mem_values(0)
            soft_exp(0)
            split_hi(mv0 + RING)
            for ft in range(FT):
                decays(ft)
            soft_exp(1)
            mem_values(1)
            prob_T(0)
            for ft in range(FT):
                eng.wait_ge(gain_sq, ft + 1)
                eng.activation(th[:, ft, :], th[:, ft, :], ACT.Sqrt).then_inc(gain, 1)
            split_hi(mv0 + 1 + RING)
            mem_values(2)
            att_split(0)
            prob_T(1)
            soft_exp(2)
            att_square(0)
            mem_values(3)
            prob_T(2)
            soft_exp(3)
            att_split(1)
            split_hi(mv0 + 2 + RING)
            att_square(1)
            prob_T(3)
            lru_square(0)
            lru_square(1)
            att_split(2)
            split_hi(mv0 + 3 + RING)
            lru_square(2)
            lru_square(3)
            att_square(2)
            att_split(3)
            wait_full(eng, ("O", NT - 1))
            for ft in range(FT):
                lru_out(ft)
            att_square(NT - 1)

            eng.wait_ge(ms_ready, 1)
            eng.activation(rms[:, :, :], rms[:, :, :], ACT.Sqrt).then_inc(rms_ready, 1)
            split_hi(o0 + 3)
            split_hi(o0 + 4)
            for t in range(NT):
                if t >= 2:
                    actT_tiles("x1T", t - 2)
                norm_deviation(1, t)
            actT_tiles("x1T", 2)
            split_hi(o0 + 5)
            actT_tiles("x1T", 3)
            split_hi(o0 + 6)

            def m_exps(h):
                b = h % 2
                eng.wait_ge(m_max, h + 1)
                if h >= 2:
                    wait_full(eng, ("mPT", h - 2, 1))
                for t in range(NT):
                    i = eng.activation(mprob[:, b, t, :], bank(("mS", h, t // 2))[:, (t % 2) * MEM:(t % 2 + 1) * MEM],
                                       ACT.Exp, bias=nmx[:, b, t:t + 1], scale=MHD ** -0.5,
                                       accum_out=psm[:, b, t:t + 1])
                    if t % 2:
                        free(i, ("mS", h, t // 2))

            def m_queries(h):
                for n in range(2):
                    wait_full(eng, ("mq", h, n))
                    i = eng.activation(mq[:, 2 * h + n, :], bank(("mq", h, n)), ACT.Copy)
                    free(i, ("mq", h, n))

            def m_out_hi(h):
                for n in range(2):
                    wait_full(eng, ("mO", h, n))
                    eng.activation(actT[:, 0, 2 * h + n, :], bank(("mO", h, n)), ACT.Copy).then_inc(mo_hi, 1)

            def m_prob_T(h):
                for m in range(MT):
                    wait_full(eng, ("mPT", h, m))
                    if h >= 2:
                        wait_full(eng, ("mO", h - 2, 1))
                    i = eng.activation(mpT[:, h % 2, m, :], bank(("mPT", h, m)), ACT.Copy)
                    free(i, ("mPT", h, m))

            def moe_split_hi(i, e=0, used=None):
                eng.wait_ge(moe_in[i], 16 * e + 16)
                if used is not None:
                    eng.wait_ge(*used)
                eng.activation(moe_w(i, 0), moe_landed(i, isinstance(e, int)), ACT.Copy).then_inc(moe_hi[i], 1)

            for h in range(MH):
                if h == 2:
                    eng.wait_ge(lru_lo, FT)
                    moe_split_hi(3)
                m_queries(h)
                if q0 + h + 3 < len(pieces):
                    split_hi(q0 + h + 3)
                if h >= 2:
                    m_prob_T(h - 2)
                if h >= 1:
                    m_exps(h - 1)
            for name, h in M_TAIL:
                {"mO": m_out_hi, "mS": m_exps, "mPT": m_prob_T}[name](h)
            split_hi(len(pieces) - 1)
            moe_split_hi(5)

            def x2T_tile(t):
                for k in range(2):
                    g = ("x2T", t, k)
                    wait_full(eng, g)
                    wait_full(eng, ("mO", 3, 1))
                    i = eng.activation(x2T[:, 4 * k:4 * k + 4, t * P:(t + 1) * P],
                                       bank(g).rearrange("p (k t) -> p k t", t=P), ACT.Copy)
                    free(i, g)

            def logits_tile(t):
                W = NG + NE
                g = ("logitsT", t)
                wait_full(eng, g)
                free(eng.activation(logT[0:W, t * P:(t + 1) * P], bank(g)[0:W, 0:P], ACT.Copy), g)

            for t in range(NT):
                inverse_deviation(2, t)
                if t >= 2:
                    x2T_tile(t - 2)
            x2T_tile(2)
            logits_tile(0)
            x2T_tile(3)
            for t in range(1, NT):
                logits_tile(t)

            wait_full(eng, ("wo", 1, NT - 1))
            for i in (0, 1, 2):
                moe_split_hi(i)

            def silu(c):
                eng.wait_ge(gateup_done, c + 1)
                eng.activation(silu_g, psum[:, 2, :], ACT.Silu).then_inc(silu_done, 1)

            def evac_x(c):
                eng.wait_ge(xtrans_done, c + 1)
                eng.activation(xgT_hi, psum[:, 0:2, :].rearrange("p a b -> p (a b)"), ACT.Copy
                               ).then_inc(xgT_hi_done, 1)

            def evac_h(c):
                eng.wait_ge(htrans_done, c + 1)
                eng.activation(hT_hi, psum[:, 4, :], ACT.Copy).then_inc(hT_hi_done, 1)

            def evac_o(c, stored):
                eng.wait_ge(down_done, c + 1)
                if stored is not None:
                    eng.wait_ge(o_stored, stored)
                eng.activation(moe_o, psum[:, 5:7, :].rearrange("p a b -> p (a b)"), ACT.Copy).then_inc(o_read, 1)
                eng.wait_ge(o_read, c + 1)
                rows = moe_rows[c * P:(c + 1) * P, :] if isinstance(c, int) else moe_rows[bass.ds(c * P, P), :]
                eng.dma_start(rows, moe_o).then_inc(o_stored, 16)

            evac_x(0)
            eng.wait_ge(moe_lo[2], 1)
            eng.wait_ge(moe_lo[5], 1)
            moe_split_hi(4)
            eng.wait_ge(onehots, 1)
            eng.activation(below_exp, below, ACT.Exp).then_inc(onehots, 1)
            eng.wait_ge(table_done, 1)
            n = table(eng, T_N, NE, CMAX)

            def new_hi(c, i, used):
                new = is_new(eng, c)
                with eng.If(new > 0):
                    e = expert_of(eng, c)
                    moe_split_hi(i, e, used)
                    moe_split_hi(i + 1, e)

            def act_chunk(c):
                new_hi(c, 0, (gu_half, c))
                silu(c - 1)
                evac_x(c)
                new_hi(c, 2, (gateup_done, c))
                if not isinstance(c, int):
                    evac_o(c - 2, 16 * (c - 2))
                elif c == 2:
                    evac_o(0, None)
                evac_h(c - 1)
                if not isinstance(c, int) or c == 2:
                    new_hi(c - 1, 4, (down_done, c - 1))

            last = table(eng, T_LAST, NE - 1, CMAX - 1)
            previous = table(eng, T_PREV, NE - 2, CMAX - 2)
            act_chunk(1)
            act_chunk(2)
            with eng.Fori(3, CMAX) as c:
                with eng.If(c < n):
                    act_chunk(c)
            silu(last)
            evac_h(last)
            evac_o(previous, 16 * previous)
            new_hi(last, 4, (down_done, last))
            evac_o(last, 16 * last)
            def last_scale(t):
                eng.wait_ge(centred, t + 1)
                eng.activation(xres[:, t, :], xres[:, t, :], ACT.Copy, scale=rstd[:, t:t + 1]).then_inc(normed, 1)

            eng.wait_ge(o_stored, 16 * n)
            eng.activation(esk[:, 0, 0:1], esk[:, 0, 1:2], ACT.Copy).then_inc(all_stored, 1)
            for t in range(NT):
                norm_deviation(3, t)
                if t >= 1:
                    last_scale(t - 1)


        @block.vector
        def _(eng):
            steps = [0]

            def link(ins):
                steps[0] += 1
                ins.then_inc(dve_step, 1)
                eng.wait_ge(dve_step, steps[0])

            def split_lo(w):
                for h in range(2):
                    eng.wait_ge(w_hi, 2 * w + h + 1)
                    s = slice(h * 1024, (h + 1) * 1024)
                    eng.tensor_tensor(wring[:, w % RING, 1, s], landed(w, h),
                                      wring[:, w % RING, 0, s].bitcast(F32), ALU.subtract).then_inc(w_lo, 1)

            def layer_norm(n, t):
                x = xres[:, t, :]
                for h in range(2):
                    last = eng.bn_stats(stats[:, t, h, :], x[:, h * 512:(h + 1) * 512])
                link(last)
                link(eng.bn_aggr(mv[:, t, :], stats[:, t, :, :]))
                link(eng.tensor_scalar(rstd[:, t:t + 1], mv[:, t, 1:2], EPS, None, ALU.add))
                eng.reciprocal(rstd[:, t:t + 1], rstd[:, t:t + 1]).then_inc(var_ready, 1)
                eng.wait_ge(lngb_in, 32 * (n + 1))
                link(eng.scalar_tensor_tensor(x, x, mv[:, t, 0:1], lngb[:, 0, :], ALU.subtract, ALU.mult))
                eng.wait_ge(rstd_ready, t + 1)
                i = eng.scalar_tensor_tensor(x, x, rstd[:, t:t + 1], lngb[:, 1, :], ALU.mult, ALU.add)
                i.then_inc(ln_done, 1)

            def norm_mean(t, halves):
                if halves == 2:
                    i = eng.tensor_scalar(nmean[:, t:t + 1], sums[:, t, 0:1], sums[:, t, 1:2], -1.0 / D,
                                          ALU.add, ALU.mult)
                else:
                    i = eng.tensor_scalar(nmean[:, t:t + 1], sums[:, t, 0:1], -1.0 / D, None, ALU.mult)
                i.then_inc(mean_ready, 1)

            def norm_rest(n, t):
                x = xres[:, t, :]
                eng.wait_ge(deviation, NORM_NTH[n] * NT + t + 1)
                i = eng.reciprocal(rstd[:, t:t + 1], rstd[:, t:t + 1])
                if n <= 1 or t == NT - 1:
                    eng.wait_ge(lngb_in, 32 * (n + 1))
                    link(eng.scalar_tensor_tensor(x, x, nmean[:, t:t + 1], lngb[:, 0, :], ALU.add, ALU.mult))
                    eng.scalar_tensor_tensor(x, x, rstd[:, t:t + 1], lngb[:, 1, :], ALU.mult, ALU.add
                                             ).then_inc(ln_done, 1)
                else:
                    eng.wait_ge(lngb_in, 32 * (n + 1))
                    eng.scalar_tensor_tensor(x, x, nmean[:, t:t + 1], lngb[:, 0, :], ALU.add, ALU.mult
                                             ).then_inc(centred, 1)

            actT_count = [0]

            def actT_lo_tile(group, t):
                for k in range(2):
                    actT_count[0] += 1
                    eng.wait_ge(actT_hi, actT_count[0])
                    d = slice(4 * k, 4 * k + 4)
                    s = slice(t * P, (t + 1) * P)
                    i = eng.tensor_tensor(actT[:, 1, d, s], bank((group, t, k)).rearrange("p (k t) -> p k t", t=P),
                                          actT[:, 0, d, s].bitcast(F32), ALU.subtract)
                    free(i, (group, t, k))

            for m in range(MT):
                for k in range(2):
                    eng.wait_ge(memT_hi, 2 * m + k + 1)
                    d = slice(4 * k, 4 * k + 4)
                    s = slice(m * P, (m + 1) * P)
                    i = eng.tensor_tensor(memT[:, 1, d, s], bank(("memT", m, k)).rearrange("p (k t) -> p k t", t=P),
                                          memT[:, 0, d, s].bitcast(F32), ALU.subtract)
                    free(i, ("memT", m, k))
            for w in range(NT):
                split_lo(w)
                norm_rest(0, w)
            for t in range(NT):
                actT_lo_tile("x0T", t)
            for w in range(NT, NT + 3):
                split_lo(w)

            lam = feat[:, FEAT["lam"], :]
            eng.wait_ge(small_in, 16 * 10)
            link(eng.tensor_scalar(sp[:, 5, :], lam, -1.0, None, ALU.mult))
            eng.tensor_tensor(sp[:, 0, :], sp[:, 5, :], lam, ALU.max).then_inc(sp_abs, 1)
            eng.wait_ge(sp_exp, 1)
            e1, z, z2, p = sp[:, 1, :], sp[:, 2, :], sp[:, 3, :], sp[:, 4, :]
            link(eng.tensor_scalar(z, e1, 2.0, None, ALU.add))
            link(eng.reciprocal(z, z))
            link(eng.tensor_tensor(z, z, e1, ALU.mult))
            link(eng.tensor_tensor(z2, z, z, ALU.mult))
            link(eng.tensor_scalar(p, z2, 1.0 / 15, None, ALU.mult))
            for k in (13, 11, 9, 7, 5, 3):
                link(eng.scalar_tensor_tensor(p, p, 1.0 / k, z2, ALU.add, ALU.mult))
            link(eng.scalar_tensor_tensor(p, p, 1.0, z, ALU.add, ALU.mult))
            link(eng.tensor_scalar(sp[:, 5, :], lam, -1.0, 0.0, ALU.mult, ALU.max))
            link(eng.scalar_tensor_tensor(p, p, 2.0, sp[:, 5, :], ALU.mult, ALU.add))
            link(eng.tensor_scalar(sp[:, 6, :], p, LRU_C, None, ALU.mult))
            eng.tensor_scalar(sp[:, 7, :], p, -LRU_C, None, ALU.mult).then_inc(sp_done, 1)

            eng.wait_ge(const_in, 16)

            def conv(ft):
                wait_read(eng, ("in", ft))
                x, y = xl[:, ft, :], xc[:, ft, :]
                link(eng.tensor_scalar(y, x, fv("conv3", ft), fv("conv_b", ft), ALU.mult, ALU.add))
                for s in (1, 2, 3):
                    i = eng.scalar_tensor_tensor(y[:, s:], x[:, :T - s], fv(f"conv{3 - s}", ft), y[:, s:],
                                                 ALU.mult, ALU.add)
                    if s < 3:
                        link(i)
                i.then_inc(xc_done, 1)

            for n in range(mv0 - in0):
                if n < 2:
                    conv(2 * n)
                    conv(2 * n + 1)
                split_lo(in0 + n + RING)

            for ft in range(FT):
                eng.wait_ge(sig_i, ft + 1)
                i = eng.tensor_tensor(xc[:, ft, :], xc[:, ft, :], bank(("gate", ft, 1)), ALU.mult)
                free(i, ("gate", ft, 1))
            eng.wait_ge(rot_in, 16)
            for n in range(5):
                dst = kpad[0][:, CHUNK:] if n == 0 else qs[:, n - 1, :]
                b = bank(("rope", n))
                wait_full(eng, ("rope", n))
                link(eng.tensor_tensor(b, b, rot[:, 1, :], ALU.mult))
                eng.wait_ge(cos_done, n + 1)
                i = eng.tensor_tensor(dst, dst, b, ALU.add)
                free(i, ("rope", n))
                if n == 0:
                    wait_read(eng, ("rope", 0))
                    eng.wait_ge(pad_zero, 3)
                    eng.tensor_copy(kpad[1][0:64, CHUNK:], kpad[0][64:128, CHUNK:])
                    eng.tensor_copy(kpad[1][64:128, CHUNK:], kpad[0][0:64, CHUNK:]).then_inc(kswap, 1)

            eng.wait_ge(sink_in, 16)

            def soft_max(t):
                b = t % 2
                for par in range(2):
                    g = ("S", t, par)
                    wait_full(eng, g)
                    s = bank(g).rearrange("p (h k) -> p h k", k=P)
                    if t == 0:
                        link(eng.tensor_tensor(s, s, mask0.unsqueeze(1).to_broadcast([P, 4, P]), ALU.add))
                    i = eng.tensor_reduce(mx[:, b, par::2], s, AX, ALU.max)
                link(i)
                link(eng.scalar_tensor_tensor(mx[:, b, :], mx[:, b, :], HD ** -0.5, sink[:, :], ALU.mult, ALU.max))
                eng.tensor_scalar(nmx[:, b, :], mx[:, b, :], -1.0, None, ALU.mult)
                eng.tensor_tensor(esk[:, b, :], sink[:, :], mx[:, b, :], ALU.subtract).then_inc(row_max, 1)

            def soft_norm(t):
                b = t % 2
                eng.wait_ge(exp_done, t + 1)
                link(eng.tensor_tensor(rden[:, b, :], psm[:, b, :], esk[:, b, :], ALU.add))
                link(eng.reciprocal(rden[:, b, :], rden[:, b, :]))
                eng.tensor_tensor(prob[:, b], prob[:, b], rden[:, b, :].unsqueeze(2).to_broadcast([P, HEADS, P]),
                                  ALU.mult).then_inc(prob_done, 1)

            def att_out(t):
                g = ("O", t)
                wait_full(eng, g)
                eng.tensor_tensor(qs[:, :, t * P:(t + 1) * P], bank(g).rearrange("p (f t) -> p f t", t=P),
                                  feat[:, FEAT["g_att"], :].unsqueeze(2).to_broadcast([P, FT, P]), ALU.mult
                                  ).then_inc(att_y, 1)

            def att_lo_t(t):
                s = slice(t * P, (t + 1) * P)
                eng.wait_ge(att_hi, t + 1)
                eng.tensor_tensor(actT[:, 1, 0:4, s], qs[:, :, s], actT[:, 0, 0:4, s].bitcast(F32),
                                  ALU.subtract).then_inc(att_lo, 1)

            def lru(ft):
                eng.wait_ge(decay, 2 * ft + 2)
                a, h, y = ra[:, ft, :], th[:, ft, :], xl[:, ft, :]
                link(eng.tensor_tensor(y, a, a, ALU.mult))
                link(eng.scalar_tensor_tensor(h, y, 1.0, h, ALU.add, ALU.mult))
                eng.tensor_scalar(h, h, 0.0, None, ALU.max).then_inc(gain_sq, 1)

            def lru_scan(ft):
                a, h, y = ra[:, ft, :], th[:, ft, :], xl[:, ft, :]
                eng.wait_ge(gain, ft + 1)
                link(eng.tensor_tensor(h, h, xc[:, ft, :], ALU.mult))
                link(eng.tensor_tensor_scan(y, a, h, 0.0, ALU.mult, ALU.add))
                eng.tensor_tensor(y, y, gel[:, ft, :], ALU.mult).then_inc(lru_y, 1)

            def lru_lo_t(ft):
                eng.wait_ge(lru_hi, ft + 1)
                eng.scalar_tensor_tensor(actT[:, 1, FT + ft, :], xl[:, ft, :], fv("g_lru", ft),
                                         actT[:, 0, FT + ft, :].bitcast(F32), ALU.mult, ALU.subtract
                                         ).then_inc(lru_lo, 1)

            soft_max(0)
            soft_norm(0)
            soft_max(1)
            split_lo(mv0 + RING)
            for ft in range(FT):
                lru(ft)
            soft_norm(1)
            split_lo(mv0 + 1 + RING)
            att_out(0)
            lru_scan(0)
            soft_max(2)
            att_lo_t(0)
            soft_norm(2)
            soft_max(3)
            att_out(1)
            lru_scan(1)
            lru_scan(2)
            soft_norm(3)
            att_lo_t(1)
            split_lo(mv0 + 2 + RING)
            lru_scan(3)
            att_out(2)
            att_lo_t(2)
            split_lo(mv0 + 3 + RING)
            att_out(3)
            att_lo_t(3)
            for ft in range(FT):
                lru_lo_t(ft)

            g = ("sq",)
            wait_full(eng, g)
            free(eng.tensor_scalar(rms[:, :, :], bank(g)[:, 0:2 * NT].rearrange("p (b t) -> p b t", b=2),
                                   1.0 / D_ATT, EPS, ALU.mult, ALU.add), g)
            wait_read(eng, g)
            eng.reciprocal(rms[:, :, :], rms[:, :, :]).then_inc(ms_ready, 1)
            eng.wait_ge(rms_ready, 1)
            eng.wait_ge(scaled, NT)

            def add_out(h, t, b):
                g = ("out", h, t, b)
                x = xres[:, t, h * 512:(h + 1) * 512]
                wait_full(eng, g)
                i = eng.scalar_tensor_tensor(x, bank(g), rms[:, b, t:t + 1], x, ALU.mult, ALU.add,
                                             accum_out=sums[:, t, h:h + 1] if b == 1 else None)
                free(i, g)
                wait_read(eng, g)

            for b in range(2):
                for t in range(NT):
                    add_out(0, t, b)
                split_lo(o0 + 3 + b)
            for t in range(NT):
                for b in range(2):
                    add_out(1, t, b)
                norm_mean(t, 2)
                if t >= 2:
                    actT_lo_tile("x1T", t - 2)
                norm_rest(1, t)
            actT_lo_tile("x1T", 2)
            split_lo(o0 + 5)
            actT_lo_tile("x1T", 3)
            split_lo(o0 + 6)

            def m_maxes(h):
                b = h % 2
                for n in range(2):
                    g = ("mS", h, n)
                    wait_full(eng, g)
                    i = eng.tensor_reduce(mx[:, b, 2 * n:2 * n + 2], bank(g).rearrange("p (t m) -> p t m", m=MEM),
                                          AX, ALU.max)
                link(i)
                eng.tensor_scalar(nmx[:, b, 0:NT], mx[:, b, 0:NT], -(MHD ** -0.5), None, ALU.mult
                                  ).then_inc(m_max, 1)

            def m_norm(h):
                b = h % 2
                wait_read(eng, ("mS", h, 0), ("mS", h, 1))
                link(eng.reciprocal(rden[:, b, 0:NT], psm[:, b, 0:NT]))
                eng.tensor_tensor(mprob[:, b], mprob[:, b], rden[:, b, 0:NT].unsqueeze(2).to_broadcast([P, NT, MEM]),
                                  ALU.mult).then_inc(m_prob, 1)

            def m_out_lo(h):
                for n in range(2):
                    eng.wait_ge(mo_hi, 2 * h + n + 1)
                    i = eng.tensor_tensor(actT[:, 1, 2 * h + n, :], bank(("mO", h, n)),
                                          actT[:, 0, 2 * h + n, :].bitcast(F32), ALU.subtract)
                    free(i, ("mO", h, n))

            def moe_split_lo(i, e=0):
                eng.wait_ge(moe_hi[i], e + 1)
                eng.tensor_tensor(moe_w(i, 1), moe_landed(i, isinstance(e, int)), moe_w(i, 0).bitcast(F32), ALU.subtract
                                  ).then_inc(moe_lo[i], 1)

            for h in range(MH):
                if h == 2:
                    moe_split_lo(3)
                if q0 + h + 3 < len(pieces):
                    split_lo(q0 + h + 3)
                if h >= 1:
                    m_maxes(h - 1)
                    m_norm(h - 1)
            for name, h in M_TAIL:
                if name == "mO":
                    m_out_lo(h)
                if name == "mS":
                    m_maxes(h)
                    m_norm(h)
            split_lo(len(pieces) - 1)
            eng.wait_ge(w_lo, 2 * len(pieces))
            eng.tensor_copy(tri_h, tri)
            eng.tensor_copy(ones_h, ones)
            moe_split_lo(5)

            eng.wait_ge(scaled, 2 * NT)
            for h in range(2):
                for t in range(NT):
                    x = xres[:, t, h * 512:(h + 1) * 512]
                    g = ("wo", h, t)
                    wait_full(eng, g)
                    i = eng.tensor_tensor(x, bank(g), x, ALU.add)
                    free(i, g)
                    wait_read(eng, g)
                    if h == 1:
                        layer_norm(2, t)

            lg = rtmp(NT, NG + NE)
            eng.wait_ge(router_in, 16 * (3 + NG))
            g = ("logits",)
            wait_full(eng, g)
            i = eng.tensor_tensor(lg, bank(g)[:, 0:NT * (NG + NE)].rearrange("p (t e) -> p t e", t=NT),
                                  b_rt[:, :].unsqueeze(1).to_broadcast([P, NT, NG + NE]), ALU.add)
            free(i, g)
            wait_read(eng, g)
            wgt = cst[:, C_WG:C_WG + EPG].unsqueeze(1).to_broadcast([P, NT, EPG])
            tmp4 = rtmp(NT, 4)
            m1 = rtmp(NT)

            def first_hot(dst, v, m):
                link(eng.tensor_tensor(tmp4, v, m.unsqueeze(2).to_broadcast([P, NT, 4]), ALU.is_equal))
                link(eng.tensor_tensor(tmp4, tmp4, wgt, ALU.mult))
                link(eng.tensor_reduce(m1, tmp4, AX, ALU.max))
                link(eng.tensor_tensor(dst, tmp4, m1.unsqueeze(2).to_broadcast([P, NT, 4]), ALU.is_equal))

            gl = lg[:, :, 0:NG]
            gm, gh = rtmp(NT), rtmp(NT, NG)
            gx = rtmp(NT, NG)
            link(eng.tensor_reduce(gm, gl, AX, ALU.max))
            first_hot(gh, gl, gm)
            link(eng.tensor_tensor(gx, gl, gm.unsqueeze(2).to_broadcast([P, NT, NG]), ALU.subtract))
            pick = rtmp(NT, NG, EPG)
            link(eng.tensor_tensor(pick, lg[:, :, NG:].rearrange("p t (g e) -> p t g e", g=NG),
                                   gh.unsqueeze(3).to_broadcast([P, NT, NG, EPG]), ALU.mult))
            el = rtmp(NT, EPG)
            link(eng.tensor_reduce(el, pick.rearrange("p t g e -> p t e g"), AX, ALU.add))
            em1, em2, eh1, eh2, el2 = rtmp(NT), rtmp(NT), rtmp(NT, EPG), rtmp(NT, EPG), rtmp(NT, EPG)
            link(eng.tensor_reduce(em1, el, AX, ALU.max))
            first_hot(eh1, el, em1)
            link(eng.scalar_tensor_tensor(el2, eh1, 2 * NEG, el, ALU.mult, ALU.add))
            link(eng.tensor_reduce(em2, el2, AX, ALU.max))
            first_hot(eh2, el2, em2)
            eng.tensor_tensor(below[:, :, 0], em2, em1, ALU.subtract)
            link(eng.tensor_copy(below[:, :, 1:], gx))
            for k, eh in enumerate((eh1, eh2)):
                m = moh[:, k].rearrange("p t (g e) -> p t g e", g=NG)
                i = eng.tensor_tensor(m, eh.unsqueeze(2).to_broadcast([P, NT, NG, EPG]),
                                      gh.unsqueeze(3).to_broadcast([P, NT, NG, EPG]), ALU.mult)
            link(i)
            eng.tensor_tensor(moh_h, moh[:, 0], moh[:, 1], ALU.add).then_inc(onehots, 1)

            g = ("rank",)
            wait_full(eng, g)
            rk_all = rtmp(NT + 1, NE)
            i = eng.tensor_copy(rk_all, bank(g)[:, 0:(NT + 1) * NE].rearrange("p (t e) -> p t e", e=NE))
            free(i, g)
            wait_read(eng, g)
            cnt = rk_all[:, NT, :]
            xe, xs, end, start = rtmp(NE), rtmp(NE), rtmp(NE), rtmp(NE)
            big = rtmp(3, NE)
            thr = cst[:, C_THR:C_THR + 3]
            experts = cst[:, C_EXP:C_EXP + NE]
            link(eng.tensor_tensor(big, cnt.unsqueeze(1).to_broadcast([P, 3, NE]),
                                   thr.unsqueeze(2).to_broadcast([P, 3, NE]), ALU.is_gt))
            link(eng.tensor_reduce(xe, big.rearrange("p j e -> p e j"), AX, ALU.add))
            one_row = cst[:, C_ONES:C_ONES + NE]
            link(eng.tensor_tensor_scan(xs, one_row, xe, 0.0, ALU.mult, ALU.add))
            link(eng.tensor_tensor(end, xs, experts, ALU.add))
            link(eng.tensor_tensor(start, end, xe, ALU.subtract))
            prod = rtmp(2, TOPK * NT, NE)
            vals = rtmp(2, TOPK * NT)
            for v, src in enumerate((rk_all[:, 0:NT, :], start.unsqueeze(1).to_broadcast([P, NT, NE]))):
                for k in range(TOPK):
                    i = eng.tensor_tensor(prod[:, v, k * NT:(k + 1) * NT, :], moh[:, k], src, ALU.mult)
            link(i)
            link(eng.tensor_reduce(vals, prod, AX, ALU.add))
            rank, first = vals[:, 0, :], vals[:, 1, :]
            over = rtmp(TOPK * NT, 3)
            jv, cv, row = rtmp(TOPK * NT), rtmp(TOPK * NT), rtmp(TOPK * NT)
            link(eng.tensor_tensor(over, rank.unsqueeze(2).to_broadcast([P, TOPK * NT, 3]),
                                   thr.unsqueeze(1).to_broadcast([P, TOPK * NT, 3]), ALU.is_ge))
            link(eng.tensor_reduce(jv, over, AX, ALU.add))
            eng.scalar_tensor_tensor(row, jv, -float(P), rank, ALU.mult, ALU.add)
            link(eng.tensor_tensor(cv, first, jv, ALU.add))
            iota_r = cst[:, C_ROW:C_ROW + P]
            iota_c = cst[:, C_CHK:C_CHK + CMAX]
            in_c = rtmp(TOPK * NT, CMAX)
            J = TOPK * NT
            eng.tensor_tensor(in_c, iota_c.unsqueeze(1).to_broadcast([P, J, CMAX]),
                              cv.unsqueeze(2).to_broadcast([P, J, CMAX]), ALU.is_equal)
            link(eng.tensor_tensor(selT, iota_r.unsqueeze(1).to_broadcast([P, J, P]),
                                   row.unsqueeze(2).to_broadcast([P, J, P]), ALU.is_equal))
            token = cst[:, C_TOK:C_TOK + NT]
            for k in range(TOPK):
                i = eng.tensor_tensor(sel_c[:, k * NT:(k + 1) * NT, :], in_c[:, k * NT:(k + 1) * NT, :],
                                      token.unsqueeze(2).to_broadcast([P, NT, CMAX]), ALU.mult)
            i.then_inc(selected, 1)
            endb = kvm[:, 3, 0:CMAX * NE].rearrange("p (c e) -> p c e", e=NE)
            ctf = rtmp(TAB_W)
            ef = ctf[:, T_EXP:T_EXP + CMAX]
            link(eng.tensor_tensor(endb, end.unsqueeze(1).to_broadcast([P, CMAX, NE]),
                                   iota_c.unsqueeze(2).to_broadcast([P, CMAX, NE]), ALU.is_lt))
            link(eng.tensor_reduce(ef, endb, AX, ALU.add))
            g = ("table",)
            wait_full(eng, g)
            i = eng.tensor_copy(tokidx[:, :], bank(g)[:, 0:CMAX])
            free(i, g)
            link(eng.tensor_scalar(ef, ef, float(NE - 1), None, ALU.min))
            eng.tensor_tensor(ctf[:, T_NEW + 1:T_NEW + CMAX], ef[:, 1:], ef[:, :CMAX - 1], ALU.is_gt)
            eng.tensor_scalar(ctf[:, T_NEW:T_NEW + 1], xs[:, 0:1], 0.0, 1.0, ALU.mult, ALU.add)
            eng.tensor_scalar(ctf[:, T_N:T_N + 1], xs[:, NE - 1:NE], float(NE), None, ALU.add)
            eng.tensor_scalar(ctf[:, T_LAST:T_LAST + 1], xs[:, NE - 1:NE], float(NE - 1), None, ALU.add)
            link(eng.tensor_scalar(ctf[:, T_PREV:T_PREV + 1], xs[:, NE - 1:NE], float(NE - 2), None, ALU.add))
            eng.tensor_copy(ctab[0:1, :], ctf[0:1, :]).then_inc(table_done, 1)
            for i in (0, 1, 2):
                moe_split_lo(i)
            slot_f = rtmp(TOPK * NT)
            link(eng.scalar_tensor_tensor(slot_f, cv, float(P), row, ALU.mult, ALU.add))
            eng.tensor_copy(slot_i[:, :, :], slot_f.rearrange("p (k t) -> p t k", k=TOPK)).then_inc(slot_done, 1)
            def evac_x(c):
                eng.wait_ge(xgT_hi_done, c + 1)
                eng.tensor_tensor(xgT_lo, psum[:, 0:2, :].rearrange("p a b -> p (a b)"), xgT_hi.bitcast(F32),
                                  ALU.subtract).then_inc(xgT_ready, 1)

            def h_mul(c):
                eng.wait_ge(silu_done, c + 1)
                eng.tensor_tensor(h_act, silu_g, psum[:, 3, :], ALU.mult).then_inc(h_ready, 1)

            def evac_h(c):
                eng.wait_ge(hT_hi_done, c + 1)
                eng.tensor_tensor(hT_lo, psum[:, 4, :], hT_hi.bitcast(F32), ALU.subtract).then_inc(hT_ready, 1)

            evac_x(0)
            moe_split_lo(4)
            eng.wait_ge(onehots, 2)
            den, dg = rtmp(NT), rtmp(NT)
            link(eng.tensor_reduce(dg, below_exp[:, :, 1:], AX, ALU.add))
            link(eng.scalar_tensor_tensor(den, below_exp[:, :, 0], 1.0, dg, ALU.add, ALU.mult))
            link(eng.reciprocal(gates[:, :, 0], den))
            link(eng.tensor_tensor(gates[:, :, 1], gates[:, :, 0], below_exp[:, :, 0], ALU.mult))
            n = table(eng, T_N, NE, CMAX)

            def new_lo(c, i):
                new = is_new(eng, c)
                with eng.If(new > 0):
                    e = expert_of(eng, c)
                    moe_split_lo(i, e)
                    moe_split_lo(i + 1, e)

            def dve_chunk(c, first=False):
                new_lo(c, 0)
                h_mul(c - 1)
                evac_x(c)
                new_lo(c, 2)
                evac_h(c - 1)
                if not first:
                    new_lo(c - 1, 4)

            last = table(eng, T_LAST, NE - 1, CMAX - 1)
            dve_chunk(1, True)
            with eng.Fori(2, CMAX) as c:
                with eng.If(c < n):
                    dve_chunk(c)
            h_mul(last)
            evac_h(last)
            new_lo(last, 4)

            eng.wait_ge(scaled, 3 * NT)
            for t in range(NT):
                for k in range(TOPK):
                    eng.wait_ge(back_in[t * TOPK + k], 16)
                    link(eng.scalar_tensor_tensor(xres[:, t, :], back[:, t * TOPK + k, :], gates[:, t, k:k + 1],
                                                  xres[:, t, :], ALU.mult, ALU.add,
                                                  accum_out=sums[:, t, 0:1] if k == 1 else None))
                norm_mean(t, 1)
                if t >= 1:
                    norm_rest(3, t - 1)
            norm_rest(3, NT - 1)

        @block.tensor
        def _(eng):
            def mm3(out, s, m, first, last):
                eng.matmul(out, s[0], m[0], start=first, stop=False)
                eng.matmul(out, s[0], m[1], start=False, stop=False)
                return eng.matmul(out, s[1], m[0], start=False, stop=last)

            def wpiece(w, width):
                return [wring[:, w % RING, i, :].rearrange("p (k n) -> p k n", n=width) for i in range(2)]

            def transposes(g, srcs, width=P):
                wait_free(eng, g)
                for j, s in enumerate(srcs):
                    i = eng.transpose(bank(g)[:, j * width:(j + 1) * width], s, ident)
                full(i, g)

            def rows_T(group, t):
                for k in range(2):
                    transposes((group, t, k), [xres[:, t, (4 * k + j) * P:(4 * k + j + 1) * P] for j in range(4)])

            eng.wait_ge(ident_in, 16)
            for m in range(MT):
                eng.wait_ge(mem_in[m], 16)
                for k in range(2):
                    transposes(("memT", m, k), [memr[:, m, (4 * k + j) * P:(4 * k + j + 1) * P] for j in range(4)])
            wait_read(eng, *[("memT", m, k) for m in range(MT) for k in range(2)])

            def mem_key(n):
                w = mk0 + n // 2
                c0 = (n % 2) * P
                eng.wait_ge(w_lo, 2 * w + 2)
                wait_free(eng, ("mk", n))
                wp = wpiece(w, 256)
                for k in range(KT):
                    i = mm3(bank(("mk", n))[:, 0:MEM], [q[:, k, c0:c0 + P] for q in wp],
                            [memT[:, j, k, :] for j in range(2)], k == 0, k == KT - 1)
                full(i, ("mk", n))

            for n in range(KT - 2):
                mem_key(n)
            for t in range(NT):
                eng.wait_ge(ln_done, t + 1)
                rows_T("x0T", t)
            mem_key(KT - 2)
            mem_key(KT - 1)
            wait_read(eng, *[("x0T", t, k) for t in range(NT) for k in range(2)])
            for n in range(D_IN // P):
                w, c0 = in_slices(n)
                eng.wait_ge(w_lo, 2 * w + 2)
                wait_free(eng, ("in", n))
                wp = wpiece(w, 256)
                for k in range(KT):
                    i = mm3(bank(("in", n)), [q[:, k, c0:c0 + P] for q in wp],
                            [actT[:, j, k, :] for j in range(2)], k == 0, k == KT - 1)
                full(i, ("in", n))
            eng.wait_ge(const_in, 16)
            eng.wait_ge(bd_in, 64)
            for ft in range(FT):
                eng.wait_ge(xc_done, ft + 1)
                for w in range(2):
                    g = ("gate", ft, w)
                    wait_free(eng, g)
                    full(eng.matmul(bank(g), gate_bd[:, w, ft, :], xc[:, ft, :], start=True, stop=True), g)
            for n in range(5):
                wait_read(eng, ("in", 8 if n == 0 else 9 + n))
                wait_free(eng, ("rope", n))
                src = kpad[0][:, CHUNK:] if n == 0 else qs[:, n - 1, :]
                full(eng.matmul(bank(("rope", n)), perm, src, start=True, stop=True), ("rope", n))
            eng.wait_ge(pad_zero, 3)
            wait_read(eng, ("in", 9))
            for b in range(2):
                transposes(("vwin", b), [vpad[:, c * CHUNK:c * CHUNK + P] for c in range(4 * b, 4 * b + 4)])

            def scores(t):
                for par in range(2):
                    g = ("S", t, par)
                    wait_free(eng, g)
                    ps = slice(par * 64, par * 64 + 64)
                    for hp in range(4):
                        kk = kpad[0 if hp // 2 == par else 1]
                        for c in range(2):
                            ch = 2 * t + c
                            i = eng.matmul(psum[c * 64:c * 64 + 64, G[g] % 8, hp * P:(hp + 1) * P],
                                           qs[ps, hp, ch * CHUNK:(ch + 1) * CHUNK],
                                           kk[ps, ch * CHUNK:ch * CHUNK + P], start=True, stop=True)
                    full(i, g)

            def prob_T(t):
                eng.wait_ge(prob_done, t + 1)
                for k in range(2):
                    transposes(("PT", t, k), [prob[:, t % 2, 4 * k + j, :] for j in range(4)])

            def att_out(t):
                g = ("O", t)
                wait_read(eng, ("PT", t, 0), ("PT", t, 1), ("vwin", 0), ("vwin", 1))
                wait_free(eng, g)
                for c in range(2):
                    for kv in range(2):
                        for par in range(2):
                            dst = psum[par * 64:par * 64 + 64, G[g] % 8, :].rearrange("p (f t) -> p f t", t=P)
                            i = eng.matmul(dst[:, 2 * kv:2 * kv + 2, c * 64:c * 64 + 64],
                                           vwin[:, 2 * t + c, kv * 64:kv * 64 + 64],
                                           probT[:, 4 * kv + par:4 * kv + par + 3:2, c * 64:c * 64 + 64],
                                           start=True, stop=True)
                full(i, g)

            def mem_values(q):
                w = mv0 + q
                eng.wait_ge(w_lo, 2 * w + 2)
                wp = wpiece(w, 256)
                for m in range(MT):
                    wait_free(eng, ("mv", q, m))
                    for k in range(KT):
                        i = mm3(bank(("mv", q, m))[:, 0:256], [memT[:, j, k, m * P:(m + 1) * P] for j in range(2)],
                                [x[:, k, :] for x in wp], k == 0, k == KT - 1)
                    full(i, ("mv", q, m))

            def squares(b):
                g = ("sq",)
                if b == 1:
                    eng.wait_ge(lru_sq, FT)
                    wait_free(eng, g)
                else:
                    wait_read(eng, *[("O", t) for t in range(NT)])
                for t in range(NT):
                    for f in range(FT):
                        src = qs[:, f, t * P:(t + 1) * P] if b == 0 else ra[:, f, t * P:(t + 1) * P]
                        i = eng.matmul(bank(g)[:, b * NT + t:b * NT + t + 1], src, ones[:, 0:1],
                                       start=f == 0, stop=f == FT - 1)
                if b == 0:
                    full(i, g)

            def out_proj(h, t, b):
                w = o0 + 2 * h + b
                eng.wait_ge(w_lo, 2 * w + 2)
                g = ("out", h, t, b)
                wait_free(eng, g)
                wp = wpiece(w, 512)
                for k in range(4):
                    i = mm3(bank(g), [actT[:, j, 4 * b + k, t * P:(t + 1) * P] for j in range(2)],
                            [x[:, k, :] for x in wp], k == 0, k == 3)
                full(i, g)

            for name, t in ATTENTION:
                if (name, t) == ("S", 0):
                    wait_read(eng, *[("rope", n) for n in range(5)])
                    eng.wait_ge(kswap, 1)
                if name == "out":
                    eng.wait_ge(att_lo, t + 1)
                    out_proj(0, t, 0)
                elif name[:2] == "sq":
                    squares(int(name[2]))
                else:
                    {"mv": mem_values, "S": scores, "PT": prob_T, "O": att_out}[name](t)
            eng.wait_ge(lru_lo, FT)
            for t in range(NT):
                out_proj(0, t, 1)

            def norm_T(n, t):
                eng.wait_ge(ln_done, n * NT + t + 1)
                rows_T(f"x{n}T", t)

            for t in range(NT):
                for b in range(2):
                    out_proj(1, t, b)
                if t >= 2:
                    norm_T(1, t - 2)
            norm_T(1, 2)

            def m_query(h, t0=0, t1=T, parts=range(2)):
                w = q0 + h
                eng.wait_ge(w_lo, 2 * w + 2)
                wp = wpiece(w, 256)
                for n in parts:
                    if t0 == 0:
                        wait_free(eng, ("mq", h, n))
                    for k in range(KT):
                        i = mm3(bank(("mq", h, n))[:, t0:t1], [x[:, k, n * P:(n + 1) * P] for x in wp],
                                [actT[:, j, k, t0:t1] for j in range(2)], k == 0, k == KT - 1)
                    if t1 == T:
                        full(i, ("mq", h, n))

            def m_scores(h):
                wait_read(eng, ("mq", h, 0), ("mq", h, 1))
                for n in range(2):
                    g = ("mS", h, n)
                    wait_free(eng, g)
                    for u in range(2):
                        t = 2 * n + u
                        for k in range(2):
                            i = eng.matmul(bank(g)[:, u * MEM:(u + 1) * MEM],
                                           mq[:, 2 * h + k, t * P:(t + 1) * P], mkT[:, 2 * h + k, :],
                                           start=k == 0, stop=k == 1)
                    full(i, g)

            def m_prob_T(h):
                eng.wait_ge(m_prob, h + 1)
                for m in range(MT):
                    transposes(("mPT", h, m), [mprob[:, h % 2, t, m * P:(m + 1) * P] for t in range(NT)])

            def m_out(h):
                wait_read(eng, ("mPT", h, 0), ("mPT", h, 1))
                for n in range(2):
                    g = ("mO", h, n)
                    wait_free(eng, g)
                    for m in range(MT):
                        i = eng.matmul(bank(g), mvv[:, m, (2 * h + n) * P:(2 * h + n + 1) * P],
                                       mpT[:, h % 2, m, :], start=m == 0, stop=m == 1)
                    full(i, g)

            wait_read(eng, *[("x1T", t, k) for t in range(2) for k in range(2)])
            m_query(0, 0, T // 2, [0])
            norm_T(1, 3)
            m_query(0, 0, T // 2, [1])
            wait_read(eng, *[("x1T", t, k) for t in (2, 3) for k in range(2)])
            m_query(0, T // 2, T)
            wait_read(eng, *[("mk", n) for n in range(KT)])
            wait_read(eng, *[("mv", q, m) for q in range(4) for m in range(MT)])
            for h in range(1, MH):
                m_query(h)
                if h >= 2:
                    m_prob_T(h - 2)
                m_scores(h - 1)
            for name, h in M_TAIL:
                {"mO": m_out, "mS": m_scores, "mPT": m_prob_T}[name](h)

            wait_read(eng, *[("mO", h, n) for h in range(MH) for n in range(2)])
            w0 = wo0
            for h in range(2):
                for t in range(NT):
                    g = ("wo", h, t)
                    wait_free(eng, g)
                    for b in range(2):
                        w = w0 + 2 * h + b
                        eng.wait_ge(w_lo, 2 * w + 2)
                        wp = wpiece(w, 512)
                        for k in range(4):
                            i = mm3(bank(g), [actT[:, j, 4 * b + k, t * P:(t + 1) * P] for j in range(2)],
                                    [x[:, k, :] for x in wp], b + k == 0, b == 1 and k == 3)
                    full(i, g)
                    if h == 1 and t >= 2:
                        norm_T(2, t - 2)

            W = NG + NE

            def logits(t):
                g = ("logitsT", t)
                wait_read(eng, ("x2T", t, 0), ("x2T", t, 1))
                if t == 0:
                    eng.wait_ge(router_in, 16 * (3 + NG))
                wait_free(eng, g)
                for k in range(KT):
                    i = eng.matmul(bank(g)[0:W, 0:P], w_rt[:, k, :], x2T[:, k, t * P:(t + 1) * P],
                                   start=k == 0, stop=k == KT - 1)
                full(i, g)

            logits(0)
            norm_T(2, 2)
            logits(1)
            norm_T(2, 3)
            logits(2)
            logits(3)
            g = ("logits",)
            wait_free(eng, g)
            for t in range(NT):
                wait_read(eng, ("logitsT", t))
                i = eng.transpose(bank(g)[:, t * W:(t + 1) * W], logT[0:W, t * P:(t + 1) * P], ident[0:W, 0:W])
            full(i, g)
            g = ("rank",)
            eng.wait_ge(onehots, 1)
            wait_free(eng, g)
            for t in range(NT + 1):
                dst = bank(g)[:, t * NE:(t + 1) * NE]
                for s in range(min(t + 1, NT)):
                    i = eng.matmul(dst, tri_h if s == t else ones_h, moh_h[:, s, :], start=s == 0,
                                   stop=s == min(t, NT - 1))
            full(i, g)
            g = ("table",)
            eng.wait_ge(selected, 1)
            wait_free(eng, g)
            for j in range(TOPK * NT):
                i = eng.matmul(bank(g)[:, 0:CMAX], selT[:, j, :], sel_c[:, j, :], start=j == 0,
                               stop=j == TOPK * NT - 1)
            full(i, g)

            def x_T(c):
                eng.wait_ge(gathered, 16 * c + 16)
                for k in range(KT):
                    i = eng.transpose(psum[:, k // 4, (k % 4) * P:(k % 4 + 1) * P], xg[:, k * P:(k + 1) * P], ident)
                i.then_inc(xtrans_done, 1)

            def gate_up(c, e):
                eng.wait_ge(xgT_ready, c + 1)
                for k in range(KT):
                    if k % 4 == 0:
                        for i in (k // 2, k // 2 + 1):
                            eng.wait_ge(moe_lo[i], e + 1)
                    s = slice((k % 4) * F, (k % 4 + 1) * F)
                    cols = slice(k * P, (k + 1) * P)
                    first, final = k == 0, k == KT - 1
                    for b in range(2):
                        for part in range(2):
                            eng.matmul(psum[:, 2 + b, :], xgT_hi[:, cols], moe_w(k // 4 * 2 + b, part)[:, s],
                                       start=first and part == 0, stop=False)
                    for b in range(2):
                        i = eng.matmul(psum[:, 2 + b, :], xgT_lo[:, cols], moe_w(k // 4 * 2 + b, 0)[:, s],
                                       start=False, stop=final)
                    if k == 3:
                        i.then_inc(gu_half, 1)
                i.then_inc(gateup_done, 1)

            def h_T(c):
                eng.wait_ge(h_ready, c + 1)
                for f in range(FFT):
                    i = eng.transpose(psum[:, 4, f * P:(f + 1) * P], h_act[:, f * P:(f + 1) * P], ident)
                i.then_inc(htrans_done, 1)

            def down(c, e):
                eng.wait_ge(hT_ready, c + 1)
                if not isinstance(c, int):
                    eng.wait_ge(o_read, c)
                for f in range(FFT):
                    if f % 2 == 0:
                        eng.wait_ge(moe_lo[4 + f // 2], e + 1)
                    cols = slice(f * P, (f + 1) * P)
                    first, final = f == 0, f == FFT - 1
                    for hf in range(2):
                        s = slice((f % 2) * D + hf * 512, (f % 2) * D + hf * 512 + 512)
                        for part in range(2):
                            eng.matmul(psum[:, 5 + hf, :], hT_hi[:, cols], moe_w(4 + f // 2, part)[:, s],
                                       start=first and part == 0, stop=False)
                    for hf in range(2):
                        s = slice((f % 2) * D + hf * 512, (f % 2) * D + hf * 512 + 512)
                        i = eng.matmul(psum[:, 5 + hf, :], hT_lo[:, cols], moe_w(4 + f // 2, 0)[:, s],
                                       start=False, stop=final)
                i.then_inc(down_done, 1)

            for b in range(8):
                last = max(v for v in G.values() if v % 8 == b)
                eng.wait_ge(psum_read[b], last // 8 + 1)
            x_T(0)
            gate_up(0, 0)
            x_T(1)
            h_T(0)
            eng.wait_ge(table_done, 1)
            n = table(eng, T_N, NE, CMAX)
            last = table(eng, T_LAST, NE - 1, CMAX - 1)
            previous = table(eng, T_PREV, NE - 2, CMAX - 2)
            previous_expert = expert_of(eng, previous)

            def pe_chunk(c):
                e_up, e_down = expert_of(eng, c), expert_of(eng, c - 2)
                x_T(c)
                down(c - 2, e_down)
                h_T(c - 1)
                gate_up(c, e_up)

            gate_up(1, expert_of(eng, 1))
            pe_chunk(2)
            with eng.Fori(3, CMAX) as c:
                with eng.If(c < n):
                    pe_chunk(c)
            down(previous, previous_expert)
            h_T(last)
            down(last, NE - 1)


_INS = ['x', 'mem', 'ln_in_g', 'ln_in_b', 'w_in', 'attn_sink', 'conv_w', 'conv_b', 'w_rgate', 'b_rgate',
        'w_igate', 'b_igate', 'lru_lambda', 'norm_attn_g', 'norm_lru_g', 'w_out', 'ln1_g', 'ln1_b', 'wq_mem',
        'wk_mem', 'wv_mem', 'wo_mem', 'ln2_g', 'ln2_b', 'w_router_group', 'b_router_group', 'w_router_expert',
        'b_router_expert', 'w_gate_e', 'w_up_e', 'w_down_e', 'ln3_g', 'ln3_b']


def kernel(**inputs):
    import concourse.bacc as bacc
    from concourse.bass_utils import run_bass_kernel_spmd

    nc = bacc.Bacc("TRN2", target_bir_lowering=False, num_devices=1)
    arrays, args = {}, {}
    for name in _INS:
        a = np.ascontiguousarray(inputs[name])
        arrays[f"in_{name}"] = a
        args[name] = nc.dram_tensor(f"in_{name}", a.shape, mybir.dt.from_np(a.dtype), kind="ExternalInput").ap()
    cst, rot = constants()
    aps = []
    for name, a in (("consts", cst), ("rots", rot)):
        arrays[name] = a
        aps.append(nc.dram_tensor(name, a.shape, F32, kind="ExternalInput").ap())
    y = nc.dram_tensor("y_out", (1, T, D), F32, kind="ExternalOutput").ap()
    encoder_layer(nc, args, aps[0], aps[1], y)
    r = run_bass_kernel_spmd(nc, [arrays], core_ids=[0])
    return r.results[0]["y_out"]
```
